# Optimizing a Trainium2 kernel written in Bass

```python
import math
import numpy as np
import jax
import jax.numpy as jnp
from jax import lax

D_MODEL = 1024
BATCH = 1
SEQ = 128
DEPTH = 2
DEC_BATCH = 1
DEC_SEQ = 512
PAST_LEN = 128

GRID_W = 64
N_EVEN = (DEPTH + 1) // 2
N_ODD = DEPTH // 2
HA = 4
DKA = 128
DVA = 128
CHUNK_A = 64
HB = 4
DKB = 128
DVB = 128
CONV_K = 3
CHUNK_B = 64
HC = 16
KVH = 4
HD = 64
WINDOW = 128
QBLOCK = 128
ROPE_THETA = 10000.0
N_GROUPS = 4
EXPERTS_PER_GROUP = 4
N_EXPERTS = N_GROUPS * EXPERTS_PER_GROUP
TOP_K_IN_GROUP = 2
EXPERT_FF = 256
DN_ALPHA = (2 * DEPTH) ** 0.25
DN_BETA = (8 * DEPTH) ** -0.25
LN_EPS = 1e-5
EVEN_SPLIT_WIDTHS = (HA * DKA, HA * DKA, HA * DVA, HA * DVA, 4 * HA,
                     2 * HB * DKB + HB * DVB, HB * DVB, 2 * HB, 2 * HB)
EVEN_IN = sum(EVEN_SPLIT_WIDTHS)
EVEN_OUT = HA * DVA + HB * DVB

kernel_name = 'bidir_mlstm_deltanet_window_gqa_hmoe_step'

def _split(x, widths):
    return jnp.split(x, np.cumsum(widths)[:-1].tolist(), axis=-1)

def _heads(t, nh):
    b, n, _ = t.shape
    return t.reshape(b, n, nh, -1).transpose(0, 2, 1, 3)

def _merge(t):
    b, h, n, d = t.shape
    return t.transpose(0, 2, 1, 3).reshape(b, n, h * d)

def _layer_norm(x, g, b):
    xf = x.astype(jnp.float32)
    mu = xf.mean(-1, keepdims=True)
    var = jnp.square(xf - mu).mean(-1, keepdims=True)
    return ((xf - mu) * lax.rsqrt(var + LN_EPS) * g + b).astype(x.dtype)

def _head_layer_norm(x, g):
    mu = x.mean(-1, keepdims=True)
    var = jnp.square(x - mu).mean(-1, keepdims=True)
    return (x - mu) * lax.rsqrt(var + LN_EPS) * g

def _head_rms_norm(x, g):
    return x * lax.rsqrt(jnp.square(x).mean(-1, keepdims=True) + LN_EPS) * g

def _l2norm(x):
    return x * lax.rsqrt(jnp.sum(jnp.square(x), -1, keepdims=True) + 1e-6)

def _modulation(cvec, w, b):
    m = jax.nn.silu(cvec) @ w + b
    return tuple(t[:, None, :] for t in jnp.split(m, 6, axis=-1))

def _to_chunks(t, L):
    b, h, n = t.shape[:3]
    return jnp.moveaxis(t.reshape(b, h, n // L, L, *t.shape[3:]), 2, 0)

def _from_chunks(t):
    nc, b, h, l, d = t.shape
    return jnp.moveaxis(t, 0, 2).reshape(b, h, nc * l, d)

def _centered_conv(x, w):
    p = w.shape[0] // 2
    n = x.shape[1]
    xp = jnp.pad(x, ((0, 0), (p, p), (0, 0)))
    return sum(xp[:, j:j + n] * w[j] for j in range(w.shape[0]))

def _rope_1d(x, pos):
    half = x.shape[-1] // 2
    inv = ROPE_THETA ** (-jnp.arange(half, dtype=jnp.float32) / half)
    ang = pos.astype(jnp.float32)[:, None] * inv[None, :]
    cos, sin = jnp.cos(ang), jnp.sin(ang)
    x1, x2 = x[..., :half], x[..., half:]
    return jnp.concatenate([x1 * cos - x2 * sin, x1 * sin + x2 * cos], axis=-1)

def _axial_rope(x, row, col):
    h = x.shape[-1] // 2
    return jnp.concatenate([_rope_1d(x[..., :h], row), _rope_1d(x[..., h:], col)], axis=-1)

def _mlstm_scan(q, k, v, log_i, log_f, c0, n0, m0):
    L = CHUNK_A
    tri = jnp.tril(jnp.ones((L, L), bool))

    def step(carry, xs):
        c, nrm, m = carry
        qj, kj, vj, ij, fj = xs
        bcum = jnp.cumsum(fj, axis=-1)
        d = jnp.where(tri, bcum[..., :, None] - bcum[..., None, :] + ij[..., None, :], -jnp.inf)
        inter = bcum + m[..., None]
        m_t = jnp.maximum(inter, d.max(-1))
        s = jnp.einsum('bhtk,bhsk->bhts', qj, kj) * jnp.exp(d - m_t[..., None])
        w_inter = jnp.exp(inter - m_t)
        num = jnp.einsum('bhts,bhsv->bhtv', s, vj) + w_inter[..., None] * jnp.einsum('bhtk,bhkv->bhtv', qj, c)
        den = s.sum(-1) + w_inter * jnp.einsum('bhtk,bhk->bht', qj, nrm)
        hj = num / jnp.maximum(jnp.abs(den), jnp.exp(-m_t))[..., None]
        g_end = bcum[..., -1:] - bcum + ij
        m_new = jnp.maximum(bcum[..., -1] + m, g_end.max(-1))
        w_end = jnp.exp(g_end - m_new[..., None])
        carry_decay = jnp.exp(bcum[..., -1] + m - m_new)
        c_new = carry_decay[..., None, None] * c + jnp.einsum('bhs,bhsk,bhsv->bhkv', w_end, kj, vj)
        n_new = carry_decay[..., None] * nrm + jnp.einsum('bhs,bhsk->bhk', w_end, kj)
        return (c_new, n_new, m_new), hj

    f32 = jnp.float32
    carry0 = (c0.astype(f32), n0.astype(f32), m0.astype(f32))
    (c, nrm, m), h = lax.scan(step, carry0, tuple(_to_chunks(t, L) for t in (q, k, v, log_i, log_f)))
    return _from_chunks(h), c, nrm, m

def _delta_scan(q, k, v, log_a, beta, s0):
    L = CHUNK_B
    dv = v.shape[-1]
    tri = jnp.tril(jnp.ones((L, L), bool))
    strict = jnp.tril(jnp.ones((L, L), bool), -1)
    eye = jnp.eye(L, dtype=jnp.float32)

    def step(s, xs):
        qj, kj, vj, gj, bj = xs
        G = jnp.cumsum(gj, axis=-1)
        decay = jnp.exp(jnp.where(tri, G[..., :, None] - G[..., None, :], -jnp.inf))
        kb = kj * bj[..., None]
        a_mat = jnp.where(strict, jnp.einsum('bhik,bhjk->bhij', kb, kj) * decay, 0.0)
        rhs = jnp.concatenate([vj * bj[..., None], kb * jnp.exp(G)[..., None]], axis=-1)
        sol = lax.linalg.triangular_solve(eye + a_mat, rhs, left_side=True, lower=True)
        v_new = sol[..., :dv] - jnp.einsum('bhlk,bhkv->bhlv', sol[..., dv:], s)
        o = (jnp.einsum('bhlk,bhkv->bhlv', qj * jnp.exp(G)[..., None], s)
             + jnp.einsum('bhij,bhjv->bhiv', jnp.einsum('bhik,bhjk->bhij', qj, kj) * decay, v_new))
        g_end = G[..., -1:]
        s_new = (jnp.exp(g_end)[..., None] * s
                 + jnp.einsum('bhlk,bhlv->bhkv', kj * jnp.exp(g_end - G)[..., None], v_new))
        return s_new, o

    s, o = lax.scan(step, s0.astype(jnp.float32), tuple(_to_chunks(t, L) for t in (q, k, v, log_a, beta)))
    return _from_chunks(o), s

def _even_mixer(h, w_in, gate_b, mnorm_g, conv_w, a_log, dt_bias, dnorm_g, w_out, mc0, mn0, mm0, ds0):
    f32 = jnp.float32
    b, n, _ = h.shape
    qa, ka, va, oa, ga, qkv_b, zb, bb, ab = _split(h @ w_in, EVEN_SPLIT_WIDTHS)
    flip = lambda t: jnp.flip(t, axis=2)
    q = _heads(qa, HA).astype(f32)
    k = _heads(ka, HA).astype(f32) * DKA ** -0.5
    v = _heads(va, HA).astype(f32)
    g = (ga.astype(f32).reshape(b, n, 2, 2, HA) + gate_b).transpose(2, 3, 0, 4, 1)
    log_i, log_f = g[:, 0], jax.nn.log_sigmoid(g[:, 1])
    hf, cf, nf, mf = _mlstm_scan(q, k, v, log_i[0], log_f[0], mc0[:, 0], mn0[:, 0], mm0[:, 0])
    hb, cb, nb, mb = _mlstm_scan(flip(q), flip(k), flip(v), flip(log_i[1]), flip(log_f[1]),
                                 mc0[:, 1], mn0[:, 1], mm0[:, 1])
    ya = jax.nn.sigmoid(_heads(oa, HA).astype(f32)) * _head_layer_norm(hf + flip(hb), mnorm_g.reshape(HA, 1, DVA))
    qkv = jax.nn.silu(_centered_conv(qkv_b, conv_w).astype(f32))
    qd, kd, vd = _split(qkv, (HB * DKB, HB * DKB, HB * DVB))
    qd = _l2norm(_heads(qd, HB)) * DKB ** -0.5
    kd = _l2norm(_heads(kd, HB))
    vd = _heads(vd, HB)
    beta = jax.nn.sigmoid(bb.astype(f32).reshape(b, n, 2, HB)).transpose(2, 0, 3, 1)
    a_pre = ab.astype(f32).reshape(b, n, 2, HB).transpose(2, 0, 3, 1)
    log_a = -jnp.exp(a_log.astype(f32))[:, None, :, None] * jax.nn.softplus(a_pre + dt_bias.astype(f32)[:, None, :, None])
    of, sf = _delta_scan(qd, kd, vd, log_a[0], beta[0], ds0[:, 0])
    ob, sb = _delta_scan(flip(qd), flip(kd), flip(vd), flip(log_a[1]), flip(beta[1]), ds0[:, 1])
    yb = _head_rms_norm(of + flip(ob), dnorm_g.reshape(HB, 1, DVB)) * jax.nn.silu(_heads(zb, HB).astype(f32))
    y = jnp.concatenate([_merge(ya), _merge(yb)], axis=-1).astype(h.dtype) @ w_out
    states = (jnp.stack([cf, cb], 1), jnp.stack([nf, nb], 1), jnp.stack([mf, mb], 1), jnp.stack([sf, sb], 1))
    return y, states

def _odd_qkv(h, w_qkv):
    q, k, v = _split((h @ w_qkv).astype(jnp.float32), (HC * HD, KVH * HD, KVH * HD))
    return _heads(q, HC) * HD ** -0.5, _heads(k, KVH), _heads(v, KVH)

def _attn_context(h, w_qkv, sink, w_out):
    b, n, _ = h.shape
    grp = HC // KVH
    q, k, v = _odd_qkv(h, w_qkv)
    qg = q.reshape(b, KVH, grp, n, HD)
    s = jnp.einsum('bkgqd,bkcd->bkgqc', qg, k)
    s_sink = jnp.broadcast_to(sink.astype(jnp.float32).reshape(1, KVH, grp, 1, 1), s.shape[:-1] + (1,))
    p = jax.nn.softmax(jnp.concatenate([s, s_sink], axis=-1), axis=-1)[..., :n]
    o = jnp.einsum('bkgqc,bkcd->bkgqd', p, v).reshape(b, HC, n, HD)
    return _merge(o).astype(h.dtype) @ w_out, k, v

def _attn_latent(h, w_qkv, sink, w_out, ck, cv, row, col):
    b, n, _ = h.shape
    nb = n // QBLOCK
    grp = HC // KVH
    f32 = jnp.float32
    q, k, v = _odd_qkv(h, w_qkv)
    q = _axial_rope(q, row, col)
    k = _axial_rope(k, row, col)
    qb = q.reshape(b, KVH, grp, nb, QBLOCK, HD)
    pad = ((0, 0), (0, 0), (QBLOCK, QBLOCK), (0, 0))
    kp = jnp.pad(k, pad).reshape(b, KVH, nb + 2, QBLOCK, HD)
    vp = jnp.pad(v, pad).reshape(b, KVH, nb + 2, QBLOCK, HD)
    band = lambda t: jnp.concatenate([t[:, :, :-2], t[:, :, 1:-1], t[:, :, 2:]], axis=3)
    kw, vw = band(kp), band(vp)
    qpos = jnp.arange(n).reshape(nb, QBLOCK)
    kpos = (jnp.arange(nb) * QBLOCK - QBLOCK)[:, None] + jnp.arange(3 * QBLOCK)[None, :]
    valid = ((jnp.abs(qpos[:, :, None] - kpos[:, None, :]) <= WINDOW)
             & (kpos[:, None, :] >= 0) & (kpos[:, None, :] < n))
    s_loc = jnp.where(valid, jnp.einsum('bkgnqd,bknjd->bkgnqj', qb, kw), -jnp.inf)
    ckf, cvf = ck.astype(f32), cv.astype(f32)
    s_ctx = jnp.einsum('bkgnqd,bkcd->bkgnqc', qb, ckf)
    s_sink = jnp.broadcast_to(sink.astype(f32).reshape(1, KVH, grp, 1, 1, 1), s_ctx.shape[:-1] + (1,))
    p = jax.nn.softmax(jnp.concatenate([s_ctx, s_loc, s_sink], axis=-1), axis=-1)
    lc = ck.shape[2]
    o = (jnp.einsum('bkgnqc,bkcd->bkgnqd', p[..., :lc], cvf)
         + jnp.einsum('bkgnqj,bknjd->bkgnqd', p[..., lc:lc + 3 * QBLOCK], vw))
    o = o.reshape(b, HC, n, HD)
    return _merge(o).astype(h.dtype) @ w_out

def _hier_moe(h, w_grp, b_grp, w_er, b_er, w_gate, w_up, w_down):
    b, n, d = h.shape
    f32 = jnp.float32
    t = h.reshape(b * n, d)
    lg = (t @ w_grp + b_grp).astype(f32)
    g_idx = jnp.argmax(lg, axis=-1)
    g_w = jnp.max(jax.nn.softmax(lg, axis=-1), axis=-1)
    g_hot = jax.nn.one_hot(g_idx, N_GROUPS, dtype=f32)
    le = (jnp.einsum('td,gde->tge', t, w_er) + b_er).astype(f32)
    le = jnp.einsum('tge,tg->te', le, g_hot)
    top_v, top_i = lax.top_k(le, TOP_K_IN_GROUP)
    w_sel = jax.nn.softmax(top_v, axis=-1) * g_w[:, None]
    e_idx = g_idx[:, None] * EXPERTS_PER_GROUP + top_i
    gates = jnp.einsum('tk,tke->te', w_sel, jax.nn.one_hot(e_idx, N_EXPERTS, dtype=f32))
    a = jnp.einsum('td,edf->tef', t, w_gate)
    u = jnp.einsum('td,edf->tef', t, w_up)
    hid = ((jax.nn.silu(a) * u).astype(f32) * gates[:, :, None]).astype(t.dtype)
    y = jnp.einsum('tef,efd->td', hid, w_down)
    return y.reshape(b, n, d)

def setup_inputs(seed: int = 0) -> dict:
    key = jax.random.key(seed)
    ks = iter(jax.random.split(key, 48))
    f32 = jnp.float32
    D = D_MODEL

    def nrm(shape, scale):
        return jax.random.normal(next(ks), shape, f32) * scale

    x_prompt = nrm((BATCH, SEQ, D), 1.0)
    x_sample = nrm((DEC_BATCH, DEC_SEQ, D), 1.0)
    c = nrm((DEC_BATCH, D), 1.0)
    c_ctx = nrm((D,), 1.0)
    state_mlstm_c = nrm((DEC_BATCH, N_EVEN, 2, HA, DKA, DVA), 0.1)
    state_mlstm_n = nrm((DEC_BATCH, N_EVEN, 2, HA, DKA), 0.1)
    state_mlstm_m = nrm((DEC_BATCH, N_EVEN, 2, HA), 0.5)
    state_delta = nrm((DEC_BATCH, N_EVEN, 2, HB, DKB, DVB), 0.1)
    cache_k = nrm((DEC_BATCH, N_ODD, KVH, PAST_LEN, HD), 1.0)
    cache_v = nrm((DEC_BATCH, N_ODD, KVH, PAST_LEN, HD), 1.0)
    w_mod = nrm((DEPTH, D, 6 * D), D ** -0.5)
    b_mod = nrm((DEPTH, 6 * D), 0.02)
    ln_g = 1.0 + nrm((DEPTH, 2, D), 0.02)
    ln_b = nrm((DEPTH, 2, D), 0.02)
    w_in_even = nrm((N_EVEN, D, EVEN_IN), D ** -0.5)
    mlstm_gate_b = jnp.stack([nrm((N_EVEN, 2, HA), 0.1), 3.0 + nrm((N_EVEN, 2, HA), 0.5)], axis=2)
    mlstm_norm_g = 1.0 + nrm((N_EVEN, HA * DVA), 0.02)
    delta_conv_w = nrm((N_EVEN, CONV_K, 2 * HB * DKB + HB * DVB), CONV_K ** -0.5)
    delta_a_log = jnp.log(jax.random.uniform(next(ks), (N_EVEN, 2, HB), f32, 1.0, 16.0))
    dt = jnp.exp(jax.random.uniform(next(ks), (N_EVEN, 2, HB), f32, math.log(1e-3), math.log(1e-1)))
    delta_dt_bias = dt + jnp.log(-jnp.expm1(-dt))
    delta_norm_g = 1.0 + nrm((N_EVEN, HB * DVB), 0.02)
    w_out_even = nrm((N_EVEN, EVEN_OUT, D), EVEN_OUT ** -0.5 * DN_BETA)
    w_qkv_odd = nrm((N_ODD, D, (HC + 2 * KVH) * HD), D ** -0.5)
    attn_sink = nrm((N_ODD, HC), 0.5)
    w_out_odd = nrm((N_ODD, HC * HD, D), (HC * HD) ** -0.5 * DN_BETA)
    w_grp = nrm((DEPTH, D, N_GROUPS), D ** -0.5)
    b_grp = nrm((DEPTH, N_GROUPS), 0.01)
    w_erouter = nrm((DEPTH, N_GROUPS, D, EXPERTS_PER_GROUP), D ** -0.5)
    b_erouter = nrm((DEPTH, N_GROUPS, EXPERTS_PER_GROUP), 0.01)
    w_gate = nrm((DEPTH, N_EXPERTS, D, EXPERT_FF), D ** -0.5)
    w_up = nrm((DEPTH, N_EXPERTS, D, EXPERT_FF), D ** -0.5)
    w_down = nrm((DEPTH, N_EXPERTS, EXPERT_FF, D), EXPERT_FF ** -0.5 * DN_BETA)
    return {'x_prompt': x_prompt, 'x_sample': x_sample, 'c': c, 'c_ctx': c_ctx,
            'state_mlstm_c': state_mlstm_c, 'state_mlstm_n': state_mlstm_n, 'state_mlstm_m': state_mlstm_m,
            'state_delta': state_delta, 'cache_k': cache_k, 'cache_v': cache_v,
            'w_mod': w_mod, 'b_mod': b_mod, 'ln_g': ln_g, 'ln_b': ln_b,
            'w_in_even': w_in_even, 'mlstm_gate_b': mlstm_gate_b, 'mlstm_norm_g': mlstm_norm_g,
            'delta_conv_w': delta_conv_w, 'delta_a_log': delta_a_log, 'delta_dt_bias': delta_dt_bias,
            'delta_norm_g': delta_norm_g, 'w_out_even': w_out_even,
            'w_qkv_odd': w_qkv_odd, 'attn_sink': attn_sink, 'w_out_odd': w_out_odd,
            'w_grp': w_grp, 'b_grp': b_grp, 'w_erouter': w_erouter, 'b_erouter': b_erouter,
            'w_gate': w_gate, 'w_up': w_up, 'w_down': w_down}

def reference(x_prompt, x_sample, c, c_ctx, state_mlstm_c, state_mlstm_n, state_mlstm_m, state_delta,
              cache_k, cache_v, w_mod, b_mod, ln_g, ln_b, w_in_even, mlstm_gate_b, mlstm_norm_g,
              delta_conv_w, delta_a_log, delta_dt_bias, delta_norm_g, w_out_even, w_qkv_odd, attn_sink,
              w_out_odd, w_grp, b_grp, w_erouter, b_erouter, w_gate, w_up, w_down):
    f32 = jnp.float32
    bp = x_prompt.shape[0]
    n_lat = x_sample.shape[1]
    rows = n_lat // GRID_W
    row = jnp.repeat(jnp.arange(rows), GRID_W)
    col = jnp.tile(jnp.arange(GRID_W), rows)
    zero_ctx = (jnp.zeros((bp, 2, HA, DKA, DVA), f32), jnp.zeros((bp, 2, HA, DKA), f32),
                jnp.zeros((bp, 2, HA), f32), jnp.zeros((bp, 2, HB, DKB, DVB), f32))
    xp, xs = x_prompt, x_sample
    out_mc, out_mn, out_mm, out_ds, out_k, out_v = [], [], [], [], [], []
    for l in range(DEPTH):
        mp = _modulation(c_ctx[None, :], w_mod[l], b_mod[l])
        ms = _modulation(c, w_mod[l], b_mod[l])
        hp = xp * (1 + mp[1]) + mp[0]
        hs = xs * (1 + ms[1]) + ms[0]
        if l % 2 == 0:
            e = l // 2
            ew = (w_in_even[e], mlstm_gate_b[e], mlstm_norm_g[e], delta_conv_w[e], delta_a_log[e],
                  delta_dt_bias[e], delta_norm_g[e], w_out_even[e])
            yp, (mc, mn, mm, ds) = _even_mixer(hp, *ew, *zero_ctx)
            ys, _ = _even_mixer(hs, *ew, state_mlstm_c[:, e], state_mlstm_n[:, e], state_mlstm_m[:, e], state_delta[:, e])
            out_mc.append(mc)
            out_mn.append(mn)
            out_mm.append(mm)
            out_ds.append(ds)
        else:
            o = l // 2
            yp, kc, vc = _attn_context(hp, w_qkv_odd[o], attn_sink[o], w_out_odd[o])
            ys = _attn_latent(hs, w_qkv_odd[o], attn_sink[o], w_out_odd[o], cache_k[:, o], cache_v[:, o], row, col)
            out_k.append(kc)
            out_v.append(vc)
        xp = _layer_norm(DN_ALPHA * xp + mp[2] * yp, ln_g[l, 0], ln_b[l, 0])
        xs = _layer_norm(DN_ALPHA * xs + ms[2] * ys, ln_g[l, 0], ln_b[l, 0])
        moe_w = (w_grp[l], b_grp[l], w_erouter[l], b_erouter[l], w_gate[l], w_up[l], w_down[l])
        xp = _layer_norm(DN_ALPHA * xp + mp[5] * _hier_moe(xp * (1 + mp[4]) + mp[3], *moe_w), ln_g[l, 1], ln_b[l, 1])
        xs = _layer_norm(DN_ALPHA * xs + ms[5] * _hier_moe(xs * (1 + ms[4]) + ms[3], *moe_w), ln_g[l, 1], ln_b[l, 1])
    dt = x_prompt.dtype
    return (xp, xs,
            jnp.stack(out_mc, 1).astype(dt), jnp.stack(out_mn, 1).astype(dt), jnp.stack(out_mm, 1).astype(dt),
            jnp.stack(out_ds, 1).astype(dt), jnp.stack(out_k, 1).astype(dt), jnp.stack(out_v, 1).astype(dt))


_drawn_inputs = setup_inputs


def setup_inputs(seed=0):
    import zlib

    import numpy as np

    out = dict(_drawn_inputs(seed))
    spreads = {}
    factors = {'state_mlstm_c': 8.0,
     'state_mlstm_n': 8.0,
     'state_mlstm_m': 8.0,
     'state_delta': 6.246,
     'cache_k': 3.404,
     'cache_v': 3.541,
     'mlstm_norm_g': 89.113,
     'delta_norm_g': 69.362,
     'attn_sink': 8.0,
     'b_grp': 14.382,
     'b_erouter': 23.501}
    for name, (base, spread) in spreads.items():
        noise = np.random.default_rng([zlib.crc32(name.encode()), seed]).standard_normal(out[name].shape)
        drawn = base * np.exp(spread * noise) if base else spread * noise
        out[name] = jnp.asarray(drawn.astype(out[name].dtype))
    for name, factor in factors.items():
        out[name] = (out[name] * factor).astype(out[name].dtype)
    return out
```

```python
import concourse.bass as bass
from concourse import mybir
from contextlib import ExitStack
import numpy as np

D = 1024
P = 128
KT = D // P
TILES = 5
T = TILES * P
LAT = T - P
HEADS = 4
HW = HEADS * P
DEPTH = 2
EVEN_IN = 4128
NEXP, GRP, EPG, FF = 16, 4, 4, 256
HC, KVH, HD = 16, 4, 64
ALPHA = float((2 * DEPTH) ** 0.25)
LN_EPS = 1e-5
NEG = -1e30
SLOT = 6144
NSLOT = 3
ETILES = 25
SLOTS_E = ETILES * P
BANKS = 8

C_ID, C_FLIP, C_UPI, C_LOI, C_ONES, C_NF, C_NB = range(7)
C_LEV = (7, 14)
N_CONST = 21


def constants():
    p, f = np.meshgrid(np.arange(P), np.arange(P), indexing="ij")
    m = np.zeros((N_CONST, P, P), np.float32)
    m[C_ID] = p == f
    m[C_FLIP] = p + f == P - 1
    m[C_UPI] = p <= f
    m[C_LOI] = p >= f
    m[C_ONES] = 1.0
    m[C_NF] = np.where(p <= f, 0.0, NEG)
    m[C_NB] = np.where(p >= f, 0.0, NEG)
    for n in range(7):
        b = 1 << n
        u = (p // (2 * b) == f // (2 * b)) & (p % (2 * b) < b) & (f % (2 * b) >= b)
        m[C_LEV[0] + n] = u
        m[C_LEV[1] + n] = u.T
    return np.ascontiguousarray(m.transpose(1, 0, 2))


def iotas():
    m = np.zeros((P, 56), np.float32)
    m[:, 0:4] = np.arange(4)
    m[:, 8:13] = P * np.arange(TILES)
    m[:, 16:16 + ETILES] = np.arange(ETILES)
    m[:, 48:53] = np.arange(P)[:, None] + P * np.arange(TILES)
    return m


def rope_tables():
    half = HD // 4
    inv = 10000.0 ** (-np.arange(half, dtype=np.float32) / half)
    t = np.arange(LAT)
    out = np.zeros((2, LAT, 2, 2, half), np.float32)
    for a, pos in enumerate((t // 64, t % 64)):
        ang = pos.astype(np.float32)[:, None] * inv[None, :].astype(np.float32)
        out[0, :, a, :, :] = np.cos(ang)[:, None, :]
        out[1, :, a, 0, :] = -np.sin(ang)
        out[1, :, a, 1, :] = np.sin(ang)
    return np.ascontiguousarray(out.reshape(2, TILES - 1, P, HD).transpose(2, 0, 1, 3))


def tile_at(d, s):
    return s if d == 0 or s == 0 else TILES - s


def weight_loads():
    out = [("mod", 0, c) for c in range(12)]
    out += [("in", n) for n in ("gates", "qa", "ka", "va", "oa", "vd", "kd", "qd", "zb")]
    out += [("wout", 0, n) for n in range(2)]
    out += [("moe", 0)]
    out += [("mod", 1, c) for c in range(12)]
    out += [("qkv", n) for n in (2, 0, 1)] + [("wout", 1, n) for n in range(2)]
    out += [("moe", 1)]
    return out


def unit_order():
    u = [("cT",)]
    u += [("convT",)]

    def mod(l):
        out = []
        for c in range(12):
            out.append(("mod", l, c))
            if c < 4:
                out.append(("modT", l, c))
        return out

    def hT(l):
        return [("hTlat", l, k) for k in range(KT)] + [("hTctx", l, g) for g in range(2)]

    def fm(name):
        return [("fm", name, m, half) for m in range(4) for half in range(2)]

    def tm(name):
        return [("tm", name, t) for t in range(TILES)]

    u += mod(0) + hT(0) + tm("gates")
    u += [("cs", 0), ("cs", 1), ("ce",)]
    u += [(n, d, part) for n in ("rowf", "rowi") for d in range(2) for part in range(2)]
    u += [("mcol", 0), ("mcol", 1), ("mflip",), ("mvb",)]
    u += fm("qa") + fm("ka") + tm("va") + [("ktok", "a", t) for t in range(TILES)]
    u += tm("oa")
    u += fm("vd") + [("vtok", t) for t in range(TILES)]
    u += fm("kd") + [("ssq", "kd", m, half) for m in range(4) for half in range(2)]
    u += [("ktok", "d", t) for t in range(TILES)]
    u += fm("qd") + [("ssq", "qd", m, half) for m in range(4) for half in range(2)]
    u += tm("zb")
    u += [("yT", 0, k, part) for k in range(KT) for part in range(2)]
    u += [("out", 0, n, t) for n in range(2) for t in range(TILES)]

    def router(l):
        return ([("h2T", l, k, part) for k in range(KT) for part in range(2)] + [("rt", l, t) for t in range(TILES)]
                + [("rank", l), ("cnt", l)])

    u += router(0)
    u += mod(1) + hT(1)
    u += [("qkv", n, t) for n in (2, 0, 1) for t in range(TILES)]
    u += [("kT", t) for t in range(TILES + 1)]
    u += [("qT", t, g) for t in range(TILES) for g in range(2)]
    u += [("yT", 1, k, part) for k in range(KT) for part in range(2)]
    u += [("out", 1, n, t) for n in range(2) for t in range(TILES)]
    u += router(1)
    return u


def build(nc, ins, outs):
    f32 = mybir.dt.float32
    ALU = mybir.AluOpType
    ACT = mybir.ActivationFunctionType
    AX = mybir.AxisListType

    ctx = ExitStack()
    with ctx:
        def sb(name, shape, dt=f32):
            return ctx.enter_context(nc.sbuf_tensor(name, shape, dt))

        def sem(name):
            return ctx.enter_context(nc.semaphore(name))

        X = sb("X", [P, TILES, D])
        HT = sb("HT", [P, KT, T])
        SLOTS = sb("SLOTS", [P, NSLOT, SLOT])
        CST = sb("CST", [P, N_CONST, P])
        Z = sb("Z", [P, 6 * 2560])
        QT, KTR = (Z[:, n * 2560:(n + 1) * 2560].rearrange("p (h t) -> p h t", h=HEADS) for n in range(2))
        KTOK, VTOK, YA, YB = (Z[:, n * 2560:(n + 1) * 2560].rearrange("p (t c) -> p t c", t=TILES) for n in range(2, 6))
        H2T = Z[:, 0:5120].rearrange("p (k t) -> p k t", k=KT)
        H2 = Z[:, 10240:15360].rearrange("p (t c) -> p t c", t=TILES)
        XG = Z[:, 0:3072].rearrange("p (b c) -> p b c", b=3)
        XGT = Z[:, 3072:6144].rearrange("p (b k c) -> p b k c", b=3, k=KT)
        YE = Z[:, 6144:9216].rearrange("p (b c) -> p b c", b=3)
        AU = Z[:, 9216:9984].rearrange("p (b c) -> p b c", b=3)
        HID = Z[:, 9984:10752].rearrange("p (b m c) -> p b m c", b=3, m=2)
        YG = Z[:, 0:4096].rearrange("p (b j c) -> p b j c", b=2, j=2)
        BC = sb("BC", [P, 4, D])
        SMALL = sb("SMALL", [P, 2380])
        PS = ctx.enter_context(nc.psum_tensor("PS", [P, BANKS, 512], f32))

        at = [0]

        def small(n):
            a = at[0]
            at[0] += n
            assert at[0] <= 2380, at[0]
            return SMALL[:, a:a + n]

        ident, flip, ones = CST[:, C_ID, :], CST[:, C_FLIP, :], CST[:, C_ONES, :]
        SCR = SLOTS[:, 2, :]
        PRE = Z[:, 12800:15360].rearrange("p (m t) -> p m t", m=4)
        BCF = BC[:, :, :].rearrange("p a b -> p (a b)")
        SM = BCF[:, 0:2048].rearrange("p (s u v) -> p s u v", s=2, u=2 * HEADS)
        SD = BCF[:, 2048:4096].rearrange("p (s u v) -> p s u v", s=2, u=2 * HEADS)

        csil = small(16)
        MODT = small(KT * 4).rearrange("p (k j) -> p k j", k=KT)
        convw = small(36)
        MROW = SLOTS[0:2, 0, 5120:6144].rearrange("p (b c) -> p b c", b=2)
        CMB = SLOTS[:, 0, 5120:6144].rearrange("p (d c) -> p d c", d=2)
        GAIN = SLOTS[:, 1, 4608:5632].rearrange("p (g c) -> p g c", g=2)
        SG = [SLOTS[:, 0, 4608:5120], SLOTS[:, 1, 5632:6144]]
        SQ = SCR[:, 0:2560].rearrange("p (m t) -> p m t", m=4)
        NRM = SCR[:, 2560:5120].rearrange("p (m t) -> p m t", m=4)
        graw = small(TILES * 32).rearrange("p (t c) -> p t c", t=TILES)
        raw = small(2 * TILES * 16)
        raw4 = raw.rearrange("p (d s c) -> p d s c", d=2, s=TILES)
        gbias = small(32).rearrange("p (d c) -> p d c", d=2)
        alog = small(8)
        lcoef = small(16).rearrange("p (d c) -> p d c", d=2)
        zf = small(2 * TILES * 8)
        zabs = small(2 * TILES * 8)
        zexp = small(2 * TILES * 8)
        zln = small(2 * TILES * 8)
        LF = small(2 * TILES * 8)
        CS = small(2 * TILES * 8)
        CE = small(2 * TILES * 8)
        MC = small(2 * TILES * 4)
        rev = small(TILES * 4)
        MVB = small(56)
        MV = small(14)
        MEX = small(56)
        M0 = small(2)
        BETA = small(2 * TILES * 4)
        ARG = small(7 * 40).rearrange("p (n c) -> p n c", n=7)
        EX = small(7 * 40).rearrange("p (n c) -> p n c", n=7)
        WI, EN, WE, DC, EG, EE, ED = range(7)
        RV = small(2 * 40).rearrange("p (n c) -> p n c", n=2)
        CB = small(2 * 40).rearrange("p (n c) -> p n c", n=2)
        NS = small(16).rearrange("p (s u) -> p s u", s=2)
        t4 = small(8)
        t4b = small(8)
        st20 = small(20)
        st20b = small(20)
        half = small(20)
        rstd = small(20)
        bnst = small(TILES * 12).rearrange("p (t s c) -> p t s c", t=TILES, s=2)
        bnag = small(TILES * 2).rearrange("p (t c) -> p t c", t=TILES)
        lnr = small(TILES)
        eps = small(2)

        def v4(x):
            return x.rearrange("p (d s h) -> p d s h", d=2, s=TILES)

        def v8(x):
            return x.rearrange("p (d s h) -> p d s h", d=2, s=TILES)

        def heads(x):
            return x.rearrange("p (h v) -> p h v", h=HEADS)

        def col(x, n):
            return x.unsqueeze(2).to_broadcast([P, HEADS, n])

        ROWF = SCR[0:4, 0:2 * T].rearrange("p (d t) -> p d t", d=2)
        ROWI = SCR[0:4, 2 * T:4 * T].rearrange("p (d t) -> p d t", d=2)
        MR = SCR[0:4, 4 * T:6 * T].rearrange("p (d t) -> p d t", d=2)
        cin = SCR[0:16, 0:P]
        convrow = SCR[0:36, P:2 * P]

        def mlb(d, n):
            return SCR[:, (4 * d + n) * 512:(4 * d + n + 1) * 512]

        def dlb(d, n):
            if n == 6:
                return CMB[:, d, :]
            return SCR[:, (6 * d + n) * 512:(6 * d + n + 1) * 512]

        def mask(c):
            return CST[:, c, :].unsqueeze(1).to_broadcast([P, HEADS, P])

        YO = [QT[:, 0, 0:512], QT[:, 1, 0:512]]
        betaexp = small(40)
        mod_dram = nc.dram_tensor("mod_rows", [DEPTH, 2, 6 * D], f32).ap()
        ht = [0]
        HTF = HT[:, :, :].rearrange("p k t -> p (k t)")

        def routing(n):
            a = ht[0]
            ht[0] += n
            return HTF[:, a:a + n]

        LG = routing(TILES * 20).rearrange("p (t c) -> p t c", t=TILES)
        gmax, cmin, gsum, gw, vmax, vsec = (routing(TILES) for _ in range(6))
        cand, ghot, LE, hot1, hot2, LE2 = (routing(TILES * 4).rearrange("p (t c) -> p t c", t=TILES) for _ in range(6))
        gx = routing(TILES * 5)
        WSEL = routing(2 * TILES).rearrange("p (c t) -> p c t", c=2)
        HE = routing(2 * TILES * 16).rearrange("p (c t e) -> p c t e", c=2, t=TILES)
        HALL = routing(TILES * 16)
        RK = routing(TILES * 16)
        rtmp = routing(TILES * 16)
        CNT = routing(16)
        TSUM, TCUM, TBASE = (routing(16) for _ in range(3))
        zero16 = small(16)
        big = routing(ETILES * 16)
        slotf = routing(2 * TILES)
        eotf = routing(ETILES)
        i32 = mybir.dt.int32
        IDX = routing(2 * TILES).bitcast(i32).rearrange("p (c t) -> p c t", c=2)
        EOT = routing(ETILES).bitcast(i32)
        TOKI = routing(ETILES).bitcast(i32)
        TOKSEL = routing(3).bitcast(i32)
        tokid = routing(TILES).bitcast(i32)
        zeroi = routing(ETILES).bitcast(i32)
        assert ht[0] <= 5120
        IOTA = small(56)
        tokgate = small(2)
        RW = raw.rearrange("p (k c) -> p k c", k=KT)
        RB = small(20)
        h2_dram = nc.dram_tensor("h2_rows", [T, D], f32).ap()
        yg_dram = nc.dram_tensor("expert_rows", [SLOTS_E, D], f32).ap()
        tok_dram = [nc.dram_tensor(f"slot_tokens{l}", [SLOTS_E, 1], i32).ap() for l in range(DEPTH)]
        SINK = small(HC)

        QR = Z[:, 10240:15360].rearrange("p (t c) -> p t c", t=TILES)
        QTT = Z[:, 0:5120].rearrange("p (g t) -> p g t", g=HC // 2)
        V = Z[:, 5120:6656].rearrange("p (t c) -> p t c", t=TILES + 1)
        KTT = Z[:, 6656:9728].rearrange("p (g t) -> p g t", g=KVH)
        ROPE = Z[:, 9728:10240].rearrange("p (a t i) -> p a t i", a=2, t=TILES - 1)
        KD = BCF[:, 0:3072].rearrange("p (t g r i) -> p t g r i", t=TILES + 1, g=KVH, r=2)
        RTMP = BC[:, 3, 0:512]
        PB = HTF[:, 0:1536].rearrange("p (b c) -> p b c", b=3)
        PTB = HTF[:, 1536:3072].rearrange("p (b c) -> p b c", b=3)
        STEPS = TILES * HC
        NM = HTF[:, 3072:3072 + STEPS]
        RS = HTF[:, 3200:3200 + STEPS]
        ES = HTF[:, 3328:3328 + STEPS]

        def key_tiles(t):
            if t == 0:
                return [0], [0]
            local = list(range(max(1, t - 1), min(TILES - 1, t + 1) + 1))
            return local, local + [TILES]

        const_loaded = sem("const_loaded")
        x_loaded = sem("x_loaded")
        small_loaded = sem("small_loaded")
        state_loaded = sem("state_loaded")
        slot_arrived = [sem(f"slot{n}_arrived") for n in range(NSLOT)]
        unit_done = sem("unit_done")
        unit_out = sem("unit_out")
        mod_stored = [sem(f"mod_stored{n}") for n in range(2)]
        dve_order = sem("dve_order")
        pool_order = sem("pool_order")
        act_order = sem("act_order")
        gate_abs = sem("gate_abs")
        gate_ln = sem("gate_ln")
        gate_lf = sem("gate_lf")
        m_scanned = sem("m_scanned")
        mex_ready = sem("mex_ready")
        arg_ready = sem("arg_ready")
        exp_ready = sem("exp_ready")
        pool_const = sem("pool_const")

        def pair(name):
            return [sem(f"{name}{d}") for d in range(2)]

        ml_st, ml_db, ml_de, ml_sw, ml_vw, ml_u, ml_done = (
            pair("ml_" + n) for n in ("scores", "decay", "exp", "weights", "vw", "update", "done"))
        dl_kk, dl_db, dl_de, dl_at, dl_cm, dl_xt1, dl_x1t, dl_x1, dl_p1, dl_p1s, dl_p2, dl_x, dl_ks, dl_r, dl_tr, \
            dl_vn, dl_o, dl_vw, dl_su, dl_done = (
                pair("dl_" + n) for n in ("kk", "decay", "exp", "at", "cm", "xt1", "x1t", "x1", "p1", "p1s", "p2",
                                          "x", "ks", "r", "tr", "vn", "o", "vw", "su", "done"))
        conv_done = sem("conv_done")
        sq_ready = sem("sq_ready")
        silu_done = sem("silu_done")
        norm_taken = sem("norm_taken")
        normed = sem("normed")
        gate_used = sem("gate_used")
        var_ready = sem("var_ready")
        rstd_ready = sem("rstd_ready")
        y_ready = sem("y_ready")
        gain_loaded = sem("gain_loaded")
        alog_exp = sem("alog_exp")
        dl_qd, dl_xt = pair("dl_qd"), pair("dl_xt")
        bc_loaded = sem("bc_loaded")
        bc_free = sem("bc_free")
        out_used = sem("out_used")
        ln_done = sem("ln_done")
        h2_ready = sem("h2_ready")
        h2_stored = sem("h2_stored")
        router_loaded = sem("router_loaded")
        tables_cleared = sem("tables_cleared")
        route_arg = sem("route_arg")
        route_exp = sem("route_exp")
        hot_ready = sem("hot_ready")
        routed = sem("routed")
        slots_scattered = sem("slots_scattered")
        tok_picked = sem("tok_picked")
        tokens_loaded = sem("tokens_loaded")
        rows_gathered = [sem(f"rows_gathered{n}") for n in range(3)]
        xt_done = sem("xt_done")
        xt_out = sem("xt_out")
        gu_done = sem("gu_done")
        silu_out = sem("silu_out")
        hid_ready = sem("hid_ready")
        down_done = sem("down_done")
        ye_ready = sem("ye_ready")
        ye_stored = [sem(f"ye_stored{n}") for n in range(3)]
        yg_gathered = [sem(f"yg_gathered{n}") for n in range(2)]
        yg_used = sem("yg_used")
        states_stored = sem("states_stored")
        attn_loaded = sem("attn_loaded")
        caches_stored = sem("caches_stored")
        keys_ready = sem("keys_ready")
        queries_ready = sem("queries_ready")
        s_done = sem("s_done")
        max_ready = sem("max_ready")
        p_ready = sem("p_ready")
        pt_done = sem("pt_done")
        pt_out = sem("pt_out")
        pv_done = sem("pv_done")
        sink_arg = sem("sink_arg")
        sink_exp = sem("sink_exp")
        o_ready = sem("o_ready")
        x_stored = sem("x_stored")

        loads = weight_loads()
        load_no = {}
        n = 0
        for item in loads:
            load_no[item] = n
            n += ETILES if item[0] == "moe" else 1
        item_of = {load_no[item]: item for item in loads}
        first_moe = load_no[("moe", 0)]

        def slot_of(n):
            return n % 2 if n < first_moe else (n - first_moe) % NSLOT

        def dmas_of(item):
            return {"mod": 2, "moe": 3}.get(item[0], 1) if item != ("in", "gates") else 2

        arrived_at, count = {}, [0] * NSLOT
        for item in loads:
            for j in range(ETILES if item[0] == "moe" else 1):
                s = slot_of(load_no[item] + j)
                count[s] += 16 * dmas_of(item)
                arrived_at[load_no[item] + j] = count[s]

        units = unit_order()
        unit_no = {name: n for n, name in enumerate(units)}
        assert len(unit_no) == len(units)

        def last_unit(item):
            if item[0] == "mod":
                return item
            if item[0] == "wout":
                return ("out", item[1], item[2], TILES - 1)
            if item[0] == "qkv":
                return item + (TILES - 1,)
            if item[1] in ("qa", "ka", "vd", "kd", "qd"):
                return ("fm", item[1], 3, 1)
            return ("tm", item[1], TILES - 1)

        def slot_cols(n, k, cols):
            return SLOTS[:, slot_of(n), 0:k * cols].rearrange("p (k c) -> p k c", k=k)

        w_in = ins["w_in_even"][0].rearrange("(k p) n -> p k n", p=P)
        in_at = {"qa": 0, "ka": 512, "va": 1024, "oa": 1536, "qd": 2064, "kd": 2576, "vd": 3088, "zb": 3600}

        block = ctx.enter_context(nc.Block())

        @block.sync
        def _(sp):
            def load(item):
                n = load_no[item]
                lag = 2 if n < first_moe else NSLOT
                if first_moe + ETILES <= n < first_moe + ETILES + NSLOT:
                    sp.wait_ge(down_done, n - first_moe - NSLOT + 1)
                elif n >= lag:
                    sp.wait_ge(unit_done, unit_no[last_unit(item_of[n - lag])] + 1)
                s = slot_of(n)
                a = slot_arrived[s]
                kind = item[0]
                if kind == "mod":
                    _, l, c = item
                    w = ins["w_mod"][l].rearrange("(k p) n -> p k n", p=P)
                    sp.dma_start(slot_cols(n, KT, 512), w[:, :, c * 512:(c + 1) * 512]).then_inc(a, 16)
                    sp.dma_start(SLOTS[0:1, s, 4096:4608], ins["b_mod"][l:l + 1, c * 512:(c + 1) * 512]).then_inc(a, 16)
                elif item == ("in", "gates"):
                    dst = slot_cols(n, KT, 32)
                    sp.dma_start(dst[:, :, 0:16], w_in[:, :, 2048:2064]).then_inc(a, 16)
                    sp.dma_start(dst[:, :, 16:32], w_in[:, :, 4112:4128]).then_inc(a, 16)
                elif kind == "in":
                    c = in_at[item[1]]
                    sp.dma_start(slot_cols(n, KT, 512), w_in[:, :, c:c + 512]).then_inc(a, 16)
                elif kind == "qkv":
                    w = ins["w_qkv_odd"][0].rearrange("(k p) n -> p k n", p=P)
                    sp.dma_start(slot_cols(n, KT, 512), w[:, :, item[1] * 512:(item[1] + 1) * 512]).then_inc(a, 16)
                elif kind == "wout":
                    _, l, c = item
                    w = (ins["w_out_even"], ins["w_out_odd"])[l][0].rearrange("(k p) n -> p k n", p=P)
                    sp.dma_start(slot_cols(n, KT, 512), w[:, :, c * 512:(c + 1) * 512]).then_inc(a, 16)

            for item in loads[:first_moe]:
                load(item)
            def sync_moe(l):
                n0 = load_no[("moe", l)]
                sp.wait_ge(routed, l + 1)
                if l == 0:
                    sp.wait_ge(gate_used, 2 * TILES)
                weights = [ins[n][l] for n in ("w_gate", "w_up", "w_down")]

                def load_expert(j, u):
                    e = sp.value_load(EOT[0:1, bass.ds(3 * j + u, 1)], min_val=0, max_val=NEXP - 1)
                    for m, w in enumerate(weights):
                        k = KT if m < 2 else 2
                        dst = SLOTS[:, u, 2048 * m:2048 * m + 2048].rearrange("p (k c) -> p k c", k=k)
                        sp.dma_start(dst, w[bass.ds(e, 1)].rearrange("o (k p) c -> p (o k) c", p=P))\
                            .then_inc(slot_arrived[u], 16)

                def store_rows(j, u):
                    i = 3 * j + u
                    sp.wait_ge(ye_ready, i + (ETILES * l + 1))
                    sp.dma_start(yg_dram[bass.ds(P * i, P), :], YE[:, u, :]).then_inc(ye_stored[u], 16)

                for u in range(3):
                    if l:
                        sp.wait_ge(unit_done, unit_no[last_unit(item_of[n0 - 3 + u])] + 1)
                    load_expert(0, u)
                with sp.Fori(0, 7) as j:
                    for u in range(3):
                        sp.wait_ge(down_done, 3 * j + (ETILES * l + u + 1))
                        load_expert(j + 1, u)
                        store_rows(j, u)
                sp.wait_ge(down_done, ETILES * l + 22)
                load_expert(8, 0)
                for i in range(21, 25):
                    store_rows(i // 3, i % 3)

            sync_moe(0)
            for item in loads[loads.index(("moe", 0)) + 1:-1]:
                load(item)
            sync_moe(1)
            for t in range(TILES):
                sp.wait_ge(ln_done, 3 * TILES + t + 1)
                dst = outs[0][0] if t == 0 else outs[1][0, (t - 1) * P:t * P, :]
                sp.dma_start(dst, X[:, t, :]).then_inc(x_stored, 16)
            sp.wait_ge(x_stored, 16 * TILES)

        @block.gpsimd
        def _(pool):
            order = [0]

            def done(ins_, s=None):
                if s is None:
                    order[0] += 1
                    ins_.then_inc(pool_order, 1)
                    pool.wait_ge(pool_order, order[0])

            sl = small_loaded
            pool.dma_start(gbias[:, :, 0:8], ins["mlstm_gate_b"][0].rearrange("d t h -> (d t h)").partition_broadcast(P)
                           .rearrange("p (d c) -> p d c", d=2)).then_inc(sl, 16)
            pool.dma_start(gbias[:, :, 12:16], ins["delta_dt_bias"][0].rearrange("d h -> (d h)").partition_broadcast(P)
                           .rearrange("p (d c) -> p d c", d=2)).then_inc(sl, 16)
            pool.dma_start(alog, ins["delta_a_log"][0].rearrange("d h -> (d h)").partition_broadcast(P)).then_inc(sl, 16)
            pool.dma_start(M0[0:4, :], ins["state_mlstm_m"][0, 0].rearrange("d h -> h d"),
                           allow_slow_non_contiguous=True).then_inc(sl, 16)
            pool.memset(gbias[:, :, 8:12], 0.0).then_inc(pool_const, 1)
            pool.memset(half, -0.5).then_inc(pool_const, 1)
            pool.memset(eps[:, 0:1], P * 1e-6).then_inc(pool_const, 1)
            pool.memset(eps[:, 1:2], 1e-6).then_inc(pool_const, 1)
            pool.memset(lcoef, -1.0).then_inc(pool_const, 1)
            pool.memset(SM[:, 0], 0.0).then_inc(pool_const, 1)
            pool.memset(SD[:, 0], 0.0).then_inc(pool_const, 1)
            pool.memset(NS[:, 0], 0.0).then_inc(pool_const, 1)
            pool.dma_start(SM[:, 1], ins["state_mlstm_c"][0, 0].rearrange("d h k v -> k (d h) v")).then_inc(state_loaded, 16)
            pool.dma_start(SD[:, 1], ins["state_delta"][0, 0].rearrange("d h k v -> k (d h) v")).then_inc(state_loaded, 16)
            pool.dma_start(NS[:, 1], ins["state_mlstm_n"][0, 0].rearrange("d h k -> k (d h)"),
                           allow_slow_non_contiguous=True).then_inc(state_loaded, 16)

            def store_mod(l):
                for c in range(4, 12):
                    pool.wait_ge(unit_out, unit_no[("mod", l, c)] + 1)
                    pool.dma_start(mod_dram[l, :, c * 512:(c + 1) * 512], MROW[:, c % 2, :]).then_inc(mod_stored[c % 2], 16)

            pool.dma_start(GAIN[:, 0, :], ins["mlstm_norm_g"][0].partition_broadcast(P)).then_inc(gain_loaded, 16)
            pool.dma_start(GAIN[:, 1, :], ins["delta_norm_g"][0].partition_broadcast(P)).then_inc(gain_loaded, 16)
            store_mod(0)
            for s in range(TILES):
                for d in range(2):
                    if s == 0 and d == 0:
                        pool.wait_ge(exp_ready, 1)
                        pool.wait_ge(unit_out, unit_no[("tm", "va", TILES - 1)] + 1)
                    if s:
                        pool.wait_ge(ml_u[d], s)
                    w = v4(EX[:, WE, :])[:, d, s, :]
                    pool.tensor_tensor(heads(mlb(d, 2)), heads(VTOK[:, tile_at(d, s), :]), col(w, P), ALU.mult)\
                        .then_inc(ml_vw[d], 1)
            pool.wait_ge(var_ready, 1)
            pool.tensor_tensor(rstd, st20, half, ALU.pow).then_inc(rstd_ready, 1)
            for n in range(2):
                pool.wait_ge(mod_stored[n], 4 * 16)
            for s in range(TILES):
                for d in range(2):
                    at_ = dlb(d, 2)
                    pool.wait_ge(dl_at[d], s + 1)
                    done(pool.tensor_tensor(heads(at_), heads(at_), col(v4(BETA)[:, d, s, :], P), ALU.mult))
                    lev = C_LEV[d]
                    done(pool.tensor_tensor(heads(dlb(d, 5)), heads(at_), mask(lev), ALU.mult))
                    pool.tensor_tensor(heads(dlb(d, 4)), mask(C_ID), heads(dlb(d, 5)), ALU.subtract).then_inc(dl_xt1[d], 1)
                    pool.tensor_tensor(heads(dlb(d, 6)), heads(at_), mask(lev + 1), ALU.mult).then_inc(dl_cm[d], 1)
                for n in range(2, 7):
                    for d in range(2):
                        if n >= 3:
                            pool.wait_ge(dl_p1[d], 6 * s + n - 2)
                        else:
                            pool.wait_ge(dl_xt1[d], s + 1)
                        pool.tensor_tensor(heads(dlb(d, 5 + n % 2)), heads(dlb(d, 2)), mask(C_LEV[d] + n), ALU.mult)\
                            .then_inc(dl_cm[d], 1)
                for d in range(2):
                    pool.wait_ge(dl_vn[d], s + 1)
                    pool.tensor_tensor(heads(dlb(d, 2)), heads(dlb(d, 3)), col(v4(EX[:, EE, :])[:, d, s, :], P), ALU.mult)\
                        .then_inc(dl_vw[d], 1)
            pool.wait_ge(var_ready, 2)
            pool.tensor_tensor(rstd, st20, half, ALU.pow).then_inc(rstd_ready, 1)

            bc = [0]

            def load_bc(rows):
                for j, r in enumerate(rows):
                    pool.dma_start(BC[:, j, :], r.partition_broadcast(P)).then_inc(bc_loaded, 16)

            def mod_row(l, v, m):
                return mod_dram[l, v, m * D:(m + 1) * D]

            for d in range(2):
                pool.wait_ge(dl_done[d], TILES)
            pool.dma_start(outs[2][0, 0].rearrange("d h k v -> k (d h) v"), SM[:, 0]).then_inc(states_stored, 16)
            pool.dma_start(outs[5][0, 0].rearrange("d h k v -> k (d h) v"), SD[:, 0]).then_inc(states_stored, 16)
            pool.dma_start(outs[3][0, 0].rearrange("d h k -> k (d h)"), NS[:, 0],
                           allow_slow_non_contiguous=True).then_inc(states_stored, 16)
            pool.dma_start(outs[4][0, 0].rearrange("d h -> h d"), MV[0:4, 1:14:7],
                           allow_slow_non_contiguous=True).then_inc(states_stored, 16)
            pool.wait_ge(states_stored, 64)
            for n in range(2):
                pool.wait_ge(mod_stored[n], 4 * 16)
            load_bc([mod_row(0, 0, 2), mod_row(0, 1, 2), ins["ln_g"][0, 0], ins["ln_b"][0, 0]])
            pool.wait_ge(var_ready, 3)
            pool.tensor_tensor(lnr, lnr, half[:, 0:TILES], ALU.pow).then_inc(rstd_ready, 1)

            def pool_moe(l):
                pool.dma_start(RW[:, :, 0:4], ins["w_grp"][l].rearrange("(k p) c -> p k c", p=P)).then_inc(router_loaded, 16)
                for g in range(GRP):
                    pool.dma_start(RW[:, :, 4 + 4 * g:8 + 4 * g], ins["w_erouter"][l, g].rearrange("(k p) c -> p k c", p=P))\
                        .then_inc(router_loaded, 16)
                pool.dma_start(RB[:, 0:4], ins["b_grp"][l].partition_broadcast(P)).then_inc(router_loaded, 16)
                pool.dma_start(RB[:, 4:20], ins["b_erouter"][l].rearrange("g e -> (g e)").partition_broadcast(P))\
                    .then_inc(router_loaded, 16)
                if l == 0:
                    pool.dma_start(IOTA, ins["iotas"]).then_inc(router_loaded, 16)
                pool.wait_ge(ln_done, TILES * (2 * l + 1))
                load_bc([mod_row(l, 0, 3), mod_row(l, 1, 3), mod_row(l, 0, 4), mod_row(l, 1, 4)])
                if l == 0:
                    pool.memset(zeroi, 0).then_inc(pool_const, 1)
                    pool.memset(zero16, 0.0).then_inc(pool_const, 1)
                    pool.wait_ge(pool_const, 10)
                    for m in range(DEPTH):
                        pool.dma_start(tok_dram[m].rearrange("(p i) o -> p (i o)", p=P), zeroi).then_inc(tables_cleared, 16)
                for t in range(TILES):
                    pool.wait_ge(h2_ready, TILES * l + t + 1)
                    pool.dma_start(h2_dram[t * P:(t + 1) * P, :], H2[:, t, :]).then_inc(h2_stored, 16)
                load_bc([mod_row(l, 0, 5), mod_row(l, 1, 5), ins["ln_g"][l, 1], ins["ln_b"][l, 1]])
                pool.wait_ge(routed, l + 1)
                if l == 0:
                    pool.wait_ge(tables_cleared, 32)
                for c in range(2):
                    for t in range(TILES):
                        pool.indirect_dma_start(tok_dram[l], bass.IndirectOffsetOnAxis(ap=IDX[:, c, t:t + 1], axis=0),
                                                tokid[:, t:t + 1], None).then_inc(slots_scattered, 16)
                pool.wait_ge(slots_scattered, 160 * (l + 1))
                pool.dma_start(TOKI, tok_dram[l].rearrange("(i p) o -> p (i o)", p=P),
                               allow_slow_non_contiguous=True).then_inc(tokens_loaded, 16)
                pool.wait_ge(tokens_loaded, 16 * (l + 1))
                pool.wait_ge(h2_stored, 16 * TILES * (l + 1))

                def gate(n):
                    pool.tensor_tensor(tokgate[:, n:n + 1], half[:, 0:1], half[:, 0:1], ALU.mult)

                def gather(j, u, first):
                    i = 3 * j + u
                    if not first:
                        pool.wait_ge(xt_done, i + (ETILES * l - 2))
                        gate(0)
                    pool.tensor_copy(TOKSEL[:, u:u + 1], TOKI[:, bass.ds(i, 1)]).then_inc(tok_picked, 1)
                    pool.wait_ge(tok_picked, i + (ETILES * l + 1))
                    gate(1)
                    pool.indirect_dma_start(XG[:, u, :], None, h2_dram,
                                            bass.IndirectOffsetOnAxis(ap=TOKSEL[:, u:u + 1], axis=0))\
                        .then_inc(rows_gathered[u], 16)

                for u in range(3):
                    gather(0, u, True)
                with pool.Fori(1, 8) as j:
                    for u in range(3):
                        gather(j, u, False)
                gather(8, 0, False)
                for u in range(3):
                    pool.wait_ge(ye_stored[u], 16 * (8 + (u == 0)) * (l + 1) + 16 * 0)
                for t in range(TILES):
                    if t >= 2:
                        pool.wait_ge(yg_used, TILES * l + t - 1)
                    for c in range(2):
                        pool.indirect_dma_start(YG[:, t % 2, c, :], None, yg_dram,
                                                bass.IndirectOffsetOnAxis(ap=IDX[:, c, t:t + 1], axis=0))\
                            .then_inc(yg_gathered[t % 2], 16)
                pool.wait_ge(var_ready, 4 + 2 * l)
                pool.tensor_tensor(lnr, lnr, half[:, 0:TILES], ALU.pow).then_inc(rstd_ready, 1)

            pool_moe(0)

            pool.dma_start(ROPE, ins["ropes"]).then_inc(attn_loaded, 16)
            pool.dma_start(V[:, TILES, :].rearrange("p (g i) -> p g i", g=KVH), ins["cache_v"][0, 0].rearrange("g s i -> s g i"))\
                .then_inc(attn_loaded, 16)
            pool.dma_start(SINK, ins["attn_sink"][0].partition_broadcast(P)).then_inc(attn_loaded, 16)
            pool.wait_ge(ln_done, 2 * TILES)
            for r in range(2):
                pool.dma_start(KD[:, TILES, :, r, :], ins["cache_k"][0, 0].rearrange("g s i -> s g i")).then_inc(attn_loaded, 16)
            store_mod(1)
            pool.wait_ge(unit_out, unit_no[("qkv", 2, 0)] + 1)
            pool.dma_start(outs[6][0, 0].rearrange("g s i -> s g i"), KD[:, 0, :, 0, :]).then_inc(caches_stored, 16)
            pool.dma_start(outs[7][0, 0].rearrange("g s i -> s g i"), V[:, 0, :].rearrange("p (g i) -> p g i", g=KVH))\
                .then_inc(caches_stored, 16)
            pool.wait_ge(caches_stored, 32)
            pool.wait_ge(unit_out, unit_no[("kT", TILES)] + 1)
            pool.wait_ge(queries_ready, 2 * TILES)
            for n in range(2):
                pool.wait_ge(mod_stored[n], 8 * 16)
            load_bc([mod_row(1, 0, 2), mod_row(1, 1, 2), ins["ln_g"][1, 0], ins["ln_b"][1, 0]])
            pool.wait_ge(var_ready, 5)
            pool.tensor_tensor(lnr, lnr, half[:, 0:TILES], ALU.pow).then_inc(rstd_ready, 1)
            pool_moe(1)

        @block.scalar
        def _(act):
            act.dma_start(CST[:, :, :], ins["consts"]).then_inc(const_loaded, 16)
            act.dma_start(cin[0:8, :], ins["c_ctx"].rearrange("(k p) -> k p", p=P)).then_inc(const_loaded, 16)
            act.dma_start(cin[8:16, :], ins["c"][0].rearrange("(k p) -> k p", p=P)).then_inc(const_loaded, 16)
            act.dma_start(convrow, ins["delta_conv_w"][0].rearrange("j (m p) -> (j m) p", p=P)).then_inc(const_loaded, 16)
            act.dma_start(X[:, 0, :], ins["x_prompt"][0]).then_inc(x_loaded, 16)
            act.dma_start(X[:, 1:TILES, :], ins["x_sample"][0].rearrange("(t p) n -> p t n", p=P)).then_inc(x_loaded, 16)

            def take(name):
                n = unit_no[name]
                act.wait_ge(unit_done, n + 1)
                return PS[:, n % BANKS, :]

            b = take(("cT",))
            act.activation(csil, b[:, 0:16], ACT.Silu).then_inc(unit_out, 1)
            b = take(("convT",))
            act.activation(convw, b[:, 0:36], ACT.Copy).then_inc(unit_out, 1)

            def mod_rows(l, mrow):
                for c in range(12):
                    b = take(("mod", l, c))
                    if l and c < 2:
                        act.wait_ge(mod_stored[c % 2], 64)
                    if c >= 6:
                        act.wait_ge(mod_stored[c % 2], 16 * (4 * l + (c - 4) // 2))
                    act.activation(mrow[:, c % 2, :], b[0:2, :], ACT.Copy).then_inc(unit_out, 1)
                    if c < 4:
                        b = take(("modT", l, c))
                        dst = MODT[:, 4 * (c % 2):4 * (c % 2) + 4, 2 * (c // 2):2 * (c // 2) + 2]
                        act.activation(dst, b[:, 0:8].rearrange("p (q v) -> p q v", q=4), ACT.Copy,
                                       bias=float(c // 2)).then_inc(unit_out, 1)

            def modulate(l):
                act.wait_ge(unit_out, unit_no[("modT", l, 3)] + 1)
                for k in range(KT):
                    b = take(("hTlat", l, k))
                    act.activation(HT[:, k, P:T], b, ACT.Identity, bias=MODT[:, k, 1:2], scale=MODT[:, k, 3:4])\
                        .then_inc(unit_out, 1)
                for g in range(2):
                    b = take(("hTctx", l, g))
                    for q in range(4):
                        k = 4 * g + q
                        i = act.activation(HT[:, k, 0:P], b[:, q * P:(q + 1) * P], ACT.Identity,
                                           bias=MODT[:, k, 0:1], scale=MODT[:, k, 2:3])
                    i.then_inc(unit_out, 1)

            def feature_major(name, dst, scale=1.0):
                for m in range(4):
                    for h in range(2):
                        b = take(("fm", name, m, h))
                        act.activation(dst[:, m, 320 * h:320 * h + 320], b[:, 0:320], ACT.Copy, scale=scale)\
                            .then_inc(unit_out, 1)

            mod_rows(0, MROW)
            modulate(0)
            for t in range(TILES):
                b = take(("tm", "gates", t))
                act.activation(graw[:, t, :], b[:, 0:32], ACT.Copy).then_inc(unit_out, 1)
            act.wait_ge(gate_abs, 1)
            act.activation(zexp, zabs, ACT.Exp, scale=-1.0).then_inc(act_order, 1)
            act.wait_ge(act_order, 1)
            act.activation(zln, zexp, ACT.Ln, bias=1.0).then_inc(gate_ln, 1)
            act.activation(v4(betaexp), raw4[:, :, :, 8:12], ACT.Exp, scale=-1.0)
            act.activation(alog, alog, ACT.Exp).then_inc(alog_exp, 1)
            for d in range(2):
                b = take(("cs", d))
                act.activation(CS[:, 40 * d:40 * d + 40], b[:, 0:40], ACT.Copy).then_inc(unit_out, 1)
            b = take(("ce",))
            act.activation(CE, b[:, 0:80], ACT.Copy).then_inc(unit_out, 1)
            for name, dst in (("rowf", ROWF), ("rowi", ROWI)):
                for d in range(2):
                    for part, (a, e) in enumerate(((0, 512), (512, T))):
                        b = take((name, d, part))
                        act.activation(dst[:, d, a:e], b[0:4, 0:e - a], ACT.Copy).then_inc(unit_out, 1)
            b = take(("mcol", 0))
            act.activation(MC[:, 0:20], b[:, 0:20], ACT.Copy).then_inc(unit_out, 1)
            b = take(("mcol", 1))
            act.activation(rev, b[:, 0:20], ACT.Copy).then_inc(unit_out, 1)
            b = take(("mflip",))
            act.activation(MC[:, 20:40], b[:, 0:20], ACT.Copy).then_inc(unit_out, 1)
            b = take(("mvb",))
            act.activation(MVB, b[:, 0:56], ACT.Copy).then_inc(unit_out, 1)
            act.wait_ge(arg_ready, 1)
            act.activation(EX[:, :, :], ARG[:, :, :], ACT.Exp).then_inc(exp_ready, 1)
            feature_major("qa", QT)
            feature_major("ka", KTR, P ** -0.5)
            for t in range(TILES):
                b = take(("tm", "va", t))
                act.activation(VTOK[:, t, :], b, ACT.Copy).then_inc(unit_out, 1)
            for t in range(TILES):
                b = take(("ktok", "a", t))
                act.activation(KTOK[:, t, :], b, ACT.Copy).then_inc(unit_out, 1)

            for s in range(TILES):
                for d in range(2):
                    act.wait_ge(ml_db[d], s + 1)
                    if s:
                        act.wait_ge(ml_sw[d], s)
                    for h in range(HEADS):
                        i = act.activation(mlb(d, 0)[:, h * P:(h + 1) * P], PS[:, 4 * d + 1, h * P:(h + 1) * P], ACT.Exp,
                                           bias=v4(CB[:, 0, :])[:, d, s, h:h + 1])
                    i.then_inc(ml_de[d], 1)

            def gate(name, func, used0):
                for t in range(TILES):
                    b = take(("tm", name, t))
                    if t >= 2 or used0:
                        act.wait_ge(gate_used, used0 + t - 1)
                    act.activation(SG[t % 2], b, func).then_inc(unit_out, 1)

            gate("oa", ACT.Sigmoid, 0)

            def silu_conv(dst, first):
                for m in range(4):
                    act.wait_ge(conv_done, first + m + 1)
                    act.activation(dst[:, m, :], dst[:, m, :], ACT.Silu).then_inc(silu_done, 1)

            def norms(name, dst, first, scale):
                for m in range(4):
                    act.wait_ge(silu_done, first + m + 1)
                    if name == "qd":
                        act.wait_ge(unit_out, unit_no[("ssq", "kd", 3, 1)] + 1)
                        act.wait_ge(normed, 4)
                    act.activation(SQ[:, m, :], dst[:, m, :], ACT.Square).then_inc(sq_ready, 1)
                for m in range(4):
                    for h in range(2):
                        b = take(("ssq", name, m, h))
                        act.activation(NRM[:, m, 320 * h:320 * h + 320], b[:, 0:320], ACT.Sqrt, scale=scale,
                                       bias=eps[:, 0:1] if name == "qd" else eps[:, 1:2]).then_inc(unit_out, 1)

            feature_major("vd", PRE)
            silu_conv(QT, 0)
            for t in range(TILES):
                b = take(("vtok", t))
                act.activation(VTOK[:, t, :], b, ACT.Copy).then_inc(unit_out, 1)
            act.wait_ge(conv_done, 4)
            feature_major("kd", PRE)
            silu_conv(KTR, 4)
            norms("kd", KTR, 4, 1.0)
            for t in range(TILES):
                b = take(("ktok", "d", t))
                act.activation(KTOK[:, t, :], b, ACT.Copy).then_inc(unit_out, 1)
            act.wait_ge(conv_done, 8)
            feature_major("qd", PRE)
            silu_conv(QT, 8)
            norms("qd", QT, 8, float(P))

            for s in range(TILES):
                for d in range(2):
                    act.wait_ge(dl_db[d], s + 1)
                    if s:
                        act.wait_ge(dl_done[d], s)
                    for h in range(HEADS):
                        i = act.activation(dlb(d, 0)[:, h * P:(h + 1) * P], PS[:, 4 * d + 1, h * P:(h + 1) * P], ACT.Exp,
                                           bias=v4(CB[:, 1, :])[:, d, s, h:h + 1])
                    i.then_inc(dl_de[d], 1)
                for d in range(2):
                    act.wait_ge(dl_x1t[d], s + 1)
                    act.activation(dlb(d, 3), PS[:, 4 * d, :], ACT.Copy).then_inc(dl_x1[d], 1)
                for n in range(1, 7):
                    for d in range(2):
                        act.wait_ge(dl_p1[d], 6 * s + n)
                        act.activation(dlb(d, 0), PS[:, 4 * d, :], ACT.Copy).then_inc(dl_p1s[d], 1)
            act.wait_ge(gate_used, TILES)
            gate("zb", ACT.Silu, TILES)
            for k in range(KT):
                for part, (a, e) in enumerate(((0, 512), (512, T))):
                    b = take(("yT", 0, k, part))
                    act.activation(HT[:, k, a:e], b[:, 0:e - a], ACT.Copy).then_inc(unit_out, 1)

            def out_rows(l):
                for n in range(2):
                    for t in range(TILES):
                        b = take(("out", l, n, t))
                        j = TILES * n + t
                        if j >= 2 or l:
                            act.wait_ge(out_used, 2 * TILES * l + j - 1)
                        act.activation(YO[j % 2], b, ACT.Copy).then_inc(unit_out, 1)

            out_rows(0)

            def act_moe(l):
                for k in range(KT):
                    for part, (a, e) in enumerate(((0, 512), (512, T))):
                        b = take(("h2T", l, k, part))
                        act.activation(H2T[:, k, a:e], b[:, 0:e - a], ACT.Copy).then_inc(unit_out, 1)
                for t in range(TILES):
                    b = take(("rt", l, t))
                    act.activation(LG[:, t, :], b[:, 0:20], ACT.Copy).then_inc(unit_out, 1)
                act.wait_ge(route_arg, l + 1)
                act.activation(gx, gx, ACT.Exp).then_inc(route_exp, 1)
                b = take(("rank", l))
                act.activation(RK, b[:, 0:80], ACT.Copy).then_inc(unit_out, 1)
                b = take(("cnt", l))
                act.activation(CNT, b[:, 0:16], ACT.Copy).then_inc(unit_out, 1)

                def tile(j, u, first=False):
                    i = 3 * j + u
                    if not first:
                        pass
                    act.wait_ge(xt_done, i + (ETILES * l + 1))
                    for h in range(2):
                        a = act.activation(XGT[:, u, 4 * h:4 * h + 4, :], PS[:, h, :].rearrange("p (k c) -> p k c", k=4), ACT.Copy)
                    a.then_inc(xt_out, 1)
                    act.wait_ge(gu_done, i + (ETILES * l + 1))
                    act.activation(AU[:, u, :], PS[:, 2 + u, 0:256], ACT.Silu).then_inc(silu_out, 1)

                with act.Fori(0, 8) as j:
                    for u in range(3):
                        tile(j, u)
                tile(8, 0)

            act_moe(0)

            mod_rows(1, MROW)
            modulate(1)
            act.wait_ge(ln_done, 2 * TILES)
            for n in (2, 0, 1):
                for t in range(TILES):
                    b = take(("qkv", n, t))
                    if n < 2:
                        act.activation(QR[:, t, 512 * n:512 * n + 512], b, ACT.Copy, scale=HD ** -0.5).then_inc(unit_out, 1)
                    else:
                        act.activation(KD[:, t, :, 0, :], b[:, 0:256].rearrange("p (g i) -> p g i", g=KVH), ACT.Copy)
                        act.activation(V[:, t, :], b[:, 256:512], ACT.Copy).then_inc(unit_out, 1)
            for t in range(TILES + 1):
                b = take(("kT", t))
                act.activation(KTT[:, :, t * P:(t + 1) * P], b.rearrange("p (g c) -> p g c", g=KVH), ACT.Copy).then_inc(unit_out, 1)
            for t in range(TILES):
                for g in range(2):
                    b = take(("qT", t, g))
                    act.activation(QTT[:, 4 * g:4 * g + 4, t * P:(t + 1) * P], b.rearrange("p (g c) -> p g c", g=4), ACT.Copy)\
                        .then_inc(unit_out, 1)

            def exponentials(n):
                w = P * len(key_tiles(n // HC)[1])
                act.wait_ge(max_ready, n + 1)
                if n >= 3:
                    act.wait_ge(pt_done, n - 2)
                act.activation(PB[:, n % 3, 0:w], PS[:, n % 3, 0:w], ACT.Exp, bias=NM[:, n:n + 1],
                               accum_out=RS[:, n:n + 1]).then_inc(p_ready, 1)

            def take_transposed(n):
                w = P * len(key_tiles(n // HC)[1])
                act.wait_ge(pt_done, n + 1)
                if n >= 3:
                    act.wait_ge(pv_done, n - 2)
                act.activation(PTB[:, n % 3, 0:w], PS[:, 3 + n % 3, 0:w], ACT.Copy).then_inc(pt_out, 1)

            for n in range(STEPS + 2):
                if n < STEPS:
                    exponentials(n)
                if n >= 2:
                    take_transposed(n - 2)
                if n % 8 == 1 and n > 8:
                    g = (n - 8) // 8
                    act.wait_ge(sink_arg, g + 1)
                    act.activation(ES[:, 8 * g:8 * g + 8], ES[:, 8 * g:8 * g + 8], ACT.Exp).then_inc(sink_exp, 1)
            for k in range(KT):
                for part, (a, e) in enumerate(((0, 512), (512, T))):
                    b = take(("yT", 1, k, part))
                    act.activation(HT[:, k, a:e], b[:, 0:e - a], ACT.Copy).then_inc(unit_out, 1)
            out_rows(1)
            act_moe(1)

        @block.vector
        def _(dve):
            count = {}

            def done(i, s=dve_order):
                count[s.name] = count.get(s.name, 0) + 1
                i.then_inc(s, 1)
                dve.wait_ge(s, count[s.name])

            tt, ts, stt = dve.tensor_tensor, dve.tensor_scalar, dve.scalar_tensor_tensor

            dve.wait_ge(unit_out, unit_no[("tm", "gates", TILES - 1)] + 1)
            dve.wait_ge(small_loaded, 64)
            dve.wait_ge(pool_const, 8)
            for d in range(2):
                for s in range(TILES):
                    t = tile_at(d, s)
                    dve.tensor_copy(raw4[:, d, s, 0:8], graw[:, t, 8 * d:8 * d + 8])
                    done(dve.tensor_copy(raw4[:, d, s, 8:16].rearrange("p (g c) -> p g c", g=2),
                                         graw[:, t, 16:32].rearrange("p (g e c) -> p g e c", g=2, e=2)[:, :, d, :]))
            for s in range(TILES):
                done(tt(raw4[:, :, s, :], raw4[:, :, s, :], gbias[:, :, :], ALU.add))
            z = v8(zf)
            done(ts(z[:, :, :, 0:4], raw4[:, :, :, 4:8], -1.0, None, ALU.mult))
            done(dve.tensor_copy(z[:, :, :, 4:8], raw4[:, :, :, 12:16]))
            done(stt(zabs, zf, -1.0, zf, ALU.mult, ALU.max), gate_abs)
            done(ts(zf, zf, 0.0, None, ALU.max))
            dve.wait_ge(gate_ln, 1)
            done(tt(LF, zf, zln, ALU.add))
            done(ts(v8(LF)[:, :, :, 0:4], v8(LF)[:, :, :, 0:4], -1.0, None, ALU.mult))
            dve.wait_ge(alog_exp, 1)
            for s in range(TILES):
                done(stt(v8(LF)[:, :, s, 4:8], v8(LF)[:, :, s, 4:8], -1.0, alog.rearrange("p (d h) -> p d h", d=2),
                         ALU.mult, ALU.mult))
            done(ts(v4(BETA), v4(betaexp), 1.0, None, ALU.add))
            done(dve.reciprocal(BETA, BETA), gate_lf)
            dve.wait_ge(unit_out, unit_no[("rowi", 1, 1)] + 1)
            for d in range(2):
                done(dve.tensor_tensor_scan(MR[:, d, 0:P], ROWF[:, d, 0:P], ROWI[:, d, 0:P], 0.0, ALU.add, ALU.max))
                done(dve.tensor_tensor_scan(MR[:, d, P:T], ROWF[:, d, P:T], ROWI[:, d, P:T], M0[0:4, d:d + 1], ALU.add,
                                            ALU.max), m_scanned)
            mv = MV.rearrange("p (d s) -> p d s", d=2)
            done(dve.memset(mv[0:4, :, 0:1], 0.0))
            done(dve.tensor_copy(mv[0:4, :, 1:2], MR[:, :, P - 1:P]))
            done(dve.tensor_copy(mv[0:4, :, 2:3], M0[0:4, :].unsqueeze(2)))
            done(dve.tensor_copy(mv[0:4, :, 3:7], MR[:, :, 2 * P - 1:T:P]))
            done(tt(MEX[0:4, :].rearrange("p (n h) -> p n h", h=4), MV[0:4, :].unsqueeze(2).to_broadcast([4, 14, 4]),
                    CST[0:4, C_ID, 0:4].unsqueeze(1).to_broadcast([4, 14, 4]), ALU.mult), mex_ready)
            dve.wait_ge(unit_out, unit_no[("mvb",)] + 1)
            cs, ce, m = v8(CS), v8(CE), v4(MC)
            mb = MVB.rearrange("p (d n h) -> p d n h", d=2, n=7)
            B, G, BE, GE = cs[:, :, :, 0:4], cs[:, :, :, 4:8], ce[:, :, :, 0:4], ce[:, :, :, 4:8]
            arg = [v4(ARG[:, n, :]) for n in range(7)]
            done(tt(v4(CB[:, 0, :]), raw4[:, :, :, 0:4], B, ALU.subtract))
            done(ts(v4(CB[:, 1, :]), G, -1.0, None, ALU.mult))
            done(tt(v4(RV[:, 0, :]), B, m, ALU.subtract))
            done(dve.tensor_copy(v4(RV[:, 1, :]), G))
            done(ts(arg[EN], m, -1.0, None, ALU.mult))
            done(tt(arg[WE], BE, v4(CB[:, 0, :]), ALU.add))
            done(dve.tensor_copy(arg[WI], v4(RV[:, 0, :])))
            done(dve.tensor_copy(arg[DC], BE))
            for s in range(TILES):
                before, after = (0, 1) if s == 0 else (s + 1, s + 2)
                done(tt(arg[WI][:, :, s, :], arg[WI][:, :, s, :], mb[:, :, before, :], ALU.add))
                done(tt(arg[DC][:, :, s, :], arg[DC][:, :, s, :], mb[:, :, before, :], ALU.add))
                done(tt(arg[DC][:, :, s, :], arg[DC][:, :, s, :], mb[:, :, after, :], ALU.subtract))
                done(tt(arg[WE][:, :, s, :], arg[WE][:, :, s, :], mb[:, :, after, :], ALU.subtract))
            done(dve.tensor_copy(arg[EG], G))
            done(tt(arg[EE], GE, G, ALU.subtract))
            done(dve.tensor_copy(arg[ED], GE), arg_ready)

            dve.wait_ge(exp_ready, 1)
            dve.wait_ge(state_loaded, 48)
            dve.wait_ge(unit_out, unit_no[("ktok", "a", TILES - 1)] + 1)

            def ex(n, d, s):
                return v4(EX[:, n, :])[:, d, s, :]

            for s in range(TILES):
                q = 1 if s else 0
                for d in range(2):
                    dve.wait_ge(ml_de[d], s + 1)
                    dve.wait_ge(ml_st[d], s + 1)
                    done(tt(mlb(d, 1), mlb(d, 0), PS[:, 4 * d, :], ALU.mult), ml_sw[d])
                for d in range(2):
                    A, Bk, C, E = (PS[:, 4 * d + n, :] for n in range(4))
                    dve.wait_ge(ml_u[d], s + 1)
                    done(tt(t4[:, 0:4], E[:, 4:8], ex(WI, d, s), ALU.mult))
                    done(tt(t4[:, 0:4], t4[:, 0:4], E[:, 0:4], ALU.add))
                    done(stt(t4b[:, 0:4], t4[:, 0:4], -1.0, t4[:, 0:4], ALU.mult, ALU.max))
                    done(tt(t4b[:, 0:4], t4b[:, 0:4], ex(EN, d, s), ALU.max))
                    done(dve.reciprocal(t4[:, 0:4], t4b[:, 0:4]))
                    w = mlb(d, 3)
                    done(tt(heads(w), heads(Bk), col(ex(WI, d, s), P), ALU.mult))
                    done(tt(w, w, A, ALU.add))
                    y = YA[:, tile_at(d, s), :]
                    if s > 2 or (s == 0 and d == 1):
                        done(tt(heads(w), heads(w), col(t4[:, 0:4], P), ALU.mult))
                        done(tt(y, y, w, ALU.add))
                    else:
                        done(tt(heads(y), heads(w), col(t4[:, 0:4], P), ALU.mult))
                    c = SM[:, q, 4 * d:4 * d + 4, :]
                    nn = NS[:, q, 4 * d:4 * d + 4]
                    done(tt(c, c, col(ex(DC, d, s), P), ALU.mult))
                    done(tt(c, c, heads(C), ALU.add))
                    done(tt(nn, nn, ex(DC, d, s), ALU.mult))
                    done(tt(nn, nn, E[:, 8:12], ALU.add), ml_done[d])

            def sums(y, dst, sq=None):
                for t in range(TILES):
                    v = heads(y[:, t, :])
                    if sq is not None:
                        done(tt(sq, y[:, t, :], y[:, t, :], ALU.mult))
                        v = heads(sq)
                    done(dve.tensor_reduce(dst[:, 4 * t:4 * t + 4], v, AX.X, ALU.add))

            sums(YA, st20)
            done(ts(st20, st20, 1.0 / P, None, ALU.mult))
            for t in range(TILES):
                done(tt(heads(YA[:, t, :]), heads(YA[:, t, :]), col(st20[:, 4 * t:4 * t + 4], P), ALU.subtract))
            sums(YA, st20b, mlb(0, 0))
            done(ts(st20, st20b, 1.0 / P, LN_EPS, ALU.mult, ALU.add), var_ready)

            def gated(y, g, first):
                for t in range(TILES):
                    v = y[:, t, :]
                    done(tt(heads(v), heads(v), col(rstd[:, 4 * t:4 * t + 4], P), ALU.mult))
                    done(tt(v, v, GAIN[:, g, :], ALU.mult))
                    dve.wait_ge(unit_out, unit_no[("tm", ("oa", "zb")[g], t)] + 1)
                    done(tt(v, v, SG[t % 2], ALU.mult), gate_used)

            dve.wait_ge(rstd_ready, 1)
            dve.wait_ge(gain_loaded, 32)
            gated(YA, 0, 0)

            def conv(name, dst, g, first):
                for m in range(4):
                    dve.wait_ge(unit_out, unit_no[("fm", name, m, 1)] + 1)
                    c = 4 * g + m
                    o, i = dst[:, m, :], PRE[:, m, :]
                    done(ts(o, i, convw[:, 12 + c:13 + c], None, ALU.mult))
                    for a, e in ((0, P), (P, T)):
                        done(stt(o[:, a + 1:e], i[:, a:e - 1], convw[:, c:c + 1], o[:, a + 1:e], ALU.mult, ALU.add))
                    done(stt(o[:, 0:P - 1], i[:, 1:P], convw[:, 24 + c:25 + c], o[:, 0:P - 1], ALU.mult, ALU.add))
                    done(stt(o[:, P:T - 1], i[:, P + 1:T], convw[:, 24 + c:25 + c], o[:, P:T - 1], ALU.mult, ALU.add),
                         conv_done)

            def unit_norm(name, dst):
                for m in range(4):
                    dve.wait_ge(unit_out, unit_no[("ssq", name, m, 1)] + 1)
                    done(dve.reciprocal(NRM[:, m, :], NRM[:, m, :]))
                    done(tt(dst[:, m, :], dst[:, m, :], NRM[:, m, :], ALU.mult), normed)

            conv("vd", QT, 2, 0)
            conv("kd", KTR, 1, 4)
            unit_norm("kd", KTR)
            dve.wait_ge(unit_out, unit_no[("vtok", TILES - 1)] + 1)
            conv("qd", QT, 0, 8)
            unit_norm("qd", QT)

            dve.wait_ge(unit_out, unit_no[("ktok", "d", TILES - 1)] + 1)
            for s in range(TILES):
                q = 1 if s else 0
                bk = [[PS[:, 4 * d + n, :] for n in range(4)] for d in range(2)]
                for d in range(2):
                    dve.wait_ge(dl_de[d], s + 1)
                    dve.wait_ge(dl_kk[d], s + 1)
                    done(tt(dlb(d, 1), dlb(d, 0), bk[d][2], ALU.mult), dl_qd[d])
                    done(tt(dlb(d, 2), dlb(d, 0), bk[d][0], ALU.mult), dl_at[d])
                for n in range(1, 7):
                    for d in range(2):
                        dve.wait_ge(dl_p2[d], 6 * s + n)
                        if n < 6:
                            done(tt(dlb(d, 3), dlb(d, 3), bk[d][1], ALU.subtract), dl_x[d])
                        done(tt(dlb(d, 4), dlb(d, 4), bk[d][2], ALU.subtract), dl_xt[d])
                for d in range(2):
                    r = dlb(d, 2)
                    dve.wait_ge(dl_ks[d], s + 1)
                    dve.wait_ge(dl_cm[d], 6 * s + 6)
                    done(tt(heads(r), heads(bk[d][3]), col(ex(EG, d, s), P), ALU.mult))
                    done(tt(r, VTOK[:, tile_at(d, s), :], r, ALU.subtract), dl_r[d])
                for d in range(2):
                    dve.wait_ge(dl_tr[d], s + 1)
                    done(tt(heads(dlb(d, 3)), heads(bk[d][0]), col(v4(BETA)[:, d, s, :], P), ALU.mult), dl_vn[d])
                for d in range(2):
                    w = dlb(d, 0)
                    y = YB[:, tile_at(d, s), :]
                    dve.wait_ge(dl_o[d], s + 1)
                    done(tt(heads(w), heads(bk[d][1]), col(ex(EG, d, s), P), ALU.mult))
                    if s > 2 or (s == 0 and d == 1):
                        done(tt(w, w, bk[d][2], ALU.add))
                        done(tt(y, y, w, ALU.add))
                    else:
                        done(tt(y, w, bk[d][2], ALU.add))
                    c = SD[:, q, 4 * d:4 * d + 4, :]
                    done(tt(c, c, col(ex(ED, d, s), P), ALU.mult))
                    dve.wait_ge(dl_su[d], s + 1)
                    done(tt(c, c, heads(bk[d][3]), ALU.add), dl_done[d])

            sums(YB, st20b, dlb(0, 0))
            done(ts(st20, st20b, 1.0 / P, LN_EPS, ALU.mult, ALU.add), var_ready)
            dve.wait_ge(rstd_ready, 2)
            gated(YB, 1, TILES)
            count_y = [0]

            def residual(l):
                dve.wait_ge(bc_loaded, 64 * (3 * l + 1))
                for n in range(2):
                    for t in range(TILES):
                        j = TILES * n + t
                        dve.wait_ge(unit_out, unit_no[("out", l, n, t)] + 1)
                        c = slice(512 * n, 512 * n + 512)
                        done(tt(YO[j % 2], YO[j % 2], BC[:, min(t, 1), c], ALU.mult))
                        done(stt(X[:, t, c], X[:, t, c], ALPHA, YO[j % 2], ALU.mult, ALU.add), out_used)

            def layer_norm(nth):
                for t in range(TILES):
                    for n in range(2):
                        done(dve.bn_stats(bnst[:, t, n, :], X[:, t, 512 * n:512 * n + 512]))
                    done(dve.bn_aggr(bnag[:, t, :], bnst[:, t, :, :]))
                done(ts(lnr, bnag[:, :, 1], LN_EPS, None, ALU.add), var_ready)
                dve.wait_ge(rstd_ready, nth)
                for t in range(TILES):
                    done(ts(X[:, t, :], X[:, t, :], bnag[:, t, 0:1], lnr[:, t:t + 1], ALU.subtract, ALU.mult))
                    done(tt(X[:, t, :], X[:, t, :], BC[:, 2, :], ALU.mult))
                    done(tt(X[:, t, :], X[:, t, :], BC[:, 3, :], ALU.add), ln_done)

            residual(0)
            layer_norm(3)

            def first_max(values, vmax_, cand_, hot):
                done(dve.tensor_reduce(vmax_, values, AX.X, ALU.max))
                done(tt(cand_, values, vmax_.unsqueeze(2).to_broadcast([P, TILES, 4]), ALU.is_equal))
                done(stt(cand_, cand_, -100.0, IOTA[:, 0:4].unsqueeze(1).to_broadcast([P, TILES, 4]), ALU.mult, ALU.add))
                done(dve.tensor_reduce(cmin, cand_, AX.X, ALU.min))
                done(tt(hot, cand_, cmin.unsqueeze(2).to_broadcast([P, TILES, 4]), ALU.is_equal))

            def dve_moe(l):
                dve.wait_ge(bc_loaded, 64 * (3 * l + 2))
                for t in range(TILES):
                    v = min(t, 1)
                    if l:
                        pass
                    done(stt(H2[:, t, :], BC[:, 2 + v, :], 1.0, X[:, t, :], ALU.add, ALU.mult))
                    done(tt(H2[:, t, :], H2[:, t, :], BC[:, v, :], ALU.add), h2_ready)
                dve.wait_ge(unit_out, unit_no[("rt", l, TILES - 1)] + 1)
                dve.wait_ge(router_loaded, 16 * (8 + 7 * l))
                done(tt(LG[:, :, :], LG[:, :, :], RB.unsqueeze(1).to_broadcast([P, TILES, 20]), ALU.add))
                lg = LG[:, :, 0:4]
                first_max(lg, gmax, cand, ghot)
                g3 = gx[:, 0:20].rearrange("p (t c) -> p t c", t=TILES)
                done(tt(g3, lg, gmax.unsqueeze(2).to_broadcast([P, TILES, 4]), ALU.subtract))
                r4 = rtmp.rearrange("p (t g e) -> p t g e", t=TILES, g=4)
                done(tt(r4, LG[:, :, 4:20].rearrange("p t (g e) -> p t g e", g=4),
                        ghot.unsqueeze(3).to_broadcast([P, TILES, 4, 4]), ALU.mult))
                done(dve.tensor_reduce(LE, rtmp.rearrange("p (t g e) -> p t e g", t=TILES, g=4), AX.X, ALU.add))
                first_max(LE, vmax, cand, hot1)
                done(stt(LE2, hot1, NEG, LE, ALU.mult, ALU.add))
                first_max(LE2, vsec, cand, hot2)
                done(tt(gx[:, 20:25], vsec, vmax, ALU.subtract), route_arg)
                dve.wait_ge(route_exp, l + 1)
                done(dve.tensor_reduce(gsum, g3, AX.X, ALU.add))
                done(dve.reciprocal(gw, gsum))
                done(ts(gsum, gx[:, 20:25], 1.0, None, ALU.add))
                done(dve.reciprocal(gsum, gsum))
                done(tt(WSEL[:, 0, :], gsum, gw, ALU.mult))
                done(tt(WSEL[:, 1, :], WSEL[:, 0, :], gx[:, 20:25], ALU.mult))
                for c, hot in enumerate((hot1, hot2)):
                    done(tt(HE[:, c].rearrange("p t (g e) -> p t g e", g=4), ghot.unsqueeze(3).to_broadcast([P, TILES, 4, 4]),
                            hot.unsqueeze(2).to_broadcast([P, TILES, 4, 4]), ALU.mult))
                done(tt(HALL.rearrange("p (t e) -> p t e", t=TILES), HE[:, 0], HE[:, 1], ALU.add), hot_ready)
                dve.wait_ge(unit_out, unit_no[("cnt", l)] + 1)
                b5 = big[:, 0:80].rearrange("p (e j) -> p e j", e=16)
                done(tt(b5, CNT.unsqueeze(2).to_broadcast([P, 16, 5]), IOTA[:, 8:13].unsqueeze(1).to_broadcast([P, 16, 5]),
                        ALU.is_gt))
                done(dve.tensor_reduce(TSUM, b5, AX.X, ALU.add))
                dve.wait_ge(pool_const, 10)
                done(dve.tensor_tensor_scan(TCUM, TSUM, zero16, 0.0, ALU.add, ALU.add))
                done(tt(TBASE, TCUM, TSUM, ALU.subtract))
                done(ts(TBASE, TBASE, float(P), -1.0, ALU.mult, ALU.add))
                rk = RK.rearrange("p (t e) -> p t e", t=TILES)
                done(tt(rk, rk, TBASE.unsqueeze(1).to_broadcast([P, TILES, 16]), ALU.add))
                for c in range(2):
                    r3 = rtmp.rearrange("p (t e) -> p t e", t=TILES)
                    done(tt(r3, rk, HE[:, c], ALU.mult))
                    done(dve.tensor_reduce(slotf[:, TILES * c:TILES * c + TILES], r3, AX.X, ALU.add))
                done(dve.tensor_copy(IDX[:, :, :], slotf.rearrange("p (c t) -> p c t", c=2)))
                b16 = big.rearrange("p (i e) -> p i e", i=ETILES)
                done(tt(b16, TCUM.unsqueeze(1).to_broadcast([P, ETILES, 16]),
                        IOTA[:, 16:16 + ETILES].unsqueeze(2).to_broadcast([P, ETILES, 16]), ALU.is_le))
                done(dve.tensor_reduce(eotf, b16, AX.X, ALU.add))
                done(ts(eotf, eotf, float(NEXP - 1), None, ALU.min))
                done(dve.tensor_copy(tokid, IOTA[:, 48:53]))
                done(dve.tensor_copy(EOT, eotf), routed)

                def tile(j, u, first=False):
                    i = 3 * j + u
                    dve.wait_ge(silu_out, i + (ETILES * l + 1))
                    dve.tensor_tensor(HID[:, u], AU[:, u, :].rearrange("p (m c) -> p m c", m=2),
                                      PS[:, 2 + u, 256:512].rearrange("p (m c) -> p m c", m=2), ALU.mult).then_inc(hid_ready, 1)
                    if not first:
                        dve.wait_ge(ye_stored[u], 16 * j + (144 if u == 0 else 128) * l)
                    dve.wait_ge(down_done, i + (ETILES * l + 1))
                    dve.tensor_copy(YE[:, u, :].rearrange("p (h c) -> p h c", h=2), PS[:, 5:7, :]).then_inc(ye_ready, 1)

                for u in range(3):
                    tile(0, u, True)
                with dve.Fori(1, 8) as j:
                    for u in range(3):
                        tile(j, u)
                tile(8, 0)
                dve.wait_ge(ye_ready, ETILES * (l + 1))
                count["ye_ready"] = ETILES * (l + 1)
                dve.wait_ge(bc_loaded, 64 * (3 * l + 3))
                for t in range(TILES):
                    g = YG[:, t % 2]
                    dve.wait_ge(yg_gathered[t % 2], 32 * (t // 2 + 1 + l * (3 - t % 2)))
                    done(ts(g[:, 0, :], g[:, 0, :], WSEL[:, 0, t:t + 1], None, ALU.mult))
                    done(stt(g[:, 0, :], g[:, 1, :], WSEL[:, 1, t:t + 1], g[:, 0, :], ALU.mult, ALU.add))
                    done(tt(g[:, 0, :], g[:, 0, :], BC[:, min(t, 1), :], ALU.mult))
                    done(stt(X[:, t, :], X[:, t, :], ALPHA, g[:, 0, :], ALU.mult, ALU.add), yg_used)
                layer_norm(4 + 2 * l)

            dve_moe(0)

            def rotate(x, heads_, t):
                w = heads_ * HD
                tmp = RTMP[:, 0:w]
                cos, sin = (ROPE[:, a, t - 1, :] for a in range(2))
                xs = x.rearrange("p h (a f i) -> p h a f i", a=2, f=2)
                ys = tmp.rearrange("p (h a f i) -> p h a f i", h=heads_, a=2, f=2)
                sn = sin.rearrange("p (a f i) -> p a f i", a=2, f=2)
                for f in range(2):
                    done(tt(ys[:, :, :, f, :], xs[:, :, :, 1 - f, :],
                            sn[:, :, f, :].unsqueeze(1).to_broadcast([P, heads_, 2, HD // 4]), ALU.mult))
                done(tt(x, x, cos.unsqueeze(1).to_broadcast([P, heads_, HD]), ALU.mult))
                return tt(x, x, tmp.rearrange("p (h i) -> p h i", h=heads_), ALU.add)

            dve.wait_ge(attn_loaded, 80)
            for t in range(TILES):
                dve.wait_ge(unit_out, unit_no[("qkv", 2, t)] + 1)
                if t:
                    done(rotate(KD[:, t, :, 0, :], KVH, t))
                done(dve.tensor_copy(KD[:, t, :, 1, :], KD[:, t, :, 0, :]), keys_ready)
            for n in range(2):
                for t in range(TILES):
                    dve.wait_ge(unit_out, unit_no[("qkv", n, t)] + 1)
                    x = QR[:, t, 512 * n:512 * n + 512].rearrange("p (h i) -> p h i", h=8)
                    if t:
                        done(rotate(x, 8, t), queries_ready)
                    else:
                        done(dve.tensor_copy(RTMP[:, 0:1], x[:, 0, 0:1]), queries_ready)
            dve.wait_ge(unit_out, unit_no[("qT", TILES - 1, 1)] + 1)

            def normalise(g):
                c = slice(8 * g, 8 * g + 8)
                dve.wait_ge(sink_exp, g + 1)
                dve.wait_ge(pv_done, 8 * g + 8)
                done(tt(ES[:, c], ES[:, c], RS[:, c], ALU.add))
                done(dve.reciprocal(ES[:, c], ES[:, c]))
                o = QR[:, g // 2, 512 * (g % 2):512 * (g % 2) + 512].rearrange("p (h i) -> p h i", h=8)
                done(tt(o, PS[:, 6 + g % 2, :].rearrange("p (h i) -> p h i", h=8),
                        ES[:, c].unsqueeze(2).to_broadcast([P, 8, HD]), ALU.mult), o_ready)

            for n in range(STEPS):
                h = n % HC
                w = P * len(key_tiles(n // HC)[1])
                dve.wait_ge(s_done, n + 1)
                done(dve.tensor_reduce(NM[:, n:n + 1], PS[:, n % 3, 0:w], AX.X, ALU.max))
                done(ts(NM[:, n:n + 1], NM[:, n:n + 1], SINK[:, h:h + 1], -1.0, ALU.max, ALU.mult), max_ready)
                if n % 8 == 7:
                    done(tt(ES[:, n - 7:n + 1], SINK[:, h - 7:h + 1], NM[:, n - 7:n + 1], ALU.add), sink_arg)
                if n % 8 == 5 and n > 8:
                    normalise((n - 8) // 8)
            normalise(STEPS // 8 - 1)
            residual(1)
            layer_norm(5)
            dve_moe(1)

        @block.tensor
        def _(pe):
            def begin(name):
                n = unit_no[name]
                if n >= BANKS:
                    pe.wait_ge(unit_out, n - BANKS + 1)
                return PS[:, n % BANKS, :]

            def out_of(name):
                pe.wait_ge(unit_out, unit_no[name] + 1)

            def weights(item):
                n = load_no[item]
                pe.wait_ge(slot_arrived[slot_of(n)], arrived_at[n])
                return slot_cols(n, KT, 32 if item == ("in", "gates") else 512), slot_of(n)

            pe.wait_ge(const_loaded, 64)
            b = begin(("cT",))
            pe.transpose(b[:, 0:16], cin, CST[0:16, C_ID, 0:16]).then_inc(unit_done, 1)
            b = begin(("convT",))
            pe.transpose(b[:, 0:36], convrow, CST[0:36, C_ID, 0:36]).then_inc(unit_done, 1)

            def mod_rows(l, mrow):
                out_of(("cT",))
                for c in range(12):
                    b = begin(("mod", l, c))
                    w, s = weights(("mod", l, c))
                    for k in range(KT):
                        pe.matmul(b[0:2, :], csil[:, k:16:8], w[:, k, :], start=(k == 0), stop=False)
                    i = pe.matmul(b[0:2, :], CST[0:1, C_ONES, 0:2], SLOTS[0:1, s, 4096:4608], start=False, stop=True)
                    i.then_inc(unit_done, 1)
                    if c < 4:
                        b = begin(("modT", l, c))
                        out_of(("mod", l, c))
                        for q in range(4):
                            i = pe.transpose(b[:, 2 * q:2 * q + 2], mrow[:, c % 2, q * P:(q + 1) * P], CST[0:2, C_ID, 0:2])
                        i.then_inc(unit_done, 1)

            def transposes_of_x(l):
                for k in range(KT):
                    b = begin(("hTlat", l, k))
                    for t in range(1, TILES):
                        i = pe.transpose(b[:, (t - 1) * P:t * P], X[:, t, k * P:(k + 1) * P], ident)
                    i.then_inc(unit_done, 1)
                for g in range(2):
                    b = begin(("hTctx", l, g))
                    for q in range(4):
                        i = pe.transpose(b[:, q * P:(q + 1) * P], X[:, 0, (4 * g + q) * P:(4 * g + q + 1) * P], ident)
                    i.then_inc(unit_done, 1)

            def feature_major(name):
                w, s = weights(("in", name))
                for m in range(4):
                    for h in range(2):
                        b = begin(("fm", name, m, h))
                        for k in range(KT):
                            i = pe.matmul(b[:, 0:320], w[:, k, m * P:(m + 1) * P], HT[:, k, 320 * h:320 * h + 320],
                                          start=(k == 0), stop=(k == KT - 1))
                        i.then_inc(unit_done, 1)

            def token_major(name, width=512):
                w, s = weights(("in", name))
                for t in range(TILES):
                    b = begin(("tm", name, t))
                    for k in range(KT):
                        i = pe.matmul(b[:, 0:width], HT[:, k, t * P:(t + 1) * P], w[:, k, :],
                                      start=(k == 0), stop=(k == KT - 1))
                    i.then_inc(unit_done, 1)

            def head_transposes(name, src):
                for t in range(TILES):
                    b = begin(name + (t,))
                    for h in range(HEADS):
                        i = pe.transpose(b[:, h * P:(h + 1) * P], src[:, h, t * P:(t + 1) * P], ident)
                    i.then_inc(unit_done, 1)

            mod_rows(0, MROW)
            pe.wait_ge(x_loaded, 32)
            transposes_of_x(0)
            out_of(("hTctx", 0, 1))
            token_major("gates", 32)
            pe.wait_ge(gate_lf, 1)
            for d in range(2):
                b = begin(("cs", d))
                pe.matmul(b[:, 0:40], CST[:, (C_UPI, C_LOI)[d], :], LF[:, 40 * d:40 * d + 40], start=True, stop=True)\
                    .then_inc(unit_done, 1)
            b = begin(("ce",))
            pe.matmul(b[:, 0:80], ones, LF, start=True, stop=True).then_inc(unit_done, 1)
            for name, src, c in (("rowf", v8(LF), 0), ("rowi", raw4, 0)):
                for d in range(2):
                    for part, steps in enumerate((range(4), range(4, 5))):
                        b = begin((name, d, part))
                        for j, s in enumerate(steps):
                            i = pe.matmul(b[0:4, j * P:(j + 1) * P], src[:, d, s, 0:4], (ident, flip)[d], start=True, stop=True)
                        i.then_inc(unit_done, 1)
            for d in range(2):
                b = begin(("mcol", d))
                pe.wait_ge(m_scanned, d + 1)
                for s in range(TILES):
                    i = pe.matmul(b[:, 4 * s:4 * s + 4], MR[:, d, s * P:(s + 1) * P], CST[0:4, C_ID, 0:4], start=True, stop=True)
                i.then_inc(unit_done, 1)
            b = begin(("mflip",))
            out_of(("mcol", 1))
            pe.matmul(b[:, 0:20], flip, rev, start=True, stop=True).then_inc(unit_done, 1)
            b = begin(("mvb",))
            pe.wait_ge(mex_ready, 1)
            pe.matmul(b[:, 0:56], CST[0:4, C_ONES, :], MEX[0:4, :], start=True, stop=True).then_inc(unit_done, 1)
            feature_major("qa")
            feature_major("ka")
            token_major("va")
            out_of(("fm", "ka", 3, 1))
            head_transposes(("ktok", "a"), KTR)

            out_of(("ktok", "a", TILES - 1))
            pe.wait_ge(state_loaded, 48)
            pe.wait_ge(pool_const, 8)
            pe.wait_ge(exp_ready, 1)

            def decay(d, s, which, bank_):
                for h in range(HEADS):
                    o = bank_[:, h * P:(h + 1) * P]
                    v = v4(RV[:, which, :])[:, d, s, h:h + 1]
                    pe.matmul(o, v.to_broadcast([P, P]), ident, start=True, stop=False)
                    i = pe.matmul(o, ident, CST[:, (C_NF, C_NB)[d], :], start=False, stop=True)
                return i

            for s in range(TILES):
                q = 1 if s else 0
                for d in range(2):
                    A, Bk, C, E = (PS[:, 4 * d + n, :] for n in range(4))
                    tk = slice(tile_at(d, s) * P, tile_at(d, s) * P + P)
                    if s:
                        pe.wait_ge(ml_done[d], s)
                    for h in range(HEADS):
                        i = pe.matmul(A[:, h * P:(h + 1) * P], KTR[:, h, tk], QT[:, h, tk], start=True, stop=True)
                    i.then_inc(ml_st[d], 1)
                    decay(d, s, 0, Bk).then_inc(ml_db[d], 1)
                for d in range(2):
                    A, Bk, C, E = (PS[:, 4 * d + n, :] for n in range(4))
                    t = tile_at(d, s)
                    tk = slice(t * P, t * P + P)
                    pe.wait_ge(ml_sw[d], s + 1)
                    for h in range(HEADS):
                        sw = mlb(d, 1)[:, h * P:(h + 1) * P]
                        pe.matmul(A[:, h * P:(h + 1) * P], sw, VTOK[:, t, h * P:(h + 1) * P], start=True, stop=True)
                        pe.matmul(E[:, h:h + 1], sw, CST[:, C_ONES, 0:1], start=True, stop=True)
                        pe.matmul(Bk[:, h * P:(h + 1) * P], QT[:, h, tk], SM[:, q, 4 * d + h, :], start=True, stop=True)
                        pe.matmul(E[:, 4 + h:5 + h], QT[:, h, tk], NS[:, q, 4 * d + h:4 * d + h + 1], start=True, stop=True)
                    pe.wait_ge(ml_vw[d], s + 1)
                    for h in range(HEADS):
                        kk = KTOK[:, t, h * P:(h + 1) * P]
                        pe.matmul(C[:, h * P:(h + 1) * P], kk, mlb(d, 2)[:, h * P:(h + 1) * P], start=True, stop=True)
                        i = pe.matmul(E[:, 8 + h:9 + h], kk, v4(EX[:, WE, :])[:, d, s, h:h + 1], start=True, stop=True)
                    i.then_inc(ml_u[d], 1)
            for d in range(2):
                pe.wait_ge(ml_done[d], TILES)
            token_major("oa")
            feature_major("vd")
            pe.wait_ge(silu_done, 4)
            head_transposes(("vtok",), QT)
            feature_major("kd")

            def square_sums(name, first):
                for m in range(4):
                    for h in range(2):
                        b = begin(("ssq", name, m, h))
                        pe.wait_ge(sq_ready, first + m + 1)
                        pe.matmul(b[:, 0:320], ones, SQ[:, m, 320 * h:320 * h + 320], start=True, stop=True)\
                            .then_inc(unit_done, 1)

            square_sums("kd", 0)
            pe.wait_ge(normed, 4)
            head_transposes(("ktok", "d"), KTR)
            feature_major("qd")
            square_sums("qd", 4)
            pe.wait_ge(normed, 8)

            out_of(("ssq", "qd", 3, 1))
            for s in range(TILES):
                q = 1 if s else 0
                bk = [[PS[:, 4 * d + n, :] for n in range(4)] for d in range(2)]

                def mm4(o, lhsT, rhs):
                    for h in range(HEADS):
                        c = slice(h * P, (h + 1) * P)
                        i = pe.matmul(o[:, c], lhsT[:, c], rhs[:, c], start=True, stop=True)
                    return i

                for d in range(2):
                    A, Bk, C, E = bk[d]
                    tk = slice(tile_at(d, s) * P, tile_at(d, s) * P + P)
                    if s:
                        pe.wait_ge(dl_done[d], s)
                    for h in range(HEADS):
                        c = slice(h * P, (h + 1) * P)
                        pe.matmul(A[:, c], KTR[:, h, tk], KTR[:, h, tk], start=True, stop=True)
                        i = pe.matmul(C[:, c], KTR[:, h, tk], QT[:, h, tk], start=True, stop=True)
                    i.then_inc(dl_kk[d], 1)
                    decay(d, s, 1, Bk).then_inc(dl_db[d], 1)
                    for h in range(HEADS):
                        c = slice(h * P, (h + 1) * P)
                        i = pe.matmul(E[:, c], KTR[:, h, tk], SD[:, q, 4 * d + h, :], start=True, stop=True)
                    i.then_inc(dl_ks[d], 1)
                for d in range(2):
                    pe.wait_ge(dl_xt1[d], s + 1)
                    for h in range(HEADS):
                        c = slice(h * P, (h + 1) * P)
                        i = pe.transpose(bk[d][0][:, c], dlb(d, 4)[:, c], ident)
                    i.then_inc(dl_x1t[d], 1)
                for n in range(1, 7):
                    for d in range(2):
                        if n == 1:
                            pe.wait_ge(dl_x1[d], s + 1)
                        else:
                            pe.wait_ge(dl_x[d], 5 * s + n - 1)
                        pe.wait_ge(dl_cm[d], 6 * s + n)
                        mm4(bk[d][0], dlb(d, 5 + n % 2), dlb(d, 3)).then_inc(dl_p1[d], 1)
                    for d in range(2):
                        pe.wait_ge(dl_p1s[d], 6 * s + n)
                        pe.wait_ge(dl_xt[d], 6 * s + n - 1) if n > 1 else pe.wait_ge(dl_qd[d], s + 1)
                        if n < 6:
                            mm4(bk[d][1], dlb(d, 4), dlb(d, 0))
                        mm4(bk[d][2], dlb(d, 0), dlb(d, 4)).then_inc(dl_p2[d], 1)
                for d in range(2):
                    A, Bk, C, E = bk[d]
                    tk = slice(tile_at(d, s) * P, tile_at(d, s) * P + P)
                    for h in range(HEADS):
                        c = slice(h * P, (h + 1) * P)
                        pe.matmul(Bk[:, c], QT[:, h, tk], SD[:, q, 4 * d + h, :], start=True, stop=True)
                    pe.wait_ge(dl_xt[d], 6 * s + 6)
                    pe.wait_ge(dl_r[d], s + 1)
                    mm4(A, dlb(d, 4), dlb(d, 2)).then_inc(dl_tr[d], 1)
                for d in range(2):
                    A, Bk, C, E = bk[d]
                    pe.wait_ge(dl_vn[d], s + 1)
                    mm4(C, dlb(d, 1), dlb(d, 3)).then_inc(dl_o[d], 1)
                    pe.wait_ge(dl_vw[d], s + 1)
                    mm4(E, KTOK[:, tile_at(d, s), :], dlb(d, 2)).then_inc(dl_su[d], 1)
            for d in range(2):
                pe.wait_ge(dl_done[d], TILES)
            token_major("zb")
            pe.wait_ge(gate_used, 2 * TILES)
            out_of(("tm", "zb", TILES - 1))

            def y_transposes(l, head):
                for k in range(KT):
                    for part, tiles in enumerate((range(4), range(4, 5))):
                        b = begin(("yT", l, k, part))
                        for j, t in enumerate(tiles):
                            i = pe.transpose(b[:, j * P:(j + 1) * P], head(k, t), ident)
                        i.then_inc(unit_done, 1)
                out_of(("yT", l, KT - 1, 1))

            def out_proj(l):
                for n in range(2):
                    w, s = weights(("wout", l, n))
                    for t in range(TILES):
                        b = begin(("out", l, n, t))
                        for k in range(KT):
                            i = pe.matmul(b, HT[:, k, t * P:(t + 1) * P], w[:, k, :], start=(k == 0), stop=(k == KT - 1))
                        i.then_inc(unit_done, 1)
    
            y_transposes(0, lambda k, t: (YA, YB)[k // 4][:, t, (k % 4) * P:(k % 4 + 1) * P])
            out_proj(0)

            def pe_moe(l):
                for k in range(KT):
                    for part, tiles in enumerate((range(4), range(4, 5))):
                        b = begin(("h2T", l, k, part))
                        for j, t in enumerate(tiles):
                            pe.wait_ge(h2_ready, TILES * l + t + 1)
                            i = pe.transpose(b[:, j * P:(j + 1) * P], H2[:, t, k * P:(k + 1) * P], ident)
                        i.then_inc(unit_done, 1)
                out_of(("h2T", l, KT - 1, 1))
                pe.wait_ge(router_loaded, 16 * (8 + 7 * l))
                for t in range(TILES):
                    b = begin(("rt", l, t))
                    for k in range(KT):
                        i = pe.matmul(b[:, 0:20], H2T[:, k, t * P:(t + 1) * P], RW[:, k, :], start=(k == 0), stop=(k == KT - 1))
                    i.then_inc(unit_done, 1)
                pe.wait_ge(hot_ready, l + 1)
                b = begin(("rank", l))
                for t in range(TILES):
                    for s in range(t + 1):
                        i = pe.matmul(b[:, 16 * t:16 * t + 16], ones if s < t else CST[:, C_UPI, :], HALL[:, 16 * s:16 * s + 16],
                                      start=(s == 0), stop=(s == t))
                i.then_inc(unit_done, 1)
                b = begin(("cnt", l))
                for t in range(TILES):
                    i = pe.matmul(b[:, 0:16], ones, HALL[:, 16 * t:16 * t + 16], start=(t == 0), stop=(t == TILES - 1))
                i.then_inc(unit_done, 1)
                out_of(("cnt", l))
                n0 = load_no[("moe", l)]

                def transposes(i, u, j, first=False):
                    pe.wait_ge(rows_gathered[u], 16 * j + (16 + (144 if u == 0 else 128) * l))
                    if not first:
                        pe.wait_ge(xt_out, i + ETILES * l)
                    for k in range(KT):
                        m = pe.transpose(PS[:, k // 4, (k % 4) * P:(k % 4 + 1) * P], XG[:, u, k * P:(k + 1) * P], ident)
                    m.then_inc(xt_done, 1)

                def tile(j, u, last=False, first=False):
                    i = 3 * j + u
                    w = SLOTS[:, u, :]
                    gate, up = (w[:, 2048 * m:2048 * m + 2048].rearrange("p (k c) -> p k c", k=KT) for m in range(2))
                    down = w[:, 4096:6144].rearrange("p (k c) -> p k c", k=2)
                    pe.wait_ge(slot_arrived[u], 48 * j + arrived_at[n0 + u])
                    pe.wait_ge(xt_out, i + (ETILES * l + 1))
                    if not first:
                        pe.wait_ge(hid_ready, i + (ETILES * l - 2))
                    for m in range(4):
                        for k in range(KT):
                            x = pe.matmul(PS[:, 2 + u, m * P:(m + 1) * P], (gate, up)[m // 2][:, k, (m % 2) * P:(m % 2 + 1) * P],
                                          XGT[:, u, k, :], start=(k == 0), stop=(k == KT - 1))
                    x.then_inc(gu_done, 1)
                    if not last:
                        un = (u + 1) % 3
                        transposes(i + 1, un, j + (u + 1) // 3)
                    pe.wait_ge(hid_ready, i + (ETILES * l + 1))
                    pe.wait_ge(ye_ready, i + ETILES * l)
                    for h in range(2):
                        for m in range(2):
                            x = pe.matmul(PS[:, 5 + h, :], HID[:, u, m, :], down[:, m, 512 * h:512 * h + 512],
                                          start=(m == 0), stop=(m == 1))
                    x.then_inc(down_done, 1)

                transposes(0, 0, 0, first=True)
                for u in range(3):
                    tile(0, u, first=True)
                with pe.Fori(1, 8) as j:
                    for u in range(3):
                        tile(j, u)
                tile(8, 0, last=True)

            pe_moe(0)

            pe.wait_ge(ye_ready, ETILES)
            mod_rows(1, MROW)
            pe.wait_ge(ln_done, 2 * TILES)
            transposes_of_x(1)
            out_of(("hTctx", 1, 1))
            for n in (2, 0, 1):
                w, _ = weights(("qkv", n))
                for t in range(TILES):
                    b = begin(("qkv", n, t))
                    for k in range(KT):
                        i = pe.matmul(b, HT[:, k, t * P:(t + 1) * P], w[:, k, :], start=(k == 0), stop=(k == KT - 1))
                    i.then_inc(unit_done, 1)
            for t in range(TILES + 1):
                b = begin(("kT", t))
                if t < TILES:
                    pe.wait_ge(keys_ready, t + 1)
                else:
                    pe.wait_ge(attn_loaded, 80)
                for g in range(KVH):
                    i = pe.transpose(b[:, g * P:(g + 1) * P], KD[:, t, g, :, :].rearrange("p r i -> p (r i)"), ident)
                i.then_inc(unit_done, 1)
            for t in range(TILES):
                for g in range(2):
                    b = begin(("qT", t, g))
                    pe.wait_ge(queries_ready, TILES * g + t + 1)
                    for q in range(4):
                        i = pe.transpose(b[:, q * P:(q + 1) * P], QR[:, t, 512 * g + q * P:512 * g + (q + 1) * P], ident)
                    i.then_inc(unit_done, 1)
            out_of(("qT", TILES - 1, 1))

            def scores(n):
                t, h = n // HC, n % HC
                local, cols = key_tiles(t)
                b = PS[:, n % 3, :]
                r = slice(HD * (h % 2), HD * (h % 2) + HD)
                q = QTT[r, h // 2, t * P:(t + 1) * P]
                kk = KTT[r, h // 4, :]
                if n >= 3:
                    pe.wait_ge(p_ready, n - 2)
                for j, kt in enumerate(cols):
                    o = b[:, j * P:(j + 1) * P]
                    m = {t - 1: C_NF, t + 1: C_NB}.get(kt) if t and kt < TILES else None
                    i = pe.matmul(o, q, kk[:, kt * P:(kt + 1) * P], start=True, stop=m is None)
                    if m is not None:
                        i = pe.matmul(o, ident, CST[:, m, :], start=False, stop=True)
                i.then_inc(s_done, 1)

            def weight_transposes(n):
                pe.wait_ge(p_ready, n + 1)
                if n >= 3:
                    pe.wait_ge(pt_out, n - 2)
                for j in range(len(key_tiles(n // HC)[1])):
                    i = pe.transpose(PS[:, 3 + n % 3, j * P:(j + 1) * P], PB[:, n % 3, j * P:(j + 1) * P], ident)
                i.then_inc(pt_done, 1)

            def values(n):
                t, h = n // HC, n % HC
                cols = key_tiles(t)[1]
                pe.wait_ge(pt_out, n + 1)
                if h % 8 == 0 and n >= HC:
                    pe.wait_ge(o_ready, n // 8 - 1)
                for j, kt in enumerate(cols):
                    i = pe.matmul(PS[:, 6 + h // 8, HD * (h % 8):HD * (h % 8) + HD], PTB[:, n % 3, j * P:(j + 1) * P],
                                  V[:, kt, HD * (h // 4):HD * (h // 4) + HD], start=(j == 0), stop=(j == len(cols) - 1))
                i.then_inc(pv_done, 1)

            for n in range(STEPS + 3):
                if n < STEPS:
                    scores(n)
                if 2 <= n < STEPS + 2:
                    weight_transposes(n - 2)
                if n >= 3:
                    values(n - 3)
            pe.wait_ge(o_ready, STEPS // 8)
            y_transposes(1, lambda k, t: QR[:, t, k * P:(k + 1) * P])
            out_proj(1)
            pe_moe(1)


_OUTS = [((1, P, D), "float32"), ((1, LAT, D), "float32"), ((1, 1, 2, HEADS, P, P), "float32"),
         ((1, 1, 2, HEADS, P), "float32"), ((1, 1, 2, HEADS), "float32"), ((1, 1, 2, HEADS, P, P), "float32"),
         ((1, 1, KVH, P, HD), "float32"), ((1, 1, KVH, P, HD), "float32")]


def kernel(**inputs):
    import numpy as _np
    import concourse.bacc as _bacc
    from concourse import mybir as _mybir
    from concourse.bass_utils import run_bass_kernel_spmd as _run

    nc = _bacc.Bacc("TRN2", target_bir_lowering=False, num_devices=1)
    data = dict(inputs)
    data["consts"] = constants()
    data["ropes"] = rope_tables()
    data["iotas"] = iotas()
    arrays, ins = {}, {}
    for name, a in data.items():
        a = _np.ascontiguousarray(a)
        arrays[f"in_{name}"] = a
        ins[name] = nc.dram_tensor(f"in_{name}", a.shape, _mybir.dt.from_np(a.dtype), kind="ExternalInput").ap()
    outs = [nc.dram_tensor(f"out_{i}", s, _mybir.dt.from_np(_np.dtype(t)), kind="ExternalOutput").ap()
            for i, (s, t) in enumerate(_OUTS)]
    build(nc, ins, outs)
    r = _run(nc, [arrays], core_ids=[0])
    return tuple(r.results[0][f"out_{i}"] for i in range(len(_OUTS)))
```

```python
import concourse.bass as bass
from concourse import mybir
from contextlib import ExitStack
import numpy as np

D = 1024
P = 128
KT = D // P
TILES = 5
T = TILES * P
LAT = T - P
HEADS = 4
HW = HEADS * P
DEPTH = 2
EVEN_IN = 4128
NEXP, GRP, EPG, FF = 16, 4, 4, 256
HC, KVH, HD = 16, 4, 64
ALPHA = float((2 * DEPTH) ** 0.25)
LN_EPS = 1e-5
NEG = -1e30
SLOT = 6144
NSLOT = 3
ETILES = 27
GROUPS = ETILES // 3
SURE = -(-NEXP // 3)
SLOTS_E = ETILES * P
KSLOT = 0
BANKS = 8
SMALLS = 2392

C_ID, C_FLIP, C_UPI, C_LOI, C_ONES, C_NF, C_NB = range(7)
C_LEV = (7, 14)
N_CONST = 21


def constants():
    p, f = np.meshgrid(np.arange(P), np.arange(P), indexing="ij")
    m = np.zeros((N_CONST, P, P), np.float32)
    m[C_ID] = p == f
    m[C_FLIP] = p + f == P - 1
    m[C_UPI] = p <= f
    m[C_LOI] = p >= f
    m[C_ONES] = 1.0
    m[C_NF] = np.where(p <= f, 0.0, NEG)
    m[C_NB] = np.where(p >= f, 0.0, NEG)
    for n in range(7):
        b = 1 << n
        u = (p // (2 * b) == f // (2 * b)) & (p % (2 * b) < b) & (f % (2 * b) >= b)
        m[C_LEV[0] + n] = u
        m[C_LEV[1] + n] = u.T
    return np.ascontiguousarray(m.transpose(1, 0, 2))


def iotas():
    m = np.zeros((P, 66), np.float32)
    m[0::32, 64] = 1.0
    m[16::32, 65] = 1.0
    m[:, 0:4] = np.arange(4)
    m[:, 8:13] = P * np.arange(TILES)
    m[:, 16:16 + ETILES] = np.arange(ETILES)
    m[:, 53:53 + GROUPS] = 3 * np.arange(GROUPS)
    m[:, 48:53] = np.arange(P)[:, None] + P * np.arange(TILES)
    return m


def rope_tables():
    half = HD // 4
    inv = 10000.0 ** (-np.arange(half, dtype=np.float32) / half)
    t = np.arange(LAT)
    out = np.zeros((2, LAT, 2, 2, half), np.float32)
    for a, pos in enumerate((t // 64, t % 64)):
        ang = pos.astype(np.float32)[:, None] * inv[None, :].astype(np.float32)
        out[0, :, a, :, :] = np.cos(ang)[:, None, :]
        out[1, :, a, 0, :] = -np.sin(ang)
        out[1, :, a, 1, :] = np.sin(ang)
    return np.ascontiguousarray(out.reshape(2, TILES - 1, P, HD).transpose(2, 0, 1, 3))


def tile_at(d, s):
    return s if d == 0 or s == 0 else TILES - s


def modulation_parts():
    order = [(l, c) for l in range(DEPTH) for c in range(12)]
    sizes = {"first": 4, "qa": 1, "ka": 1, "va": 1, "vd": 2, "kd": 2, "kd2": 2, "qd": 2, "qd2": 2, "norm": 3, "moe": 4}
    assert sum(sizes.values()) == len(order)
    out, a = {}, 0
    for name, n in sizes.items():
        out[name] = order[a:a + n]
        a += n
    return out


def weight_loads():
    parts = modulation_parts()

    def mod(name):
        return [("mod",) + lc for lc in parts[name]]

    out = mod("first") + [("in", "gates")]
    for n in ("qa", "ka", "va"):
        out += [("in", n)] + mod(n)
    out += [("in", "oa"), ("in", "vd")] + mod("vd") + [("in", "kd")] + mod("kd") + mod("kd2")
    out += [("in", "qd")] + mod("qd") + mod("qd2") + [("in", "zb")]
    out += [("wout", 0, n) for n in range(2)] + mod("norm")
    out += [("moe", 0)] + mod("moe")
    out += [("qkv", n) for n in (2, 0, 1)] + [("wout", 1, n) for n in range(2)]
    out += [("moe", 1)]
    return out


def unit_order():
    u = [("cT",)]
    u += [("convT",)]

    def mod(name):
        out, part = [], modulation_parts()[name]
        for j, (l, c) in enumerate(part):
            out += [("mod",) + lc for lc in (part[0:2] if j == 0 else part[j + 1:j + 2])]
            out.append(("modS", l, c))
            if c < 4:
                out.append(("modT", l, c))
        return out

    def hT(l):
        return [("hTlat", l, k) for k in range(KT)] + [("hTctx", l, g) for g in range(2)]

    def fm(name):
        return [("fm", name, m, half) for m in range(4) for half in range(2)]

    def tm(name):
        return [("tm", name, t) for t in range(TILES)]

    u += mod("first") + hT(0) + tm("gates")
    u += fm("qa") + mod("qa")
    u += [("cs", 0), ("cs", 1), ("ce",)]
    u += [(n, d, part) for n in ("rowf", "rowi") for d in range(2) for part in range(2)]
    u += fm("ka") + mod("ka")
    u += [("mcol", 0), ("mcol", 1), ("mflip",), ("mvb",)]
    u += tm("va") + mod("va") + [("ktok", "a", t) for t in range(TILES)]
    u += tm("oa")
    u += fm("vd") + mod("vd") + [("vtok", t) for t in range(TILES)]
    u += fm("kd") + mod("kd") + [("ssq", "kd", m, half) for m in range(4) for half in range(2)]
    u += mod("kd2") + [("ktok", "d", t) for t in range(TILES)]
    u += fm("qd") + mod("qd") + [("ssq", "qd", m, half) for m in range(4) for half in range(2)]
    u += mod("qd2")
    u += tm("zb")
    u += [("yT", 0, k, part) for k in range(KT) for part in range(2)]
    u += [("out", 0, n, t) for n in range(2) for t in range(TILES)]

    def router(l):
        out = []
        for t in range(TILES + 1):
            if t < TILES:
                out += [("h2T", l, t, g) for g in range(2)]
            if t:
                out.append(("rt", l, t - 1))
        return out + [("iota", l), ("rank", l), ("cnt", l), ("tok", l)]

    u += mod("norm") + router(0)
    u += mod("moe") + hT(1)
    u += [("qkv", n, t) for n in (2, 0, 1) for t in range(TILES)]
    u += [("kT", t, r) for t in range(TILES + 1) for r in range(2)]
    u += [("qT", t, g) for t in range(TILES) for g in range(2)]
    u += [("yT", 1, k, part) for k in range(KT) for part in range(2)]
    u += [("out", 1, n, t) for n in range(2) for t in range(TILES)]
    u += router(1)
    return u


def build(nc, ins, outs):
    f32 = mybir.dt.float32
    ALU = mybir.AluOpType
    ACT = mybir.ActivationFunctionType
    AX = mybir.AxisListType

    ctx = ExitStack()
    with ctx:
        def sb(name, shape, dt=f32):
            return ctx.enter_context(nc.sbuf_tensor(name, shape, dt))

        def sem(name):
            return ctx.enter_context(nc.semaphore(name))

        X = sb("X", [P, TILES, D])
        HT = sb("HT", [P, KT, T])
        SLOTS = sb("SLOTS", [P, NSLOT, SLOT])
        CST = sb("CST", [P, N_CONST, P])
        Z = sb("Z", [P, 6 * 2560])
        QT, KTR = (Z[:, n * 2560:(n + 1) * 2560].rearrange("p (h t) -> p h t", h=HEADS) for n in range(2))
        KTOK, VTOK, YA, YB = (Z[:, n * 2560:(n + 1) * 2560].rearrange("p (t c) -> p t c", t=TILES) for n in range(2, 6))
        H2T = Z[:, 0:5120].rearrange("p (k t) -> p k t", k=KT)
        H2 = Z[:, 10240:15360].rearrange("p (t c) -> p t c", t=TILES)
        XG = Z[:, 0:3072].rearrange("p (b c) -> p b c", b=3)
        XGT = Z[:, 3072:6144].rearrange("p (b k c) -> p b k c", b=3, k=KT)
        YE = Z[:, 6144:9216].rearrange("p (b c) -> p b c", b=3)
        AU = Z[:, 9216:9984].rearrange("p (b c) -> p b c", b=3)
        HID = Z[:, 9984:10752].rearrange("p (b m c) -> p b m c", b=3, m=2)
        HIDR = Z[:, 10752:11520].rearrange("p (b c) -> p b c", b=3)
        YG = Z[:, 0:4096].rearrange("p (b j c) -> p b j c", b=2, j=2)
        BC = sb("BC", [P, 4, D])
        SMALL = sb("SMALL", [P, SMALLS])
        PS = ctx.enter_context(nc.psum_tensor("PS", [P, BANKS, 512], f32))

        at = [0]

        def small(n):
            a = at[0]
            at[0] += n
            assert at[0] <= SMALLS, at[0]
            return SMALL[:, a:a + n]

        ident, flip, ones = CST[:, C_ID, :], CST[:, C_FLIP, :], CST[:, C_ONES, :]
        SCR = SLOTS[:, 2, :]
        PRE = Z[:, 12800:15360].rearrange("p (m t) -> p m t", m=4)
        BCF = BC[:, :, :].rearrange("p a b -> p (a b)")
        SM = BCF[:, 0:2048].rearrange("p (s u v) -> p s u v", s=2, u=2 * HEADS)
        SD = BCF[:, 2048:4096].rearrange("p (s u v) -> p s u v", s=2, u=2 * HEADS)

        csil = small(KT * 32)
        MODT = [small(KT * 4).rearrange("p (k j) -> p k j", k=KT) for _ in range(DEPTH)]
        convw = small(36)
        MSUM = SLOTS[:, 0, 5120:6144].rearrange("p (b c) -> p b c", b=2)
        MROW = MSUM[0:2]
        CMB = SLOTS[:, 0, 5120:6144].rearrange("p (d c) -> p d c", d=2)
        GAIN = SLOTS[:, 1, 4608:5632].rearrange("p (g c) -> p g c", g=2)
        SG = [SLOTS[:, 0, 4608:5120], SLOTS[:, 1, 5632:6144]]
        SQ = SCR[:, 0:2560].rearrange("p (m t) -> p m t", m=4)
        NRM = SCR[:, 2560:5120].rearrange("p (m t) -> p m t", m=4)
        graw = small(TILES * 32).rearrange("p (t c) -> p t c", t=TILES)
        raw = small(2 * TILES * 16)
        raw4 = raw.rearrange("p (d s c) -> p d s c", d=2, s=TILES)
        gbias = small(32).rearrange("p (d c) -> p d c", d=2)
        alog = small(8)
        lcoef = small(16).rearrange("p (d c) -> p d c", d=2)
        zf = small(2 * TILES * 8)
        zabs = small(2 * TILES * 8)
        zexp = zln = zabs
        LF = small(2 * TILES * 8)
        CS = small(2 * TILES * 8)
        CE = small(2 * TILES * 8)
        MC = small(2 * TILES * 4)
        rev = small(TILES * 4)
        MVB = small(56)
        MV = small(14)
        MEX = small(56)
        M0 = small(2)
        BETA = small(2 * TILES * 4)
        ARG = small(7 * 40).rearrange("p (n c) -> p n c", n=7)
        EX = small(7 * 40).rearrange("p (n c) -> p n c", n=7)
        WI, EN, WE, DC, EG, EE, ED = range(7)
        RV = small(2 * 40).rearrange("p (n c) -> p n c", n=2)
        CB = small(2 * 40).rearrange("p (n c) -> p n c", n=2)
        NS = small(16).rearrange("p (s u) -> p s u", s=2)
        t4 = small(8)
        t4b = small(8)
        st20 = small(20)
        st20b = small(20)
        half = small(20)
        rstd = small(20)
        bnst = ARG[:, 0:2, :].rearrange("p n c -> p (n c)")[:, 0:TILES * 12].rearrange("p (t s c) -> p t s c", t=TILES, s=2)
        bnag = ARG[:, 2, 0:TILES * 2].rearrange("p (t c) -> p t c", t=TILES)
        lnr = small(TILES)
        eps = small(2)

        def v4(x):
            return x.rearrange("p (d s h) -> p d s h", d=2, s=TILES)

        def v8(x):
            return x.rearrange("p (d s h) -> p d s h", d=2, s=TILES)

        def heads(x):
            return x.rearrange("p (h v) -> p h v", h=HEADS)

        def col(x, n):
            return x.unsqueeze(2).to_broadcast([P, HEADS, n])

        ROWF = SCR[0:4, 0:2 * T].rearrange("p (d t) -> p d t", d=2)
        ROWI = SCR[0:4, 2 * T:4 * T].rearrange("p (d t) -> p d t", d=2)
        MR = SCR[0:4, 4 * T:6 * T].rearrange("p (d t) -> p d t", d=2)
        cin = SCR[0:16, 0:P]
        convrow = SCR[0:36, P:2 * P]

        def mlb(d, n):
            return SCR[:, (4 * d + n) * 512:(4 * d + n + 1) * 512]

        def dlb(d, n):
            if n == 6:
                return CMB[:, d, :]
            return SCR[:, (6 * d + n) * 512:(6 * d + n + 1) * 512]

        def mask(c):
            return CST[:, c, :].unsqueeze(1).to_broadcast([P, HEADS, P])

        YO = [Z[:, 9216:9728], Z[:, 9728:10240]]
        BC2 = Z[:, 5120:9216].rearrange("p (r c) -> p r c", r=4)
        betaexp = small(40)
        mod_dram = nc.dram_tensor("mod_rows", [DEPTH, 2, 6 * D], f32).ap()
        ht = [0]
        HTF = HT[:, :, :].rearrange("p k t -> p (k t)")

        def routing(n):
            a = ht[0]
            ht[0] += n
            return HTF[:, a:a + n]

        LG = routing(TILES * 20).rearrange("p (t c) -> p t c", t=TILES)
        gmax, cmin, gsum, gw, vmax, vsec = (routing(TILES) for _ in range(6))
        cand, ghot, LE, hot1, hot2, LE2 = (routing(TILES * 4).rearrange("p (t c) -> p t c", t=TILES) for _ in range(6))
        gx = routing(TILES * 5)
        WSEL = routing(2 * TILES).rearrange("p (c t) -> p c t", c=2)
        HE = routing(2 * TILES * 16).rearrange("p (c t e) -> p c t e", c=2, t=TILES)
        HALL = routing(TILES * 16)
        RK = routing(TILES * 16)
        rtmp = routing(TILES * 16)
        CNT = routing(16)
        OV, OVC, EBASE, OBASE = (routing(16) for _ in range(4))
        past = routing(TILES * 16)
        iota_row = routing(P)
        tile_at_slot = routing(2 * TILES)
        low = routing(2 * TILES)
        HOTT = routing(2 * TILES * ETILES).rearrange("p (n i) -> p n i", n=2 * TILES)
        HOTL = routing(2 * TILES * P).rearrange("p (n i) -> p n i", n=2 * TILES)
        zero16 = small(16)
        big = routing(2 * TILES * ETILES)
        slotf = routing(2 * TILES)
        eotf = routing(ETILES)
        i32 = mybir.dt.int32
        IDX = routing(2 * TILES).bitcast(i32).rearrange("p (c t) -> p c t", c=2)
        EOT = routing(ETILES).bitcast(i32)
        TOKI = routing(ETILES).bitcast(i32)
        ngf = routing(1)
        NG = routing(1).bitcast(i32)
        TOKSEL = routing(3).bitcast(i32)
        assert ht[0] <= 5120
        IOTA = small(66)
        tokgate = small(2)
        RW = raw.rearrange("p (k c) -> p k c", k=KT)
        RB = small(20)
        h2_dram = nc.dram_tensor("h2_rows", [T, D], f32).ap()
        yg_dram = nc.dram_tensor("expert_rows", [SLOTS_E, D], f32).ap()
        SINK = small(HC)

        QR = Z[:, 10240:15360].rearrange("p (t c) -> p t c", t=TILES)
        QTT = Z[:, 0:5120].rearrange("p (g t) -> p g t", g=HC // 2)
        V = Z[:, 5120:6656].rearrange("p (t c) -> p t c", t=TILES + 1)
        KTT = [Z[:, 6656:9728].rearrange("p (g t) -> p g t", g=KVH), SLOTS[:, KSLOT, 0:3072].rearrange("p (g t) -> p g t", g=KVH)]
        ROPE = Z[:, 9728:10240].rearrange("p (a t i) -> p a t i", a=2, t=TILES - 1)
        KEYS = 64 + 2 * HD * KVH * (TILES + 1)
        KD = BCF[:, HD:KEYS].rearrange("p (t g r i) -> p t g r i", t=TILES + 1, g=KVH, r=2)[:, :, :, 0, :]
        KZERO = BCF[:, 0:KEYS + HD].rearrange("p (n r i) -> p n r i", r=2, i=HD)[:, :, 0, :]
        RTMP = BC[:, 3, 512:1024]
        PB = HTF[:, 0:1536].rearrange("p (b c) -> p b c", b=3)
        PTB = HTF[:, 1536:3072].rearrange("p (b c) -> p b c", b=3)
        STEPS = TILES * HC
        NM = HTF[:, 3072:3072 + STEPS]
        RS = HTF[:, 3200:3200 + STEPS]
        ES = HTF[:, 3328:3328 + STEPS]

        MASKS = HTF[:, 3456:3648].bitcast(mybir.dt.bfloat16).rearrange("p (n c) -> p n c", n=3)

        def key_tiles(t):
            if t == 0:
                return [0], [0]
            local = list(range(max(1, t - 1), min(TILES - 1, t + 1) + 1))
            return local, local + [TILES]

        const_loaded = sem("const_loaded")
        x_loaded = sem("x_loaded")
        small_loaded = sem("small_loaded")
        state_loaded = sem("state_loaded")
        slot_arrived = [sem(f"slot{n}_arrived") for n in range(NSLOT)]
        unit_done = sem("unit_done")
        unit_out = sem("unit_out")
        mod_stored = [sem(f"mod_stored{n}") for n in range(2)]
        dve_order = sem("dve_order")
        pool_order = sem("pool_order")
        act_order = sem("act_order")
        gate_abs = sem("gate_abs")
        gate_ln = sem("gate_ln")
        gate_lf = sem("gate_lf")
        m_scanned = sem("m_scanned")
        mex_ready = sem("mex_ready")
        arg_ready = sem("arg_ready")
        exp_ready = sem("exp_ready")
        pool_const = sem("pool_const")

        def pair(name):
            return [sem(f"{name}{d}") for d in range(2)]

        ml_st, ml_db, ml_de, ml_sw, ml_vw, ml_u, ml_done = (
            pair("ml_" + n) for n in ("scores", "decay", "exp", "weights", "vw", "update", "done"))
        dl_kk, dl_db, dl_de, dl_at, dl_cm, dl_xt1, dl_x1t, dl_x1, dl_p1, dl_p1s, dl_p2, dl_x, dl_ks, dl_r, dl_tr, \
            dl_vn, dl_o, dl_vw, dl_su, dl_done = (
                pair("dl_" + n) for n in ("kk", "decay", "exp", "at", "cm", "xt1", "x1t", "x1", "p1", "p1s", "p2",
                                          "x", "ks", "r", "tr", "vn", "o", "vw", "su", "done"))
        conv_done = sem("conv_done")
        sq_ready = sem("sq_ready")
        silu_done = sem("silu_done")
        norm_taken = sem("norm_taken")
        normed = sem("normed")
        gate_used = sem("gate_used")
        var_ready = sem("var_ready")
        rstd_ready = sem("rstd_ready")
        y_ready = sem("y_ready")
        gain_loaded = sem("gain_loaded")
        alog_exp = sem("alog_exp")
        dl_qd, dl_xt = pair("dl_qd"), pair("dl_xt")
        bc_loaded = sem("bc_loaded")
        bc2_loaded = sem("bc2_loaded")
        out_used = sem("out_used")
        ln_done = sem("ln_done")
        h2_ready = sem("h2_ready")
        h2_stored = sem("h2_stored")
        router_loaded = sem("router_loaded")
        rows_cleared = sem("rows_cleared")
        route_arg = sem("route_arg")
        route_exp = sem("route_exp")
        hot_ready = sem("hot_ready")
        routed = sem("routed")
        tok_picked = sem("tok_picked")
        slots_ready = sem("slots_ready")
        slots_cast = sem("slots_cast")
        ht_done = sem("ht_done")
        ht_out = sem("ht_out")
        rows_gathered = [[sem(f"rows_gathered{l}_{n}") for n in range(3)] for l in range(DEPTH)]
        xt_done = sem("xt_done")
        xt_out = sem("xt_out")
        gu_done = sem("gu_done")
        silu_out = sem("silu_out")
        hid_ready = sem("hid_ready")
        down_done = sem("down_done")
        ye_ready = sem("ye_ready")
        ye_stored = [sem(f"ye_stored{n}") for n in range(3)]
        yg_gathered = [sem(f"yg_gathered{n}") for n in range(2)]
        yg_used = sem("yg_used")
        states_stored = sem("states_stored")
        attn_loaded = sem("attn_loaded")
        caches_stored = sem("caches_stored")
        keys_ready = sem("keys_ready")
        queries_ready = sem("queries_ready")
        masks_ready = sem("masks_ready")
        s_done = sem("s_done")
        max_ready = sem("max_ready")
        p_ready = sem("p_ready")
        pt_done = sem("pt_done")
        pt_out = sem("pt_out")
        pv_done = sem("pv_done")
        sink_arg = sem("sink_arg")
        sink_exp = sem("sink_exp")
        o_ready = sem("o_ready")
        x_stored = sem("x_stored")

        loads = weight_loads()
        load_no = {}
        n = 0
        for item in loads:
            load_no[item] = n
            n += ETILES if item[0] == "moe" else 1
        item_of = {load_no[item]: item for item in loads}
        first_moe, last_moe = load_no[("moe", 0)], load_no[("moe", 1)]

        def slot_of(n):
            if n < first_moe:
                return n % 2
            return (n - first_moe) % NSLOT if n < last_moe else (n - last_moe) % NSLOT

        def last_in_slot(n):
            return max(m for m in range(n) if slot_of(m) == slot_of(n))

        def dmas_of(item):
            return {"mod": 2, "moe": 3}.get(item[0], 1) if item != ("in", "gates") else 2

        arrived_at, count = {}, [0] * NSLOT
        for item in loads:
            for j in range(ETILES if item[0] == "moe" else 1):
                s = slot_of(load_no[item] + j)
                count[s] += 16 * dmas_of(item)
                arrived_at[load_no[item] + j] = count[s]

        units = unit_order()
        unit_no = {name: n for n, name in enumerate(units)}
        assert len(unit_no) == len(units)

        def last_unit(item):
            if item[0] == "mod":
                return item
            if item[0] == "wout":
                return ("out", item[1], item[2], TILES - 1)
            if item[0] == "qkv":
                return item + (TILES - 1,)
            if item[1] in ("qa", "ka", "vd", "kd", "qd"):
                return ("fm", item[1], 3, 1)
            return ("tm", item[1], TILES - 1)

        assert slot_of(load_no["qkv", 1]) == KSLOT
        mod_parts = modulation_parts()
        rows_stored, stored = {}, [0, 0]
        for name, part in mod_parts.items():
            for _, c in part:
                stored[c % 2] += c >= 4
            for n in range(2):
                rows_stored[n, name] = stored[n]

        def slot_cols(n, k, cols):
            return SLOTS[:, slot_of(n), 0:k * cols].rearrange("p (k c) -> p k c", k=k)

        w_in = ins["w_in_even"][0].rearrange("(k p) n -> p k n", p=P)
        in_at = {"qa": 0, "ka": 512, "va": 1024, "oa": 1536, "qd": 2064, "kd": 2576, "vd": 3088, "zb": 3600}

        block = ctx.enter_context(nc.Block())

        @block.sync
        def _(sp):
            def load(item):
                n = load_no[item]
                if n >= 2:
                    m = last_in_slot(n)
                    if first_moe <= m < first_moe + ETILES:
                        sp.wait_ge(down_done, m - first_moe + 1)
                    else:
                        sp.wait_ge(unit_done, unit_no[last_unit(item_of[m])] + 1)
                s = slot_of(n)
                a = slot_arrived[s]
                kind = item[0]
                if kind == "mod":
                    _, l, c = item
                    w = ins["w_mod"][l].rearrange("(k p) n -> p k n", p=P)
                    sp.dma_start(slot_cols(n, KT, 512), w[:, :, c * 512:(c + 1) * 512]).then_inc(a, 16)
                    sp.dma_start(SLOTS[0:1, s, 4096:4608], ins["b_mod"][l:l + 1, c * 512:(c + 1) * 512]).then_inc(a, 16)
                elif item == ("in", "gates"):
                    dst = slot_cols(n, KT, 32)
                    sp.dma_start(dst[:, :, 0:16], w_in[:, :, 2048:2064]).then_inc(a, 16)
                    sp.dma_start(dst[:, :, 16:32], w_in[:, :, 4112:4128]).then_inc(a, 16)
                elif kind == "in":
                    c = in_at[item[1]]
                    sp.dma_start(slot_cols(n, KT, 512), w_in[:, :, c:c + 512]).then_inc(a, 16)
                elif kind == "qkv":
                    w = ins["w_qkv_odd"][0].rearrange("(k p) n -> p k n", p=P)
                    sp.dma_start(slot_cols(n, KT, 512), w[:, :, item[1] * 512:(item[1] + 1) * 512]).then_inc(a, 16)
                elif kind == "wout":
                    _, l, c = item
                    w = (ins["w_out_even"], ins["w_out_odd"])[l][0].rearrange("(k p) n -> p k n", p=P)
                    sp.dma_start(slot_cols(n, KT, 512), w[:, :, c * 512:(c + 1) * 512]).then_inc(a, 16)

            def load_router(l):
                sp.dma_start(RW[:, :, 0:4], ins["w_grp"][l].rearrange("(k p) c -> p k c", p=P)).then_inc(router_loaded, 16)
                for g in range(GRP):
                    sp.dma_start(RW[:, :, 4 + 4 * g:8 + 4 * g], ins["w_erouter"][l, g].rearrange("(k p) c -> p k c", p=P))\
                        .then_inc(router_loaded, 16)
                sp.dma_start(RB[:, 0:4], ins["b_grp"][l].partition_broadcast(P)).then_inc(router_loaded, 16)
                sp.dma_start(RB[:, 4:20], ins["b_erouter"][l].rearrange("g e -> (g e)").partition_broadcast(P))\
                    .then_inc(router_loaded, 16)

            for item in loads[:first_moe]:
                if item == ("in", "qd"):
                    sp.wait_ge(arg_ready, 1)
                    load_router(0)
                load(item)

            def sync_moe(l):
                n0 = load_no[("moe", l)]
                if l == 0:
                    sp.wait_ge(gate_used, 2 * TILES)
                for n in range(2):
                    sp.wait_ge(mod_stored[n], 16 * rows_stored[n, ("norm", "moe")[l]])
                weights = [ins[n][l] for n in ("w_gate", "w_up", "w_down")]

                def load_expert(u, e):
                    for m, w in enumerate(weights):
                        k = KT if m < 2 else 2
                        dst = SLOTS[:, u, 2048 * m:2048 * m + 2048].rearrange("p (k c) -> p k c", k=k)
                        sp.dma_start(dst, w[e].rearrange("o (k p) c -> p (o k) c", p=P))\
                            .then_inc(slot_arrived[u], 16)

                def store_rows(j, u):
                    i = 3 * j + u
                    sp.wait_ge(ye_ready, i + (ETILES * l + 1))
                    sp.dma_start(yg_dram[bass.ds(P * i, P), :], YE[:, u, :]).then_inc(ye_stored[u], 16)

                for u in range(3):
                    if l or u < 2:
                        sp.wait_ge(unit_done, unit_no[last_unit(item_of[last_in_slot(n0 + u)])] + 1)
                    if l and u == KSLOT:
                        sp.wait_ge(s_done, STEPS)
                    load_expert(u, slice(u, u + 1))
                sp.wait_ge(routed, l + 1)
                groups = sp.value_load(NG[0:1, 0:1], min_val=1, max_val=GROUPS)

                def load_next(j):
                    for u in range(3):
                        sp.wait_ge(down_done, 3 * j + (ETILES * l + u + 1))
                        e = sp.value_load(EOT[0:1, bass.ds(3 * j + (3 + u), 1)], min_val=0, max_val=NEXP - 1)
                        load_expert(u, bass.ds(e, 1))

                def store_group(j):
                    for u in range(3):
                        store_rows(j, u)

                def pass_over_stores(j):
                    for u in range(3):
                        sp.wait_ge(ye_stored[u], 16 * j + 16 * GROUPS * l)
                        sp.sem_inc(ye_stored[u], 16)

                with sp.Fori(0, SURE - 1) as j:
                    load_next(j)
                    store_group(j)
                with sp.Fori(SURE - 1, GROUPS - 1) as j:
                    with sp.If(j + 1 < groups):
                        load_next(j)
                    with sp.Else():
                        for u in range(3):
                            sp.wait_ge(slot_arrived[u], 48 * j + arrived_at[n0 + u])
                            sp.sem_inc(slot_arrived[u], 48)
                    with sp.If(j < groups):
                        store_group(j)
                    with sp.Else():
                        pass_over_stores(j)
                with sp.If(groups > GROUPS - 1):
                    store_group(GROUPS - 1)
                with sp.Else():
                    pass_over_stores(GROUPS - 1)

            sync_moe(0)
            load_router(1)
            for item in loads[loads.index(("moe", 0)) + 1:-1]:
                load(item)
            sync_moe(1)
            for t in range(TILES):
                sp.wait_ge(ln_done, 3 * TILES + t + 1)
                dst = outs[0][0] if t == 0 else outs[1][0, (t - 1) * P:t * P, :]
                sp.dma_start(dst, X[:, t, :]).then_inc(x_stored, 16)
            sp.wait_ge(x_stored, 16 * TILES)

        @block.gpsimd
        def _(pool):
            order = [0]

            def done(ins_, s=None):
                if s is None:
                    order[0] += 1
                    ins_.then_inc(pool_order, 1)
                    pool.wait_ge(pool_order, order[0])

            sl = small_loaded
            pool.dma_start(gbias[:, :, 0:8], ins["mlstm_gate_b"][0].rearrange("d t h -> (d t h)").partition_broadcast(P)
                           .rearrange("p (d c) -> p d c", d=2)).then_inc(sl, 16)
            pool.dma_start(gbias[:, :, 12:16], ins["delta_dt_bias"][0].rearrange("d h -> (d h)").partition_broadcast(P)
                           .rearrange("p (d c) -> p d c", d=2)).then_inc(sl, 16)
            pool.dma_start(alog, ins["delta_a_log"][0].rearrange("d h -> (d h)").partition_broadcast(P)).then_inc(sl, 16)
            pool.dma_start(M0[0:4, :], ins["state_mlstm_m"][0, 0].rearrange("d h -> h d"),
                           allow_slow_non_contiguous=True).then_inc(sl, 16)
            pool.memset(gbias[:, :, 8:12], 0.0).then_inc(pool_const, 1)
            pool.memset(half, -0.5).then_inc(pool_const, 1)
            pool.memset(eps[:, 0:1], P * 1e-6).then_inc(pool_const, 1)
            pool.memset(eps[:, 1:2], 1e-6).then_inc(pool_const, 1)
            pool.memset(lcoef, -1.0).then_inc(pool_const, 1)
            pool.memset(SM[:, 0], 0.0).then_inc(pool_const, 1)
            pool.memset(SD[:, 0], 0.0).then_inc(pool_const, 1)
            pool.memset(NS[:, 0], 0.0).then_inc(pool_const, 1)
            pool.memset(zero16, 0.0).then_inc(pool_const, 1)
            pool.dma_start(SM[:, 1], ins["state_mlstm_c"][0, 0].rearrange("d h k v -> k (d h) v")).then_inc(state_loaded, 16)
            pool.dma_start(SD[:, 1], ins["state_delta"][0, 0].rearrange("d h k v -> k (d h) v")).then_inc(state_loaded, 16)
            pool.dma_start(NS[:, 1], ins["state_mlstm_n"][0, 0].rearrange("d h k -> k (d h)"),
                           allow_slow_non_contiguous=True).then_inc(state_loaded, 16)

            pool.dma_start(GAIN[:, 0, :], ins["mlstm_norm_g"][0].partition_broadcast(P)).then_inc(gain_loaded, 16)
            pool.dma_start(GAIN[:, 1, :], ins["delta_norm_g"][0].partition_broadcast(P)).then_inc(gain_loaded, 16)
            for s in range(TILES):
                for d in range(2):
                    if s == 0 and d == 0:
                        pool.wait_ge(exp_ready, 1)
                        pool.wait_ge(unit_out, unit_no[("tm", "va", TILES - 1)] + 1)
                        pool.wait_ge(pool_const, 9)
                        spare = ETILES - 3 * SURE
                        pool.dma_start(yg_dram[3 * SURE * P:SLOTS_E, :].rearrange("(i p) c -> p i c", p=P),
                                       SD[:, 0].rearrange("p u v -> p (u v)").unsqueeze(1).to_broadcast([P, spare, D]))\
                            .then_inc(rows_cleared, 16)
                    if s:
                        pool.wait_ge(ml_u[d], s)
                    w = v4(EX[:, WE, :])[:, d, s, :]
                    pool.tensor_tensor(heads(mlb(d, 2)), heads(VTOK[:, tile_at(d, s), :]), col(w, P), ALU.mult)\
                        .then_inc(ml_vw[d], 1)
            pool.wait_ge(var_ready, 1)
            pool.tensor_tensor(rstd, st20, half, ALU.pow).then_inc(rstd_ready, 1)
            pool.wait_ge(rows_cleared, 16)
            for n in range(2):
                pool.wait_ge(mod_stored[n], 16 * rows_stored[n, "qd2"])
            for s in range(TILES):
                for d in range(2):
                    at_ = dlb(d, 2)
                    pool.wait_ge(dl_at[d], s + 1)
                    done(pool.tensor_tensor(heads(at_), heads(at_), col(v4(BETA)[:, d, s, :], P), ALU.mult))
                    lev = C_LEV[d]
                    done(pool.tensor_tensor(heads(dlb(d, 5)), heads(at_), mask(lev), ALU.mult))
                    pool.tensor_tensor(heads(dlb(d, 4)), mask(C_ID), heads(dlb(d, 5)), ALU.subtract).then_inc(dl_xt1[d], 1)
                    pool.tensor_tensor(heads(dlb(d, 6)), heads(at_), mask(lev + 1), ALU.mult).then_inc(dl_cm[d], 1)
                for n in range(2, 7):
                    for d in range(2):
                        if n >= 3:
                            pool.wait_ge(dl_p1[d], 6 * s + n - 2)
                        else:
                            pool.wait_ge(dl_xt1[d], s + 1)
                        pool.tensor_tensor(heads(dlb(d, 5 + n % 2)), heads(dlb(d, 2)), mask(C_LEV[d] + n), ALU.mult)\
                            .then_inc(dl_cm[d], 1)
                for d in range(2):
                    pool.wait_ge(dl_vn[d], s + 1)
                    pool.tensor_tensor(heads(dlb(d, 2)), heads(dlb(d, 3)), col(v4(EX[:, EE, :])[:, d, s, :], P), ALU.mult)\
                        .then_inc(dl_vw[d], 1)
            pool.wait_ge(var_ready, 2)
            pool.tensor_tensor(rstd, st20, half, ALU.pow).then_inc(rstd_ready, 1)

            bc = [0]

            def load_bc(rows, dst=BC, loaded=bc_loaded):
                for j, r in enumerate(rows):
                    pool.dma_start(dst[:, j, :], r.partition_broadcast(P)).then_inc(loaded, 16)

            def roots(nth, tiles=range(TILES)):
                for t in tiles:
                    pool.wait_ge(var_ready, 3 + TILES * nth + t)
                    pool.tensor_tensor(lnr[:, t:t + 1], lnr[:, t:t + 1], half[:, 0:1], ALU.pow).then_inc(rstd_ready, 1)

            def mod_row(l, v, m):
                return mod_dram[l, v, m * D:(m + 1) * D]

            for d in range(2):
                pool.wait_ge(dl_done[d], TILES)
            pool.dma_start(outs[2][0, 0].rearrange("d h k v -> k (d h) v"), SM[:, 0]).then_inc(states_stored, 16)
            pool.dma_start(outs[5][0, 0].rearrange("d h k v -> k (d h) v"), SD[:, 0]).then_inc(states_stored, 16)
            pool.dma_start(outs[3][0, 0].rearrange("d h k -> k (d h)"), NS[:, 0],
                           allow_slow_non_contiguous=True).then_inc(states_stored, 16)
            pool.dma_start(outs[4][0, 0].rearrange("d h -> h d"), MV[0:4, 1:14:7],
                           allow_slow_non_contiguous=True).then_inc(states_stored, 16)
            pool.wait_ge(states_stored, 64)
            for n in range(2):
                pool.wait_ge(mod_stored[n], 16 * rows_stored[n, "qd2"])
            load_bc([mod_row(0, 0, 2), mod_row(0, 1, 2), ins["ln_g"][0, 0], ins["ln_b"][0, 0]])
            load_bc([mod_row(0, 0, 3), mod_row(0, 1, 3), mod_row(0, 0, 4), mod_row(0, 1, 4)], BC2, bc2_loaded)
            roots(0)

            def pool_moe(l):
                for t in range(TILES):
                    pool.wait_ge(h2_ready, TILES * l + t + 1)
                    pool.dma_start(h2_dram[t * P:(t + 1) * P, :], H2[:, t, :]).then_inc(h2_stored, 16)
                pool.wait_ge(ln_done, TILES * (2 * l + 1))
                load_bc([mod_row(l, 0, 5), mod_row(l, 1, 5), ins["ln_g"][l, 1], ins["ln_b"][l, 1]])
                pool.wait_ge(unit_out, unit_no[("tok", l)] + 1)
                pool.wait_ge(h2_stored, 16 * TILES * (l + 1))

                def gate(n):
                    pool.tensor_tensor(tokgate[:, n:n + 1], half[:, 0:1], half[:, 0:1], ALU.mult)

                def gather(j, u, first):
                    i = 3 * j + u
                    if not first:
                        pool.wait_ge(xt_done, i + (ETILES * l - 2))
                        gate(0)
                    pool.tensor_copy(TOKSEL[:, u:u + 1], TOKI[:, bass.ds(i, 1)]).then_inc(tok_picked, 1)
                    pool.wait_ge(tok_picked, i + (ETILES * l + 1))
                    gate(1)
                    pool.indirect_dma_start(XG[:, u, :], None, h2_dram,
                                            bass.IndirectOffsetOnAxis(ap=TOKSEL[:, u:u + 1], axis=0))\
                        .then_inc(rows_gathered[l][u], 16)

                for u in range(3):
                    gather(0, u, True)
                pool.wait_ge(routed, l + 1)
                groups = pool.value_load(NG[0:1, 0:1], min_val=1, max_val=GROUPS)
                with pool.Fori(1, SURE) as j:
                    for u in range(3):
                        gather(j, u, False)
                with pool.Fori(SURE, GROUPS) as j:
                    with pool.If(j < groups):
                        for u in range(3):
                            gather(j, u, False)
                    with pool.Else():
                        pool.wait_ge(tok_picked, 3 * j + ETILES * l)
                        pool.sem_inc(tok_picked, 3)
                pool.wait_ge(slots_cast, l + 1)
                for u in range(3):
                    pool.wait_ge(ye_stored[u], 16 * GROUPS * (l + 1))
                for t in range(TILES):
                    if t >= 2:
                        pool.wait_ge(yg_used, TILES * l + t - 1)
                    for c in range(2):
                        pool.indirect_dma_start(YG[:, t % 2, c, :], None, yg_dram,
                                                bass.IndirectOffsetOnAxis(ap=IDX[:, c, t:t + 1], axis=0))\
                            .then_inc(yg_gathered[t % 2], 16)
                    if t:
                        roots(2 * l + 1, [t - 1])
                roots(2 * l + 1, [TILES - 1])

            pool_moe(0)

            pool.dma_start(ROPE, ins["ropes"]).then_inc(attn_loaded, 16)
            pool.dma_start(V[:, TILES, :].rearrange("p (g i) -> p g i", g=KVH), ins["cache_v"][0, 0].rearrange("g s i -> s g i"))\
                .then_inc(attn_loaded, 16)
            pool.dma_start(SINK, ins["attn_sink"][0].partition_broadcast(P)).then_inc(attn_loaded, 16)
            pool.wait_ge(ln_done, 2 * TILES)
            pool.dma_start(KD[:, TILES, :, :], ins["cache_k"][0, 0].rearrange("g s i -> s g i")).then_inc(attn_loaded, 16)
            pool.wait_ge(unit_out, unit_no[("qkv", 2, 0)] + 1)
            pool.dma_start(outs[6][0, 0].rearrange("g s i -> s g i"), KD[:, 0, :, :]).then_inc(caches_stored, 16)
            pool.dma_start(outs[7][0, 0].rearrange("g s i -> s g i"), V[:, 0, :].rearrange("p (g i) -> p g i", g=KVH))\
                .then_inc(caches_stored, 16)
            pool.wait_ge(caches_stored, 32)
            pool.wait_ge(unit_out, unit_no[("kT", TILES, 1)] + 1)
            pool.wait_ge(queries_ready, 2 * TILES)
            for n in range(2):
                pool.wait_ge(mod_stored[n], 8 * 16)
            load_bc([mod_row(1, 0, 2), mod_row(1, 1, 2), ins["ln_g"][1, 0], ins["ln_b"][1, 0]])
            pool.wait_ge(pv_done, STEPS)
            load_bc([mod_row(1, 0, 3), mod_row(1, 1, 3), mod_row(1, 0, 4), mod_row(1, 1, 4)], BC2, bc2_loaded)
            roots(2)
            pool_moe(1)

        @block.scalar
        def _(act):
            act.dma_start(CST[:, :, :], ins["consts"]).then_inc(const_loaded, 16)
            act.dma_start(cin[0:8, :], ins["c_ctx"].rearrange("(k p) -> k p", p=P)).then_inc(const_loaded, 16)
            act.dma_start(cin[8:16, :], ins["c"][0].rearrange("(k p) -> k p", p=P)).then_inc(const_loaded, 16)
            act.dma_start(convrow, ins["delta_conv_w"][0].rearrange("j (m p) -> (j m) p", p=P)).then_inc(const_loaded, 16)
            act.dma_start(IOTA, ins["iotas"]).then_inc(const_loaded, 16)
            act.dma_start(X[:, 0, :], ins["x_prompt"][0]).then_inc(x_loaded, 16)
            act.dma_start(X[:, 1:TILES, :], ins["x_sample"][0].rearrange("(t p) n -> p t n", p=P)).then_inc(x_loaded, 16)

            def take(name):
                n = unit_no[name]
                act.wait_ge(unit_done, n + 1)
                return PS[:, n % BANKS, :]

            b = take(("cT",))
            act.activation(csil.rearrange("p (k v r) -> p k v r", k=KT, v=2),
                           b[:, 0:16].rearrange("p (v k) -> p k v", v=2).unsqueeze(3).to_broadcast([P, KT, 2, 16]),
                           ACT.Silu).then_inc(unit_out, 1)
            b = take(("convT",))
            act.activation(convw, b[:, 0:36], ACT.Copy).then_inc(unit_out, 1)

            def mod_rows(name):
                part = mod_parts[name]

                def partial(l, c):
                    b = take(("mod", l, c))
                    if l or c >= 6:
                        act.wait_ge(mod_stored[c % 2], 16 * (4 * l + max(0, (c - 4) // 2)))
                    act.activation(MSUM[:, c % 2, :], b, ACT.Copy).then_inc(unit_out, 1)

                for j, (l, c) in enumerate(part):
                    for lc in part[0:2] if j == 0 else part[j + 1:j + 2]:
                        partial(*lc)
                    b = take(("modS", l, c))
                    act.activation(MROW[:, c % 2, :], b[0:2, :], ACT.Copy).then_inc(unit_out, 1)
                    if c < 4:
                        b = take(("modT", l, c))
                        dst = MODT[l][:, 4 * (c % 2):4 * (c % 2) + 4, 2 * (c // 2):2 * (c // 2) + 2]
                        act.activation(dst, b[:, 0:8].rearrange("p (q v) -> p q v", q=4), ACT.Copy,
                                       bias=float(c // 2)).then_inc(unit_out, 1)
                    else:
                        act.wait_ge(unit_out, unit_no[("modS", l, c)] + 1)
                        act.dma_start(mod_dram[l, :, c * 512:(c + 1) * 512], MROW[:, c % 2, :]).then_inc(mod_stored[c % 2], 16)

            def modulate(l):
                act.wait_ge(unit_out, unit_no[("modT", l, 3)] + 1)
                for k in range(KT):
                    b = take(("hTlat", l, k))
                    act.activation(HT[:, k, P:T], b, ACT.Identity, bias=MODT[l][:, k, 1:2], scale=MODT[l][:, k, 3:4])\
                        .then_inc(unit_out, 1)
                for g in range(2):
                    b = take(("hTctx", l, g))
                    for q in range(4):
                        k = 4 * g + q
                        i = act.activation(HT[:, k, 0:P], b[:, q * P:(q + 1) * P], ACT.Identity,
                                           bias=MODT[l][:, k, 0:1], scale=MODT[l][:, k, 2:3])
                    i.then_inc(unit_out, 1)

            def feature_major(name, dst, scale=1.0):
                for m in range(4):
                    for h in range(2):
                        b = take(("fm", name, m, h))
                        act.activation(dst[:, m, 320 * h:320 * h + 320], b[:, 0:320], ACT.Copy, scale=scale)\
                            .then_inc(unit_out, 1)

            mod_rows("first")
            modulate(0)
            for t in range(TILES):
                b = take(("tm", "gates", t))
                act.activation(graw[:, t, :], b[:, 0:32], ACT.Copy).then_inc(unit_out, 1)
            act.wait_ge(gate_abs, 1)
            act.activation(zexp, zabs, ACT.Exp, scale=-1.0).then_inc(act_order, 1)
            act.wait_ge(act_order, 1)
            act.activation(zln, zexp, ACT.Ln, bias=1.0).then_inc(gate_ln, 1)
            act.activation(v4(betaexp), raw4[:, :, :, 8:12], ACT.Exp, scale=-1.0)
            act.activation(alog, alog, ACT.Exp).then_inc(alog_exp, 1)
            feature_major("qa", QT)
            mod_rows("qa")
            for d in range(2):
                b = take(("cs", d))
                act.activation(CS[:, 40 * d:40 * d + 40], b[:, 0:40], ACT.Copy).then_inc(unit_out, 1)
            b = take(("ce",))
            act.activation(CE, b[:, 0:80], ACT.Copy).then_inc(unit_out, 1)
            for name, dst in (("rowf", ROWF), ("rowi", ROWI)):
                for d in range(2):
                    for part, (a, e) in enumerate(((0, 512), (512, T))):
                        b = take((name, d, part))
                        act.activation(dst[:, d, a:e], b[0:4, 0:e - a], ACT.Copy).then_inc(unit_out, 1)
            feature_major("ka", KTR, P ** -0.5)
            mod_rows("ka")
            b = take(("mcol", 0))
            act.activation(MC[:, 0:20], b[:, 0:20], ACT.Copy).then_inc(unit_out, 1)
            b = take(("mcol", 1))
            act.activation(rev, b[:, 0:20], ACT.Copy).then_inc(unit_out, 1)
            b = take(("mflip",))
            act.activation(MC[:, 20:40], b[:, 0:20], ACT.Copy).then_inc(unit_out, 1)
            b = take(("mvb",))
            act.activation(MVB, b[:, 0:56], ACT.Copy).then_inc(unit_out, 1)
            act.wait_ge(arg_ready, 1)
            act.activation(EX[:, :, :], ARG[:, :, :], ACT.Exp).then_inc(exp_ready, 1)
            for t in range(TILES):
                b = take(("tm", "va", t))
                act.activation(VTOK[:, t, :], b, ACT.Copy).then_inc(unit_out, 1)
            mod_rows("va")
            for t in range(TILES):
                b = take(("ktok", "a", t))
                act.activation(KTOK[:, t, :], b, ACT.Copy).then_inc(unit_out, 1)

            for s in range(TILES):
                for d in range(2):
                    act.wait_ge(ml_db[d], s + 1)
                    if s:
                        act.wait_ge(ml_sw[d], s)
                    for h in range(HEADS):
                        i = act.activation(mlb(d, 0)[:, h * P:(h + 1) * P], PS[:, 4 * d + 1, h * P:(h + 1) * P], ACT.Exp,
                                           bias=v4(CB[:, 0, :])[:, d, s, h:h + 1])
                    i.then_inc(ml_de[d], 1)

            def gate(name, func, used0):
                for t in range(TILES):
                    b = take(("tm", name, t))
                    if t >= 2 or used0:
                        act.wait_ge(gate_used, used0 + t - 1)
                    act.activation(SG[t % 2], b, func).then_inc(unit_out, 1)

            gate("oa", ACT.Sigmoid, 0)

            def silu_conv(dst, first):
                for m in range(4):
                    act.wait_ge(conv_done, first + m + 1)
                    act.activation(dst[:, m, :], dst[:, m, :], ACT.Silu).then_inc(silu_done, 1)

            def norms(name, dst, first, scale):
                for m in range(4):
                    act.wait_ge(silu_done, first + m + 1)
                    if name == "qd":
                        act.wait_ge(unit_out, unit_no[("ssq", "kd", 3, 1)] + 1)
                        act.wait_ge(normed, 4)
                    act.activation(SQ[:, m, :], dst[:, m, :], ACT.Square).then_inc(sq_ready, 1)
                for m in range(4):
                    for h in range(2):
                        b = take(("ssq", name, m, h))
                        act.activation(NRM[:, m, 320 * h:320 * h + 320], b[:, 0:320], ACT.Sqrt, scale=scale,
                                       bias=eps[:, 0:1] if name == "qd" else eps[:, 1:2]).then_inc(unit_out, 1)

            feature_major("vd", PRE)
            mod_rows("vd")
            silu_conv(QT, 0)
            for t in range(TILES):
                b = take(("vtok", t))
                act.activation(VTOK[:, t, :], b, ACT.Copy).then_inc(unit_out, 1)
            act.wait_ge(conv_done, 4)
            feature_major("kd", PRE)
            mod_rows("kd")
            silu_conv(KTR, 4)
            norms("kd", KTR, 4, 1.0)
            mod_rows("kd2")
            for t in range(TILES):
                b = take(("ktok", "d", t))
                act.activation(KTOK[:, t, :], b, ACT.Copy).then_inc(unit_out, 1)
            act.wait_ge(conv_done, 8)
            feature_major("qd", PRE)
            mod_rows("qd")
            silu_conv(QT, 8)
            norms("qd", QT, 8, float(P))
            mod_rows("qd2")

            for s in range(TILES):
                for d in range(2):
                    act.wait_ge(dl_db[d], s + 1)
                    if s:
                        act.wait_ge(dl_done[d], s)
                    for h in range(HEADS):
                        i = act.activation(dlb(d, 0)[:, h * P:(h + 1) * P], PS[:, 4 * d + 1, h * P:(h + 1) * P], ACT.Exp,
                                           bias=v4(CB[:, 1, :])[:, d, s, h:h + 1])
                    i.then_inc(dl_de[d], 1)
                for d in range(2):
                    act.wait_ge(dl_x1t[d], s + 1)
                    act.activation(dlb(d, 3), PS[:, 4 * d, :], ACT.Copy).then_inc(dl_x1[d], 1)
                for n in range(1, 7):
                    for d in range(2):
                        act.wait_ge(dl_p1[d], 6 * s + n)
                        act.activation(dlb(d, 0), PS[:, 4 * d, :], ACT.Copy).then_inc(dl_p1s[d], 1)
            act.wait_ge(gate_used, TILES)
            gate("zb", ACT.Silu, TILES)
            for k in range(KT):
                for part, (a, e) in enumerate(((0, 512), (512, T))):
                    b = take(("yT", 0, k, part))
                    act.activation(HT[:, k, a:e], b[:, 0:e - a], ACT.Copy).then_inc(unit_out, 1)

            def out_rows(l):
                for n in range(2):
                    for t in range(TILES):
                        b = take(("out", l, n, t))
                        j = TILES * n + t
                        if j >= 2 or l:
                            act.wait_ge(out_used, 2 * TILES * l + j - 1)
                        act.activation(YO[j % 2], b, ACT.Copy).then_inc(unit_out, 1)

            out_rows(0)

            def act_moe(l):
                if l == 0:
                    mod_rows("norm")
                for t in range(TILES + 1):
                    if t < TILES:
                        for g in range(2):
                            b = take(("h2T", l, t, g))
                            act.activation(H2T[:, 4 * g:4 * g + 4, t * P:(t + 1) * P], b.rearrange("p (k c) -> p k c", k=4), ACT.Copy)\
                                .then_inc(unit_out, 1)
                    if t:
                        b = take(("rt", l, t - 1))
                        act.activation(LG[:, t - 1, :], b[:, 0:20], ACT.Copy).then_inc(unit_out, 1)
                b = take(("iota", l))
                act.activation(iota_row, b[:, 0:P], ACT.Copy).then_inc(unit_out, 1)
                act.wait_ge(route_arg, l + 1)
                act.activation(gx, gx, ACT.Exp).then_inc(route_exp, 1)
                b = take(("rank", l))
                act.activation(RK, b[:, 0:80], ACT.Copy).then_inc(unit_out, 1)
                b = take(("cnt", l))
                act.activation(CNT, b[:, 0:16], ACT.Copy).then_inc(unit_out, 1)

                def rows_and_silu(i, u):
                    act.wait_ge(xt_done, i + (ETILES * l + 1))
                    for h in range(2):
                        a = act.activation(XGT[:, u, 4 * h:4 * h + 4, :], PS[:, h, :].rearrange("p (k c) -> p k c", k=4), ACT.Copy)
                    a.then_inc(xt_out, 1)
                    act.wait_ge(gu_done, i + (ETILES * l + 1))
                    act.activation(AU[:, u, :], PS[:, 2 + u, 0:256], ACT.Silu).then_inc(silu_out, 1)

                def hidden(i, u):
                    act.wait_ge(ht_done, i + (ETILES * l + 1))
                    act.activation(HID[:, u], PS[:, 7, 0:256].rearrange("p (m c) -> p m c", m=2), ACT.Copy).then_inc(ht_out, 1)

                def group(j):
                    rows_and_silu(3 * j, 0)
                    rows_and_silu(3 * j + 1, 1)
                    hidden(3 * j, 0)
                    rows_and_silu(3 * j + 2, 2)
                    hidden(3 * j + 1, 1)
                    hidden(3 * j + 2, 2)

                act.wait_ge(routed, l + 1)
                groups = act.value_load(NG[0:1, 0:1], min_val=1, max_val=GROUPS)
                group(0)
                with act.Fori(1, SURE) as j:
                    group(j)
                with act.Fori(SURE, GROUPS) as j:
                    with act.If(j < groups):
                        group(j)
                    with act.Else():
                        for moved in (xt_out, silu_out, ht_out):
                            act.wait_ge(moved, 3 * j + ETILES * l)
                            act.sem_inc(moved, 3)

            act_moe(0)

            mod_rows("moe")
            modulate(1)
            act.wait_ge(ln_done, 2 * TILES)
            for n in (2, 0, 1):
                for t in range(TILES):
                    b = take(("qkv", n, t))
                    if n < 2:
                        act.activation(QR[:, t, 512 * n:512 * n + 512], b, ACT.Copy, scale=HD ** -0.5).then_inc(unit_out, 1)
                    else:
                        act.activation(KD[:, t, :, :], b[:, 0:256].rearrange("p (g i) -> p g i", g=KVH), ACT.Copy)
                        act.activation(V[:, t, :], b[:, 256:512], ACT.Copy).then_inc(unit_out, 1)
            for t in range(TILES + 1):
                for r in range(2):
                    b = take(("kT", t, r))
                    act.activation(KTT[r][:, :, t * P:(t + 1) * P], b.rearrange("p (g c) -> p g c", g=KVH), ACT.Copy)\
                        .then_inc(unit_out, 1)
            for t in range(TILES):
                for g in range(2):
                    b = take(("qT", t, g))
                    act.activation(QTT[:, 4 * g:4 * g + 4, t * P:(t + 1) * P], b.rearrange("p (g c) -> p g c", g=4), ACT.Copy)\
                        .then_inc(unit_out, 1)

            def exponentials(n):
                w = P * len(key_tiles(n // HC)[1])
                act.wait_ge(max_ready, n + 1)
                if n >= 3:
                    act.wait_ge(pt_done, n - 2)
                act.activation(PB[:, n % 3, 0:w], PS[:, n % 3, 0:w], ACT.Exp, bias=NM[:, n:n + 1],
                               accum_out=RS[:, n:n + 1]).then_inc(p_ready, 1)

            def take_transposed(n):
                w = P * len(key_tiles(n // HC)[1])
                act.wait_ge(pt_done, n + 1)
                if n >= 3:
                    act.wait_ge(pv_done, n - 2)
                act.activation(PTB[:, n % 3, 0:w], PS[:, 3 + n % 3, 0:w], ACT.Copy).then_inc(pt_out, 1)

            for n in range(STEPS + 2):
                if n < STEPS:
                    exponentials(n)
                if n >= 2:
                    take_transposed(n - 2)
                if n % 8 == 1 and n > 8:
                    g = (n - 8) // 8
                    act.wait_ge(sink_arg, g + 1)
                    act.activation(ES[:, 8 * g:8 * g + 8], ES[:, 8 * g:8 * g + 8], ACT.Exp).then_inc(sink_exp, 1)
            for k in range(KT):
                for part, (a, e) in enumerate(((0, 512), (512, T))):
                    b = take(("yT", 1, k, part))
                    act.activation(HT[:, k, a:e], b[:, 0:e - a], ACT.Copy).then_inc(unit_out, 1)
            out_rows(1)
            act_moe(1)

        @block.vector
        def _(dve):
            count = {}

            def done(i, s=dve_order):
                count[s.name] = count.get(s.name, 0) + 1
                i.then_inc(s, 1)
                dve.wait_ge(s, count[s.name])

            tt, ts, stt = dve.tensor_tensor, dve.tensor_scalar, dve.scalar_tensor_tensor

            dve.wait_ge(unit_out, unit_no[("tm", "gates", TILES - 1)] + 1)
            dve.wait_ge(small_loaded, 64)
            dve.wait_ge(pool_const, 9)
            for d in range(2):
                for s in range(TILES):
                    t = tile_at(d, s)
                    dve.tensor_copy(raw4[:, d, s, 0:8], graw[:, t, 8 * d:8 * d + 8])
                    done(dve.tensor_copy(raw4[:, d, s, 8:16].rearrange("p (g c) -> p g c", g=2),
                                         graw[:, t, 16:32].rearrange("p (g e c) -> p g e c", g=2, e=2)[:, :, d, :]))
            for s in range(TILES):
                done(tt(raw4[:, :, s, :], raw4[:, :, s, :], gbias[:, :, :], ALU.add))
            z = v8(zf)
            done(ts(z[:, :, :, 0:4], raw4[:, :, :, 4:8], -1.0, None, ALU.mult))
            done(dve.tensor_copy(z[:, :, :, 4:8], raw4[:, :, :, 12:16]))
            done(stt(zabs, zf, -1.0, zf, ALU.mult, ALU.max), gate_abs)
            done(ts(zf, zf, 0.0, None, ALU.max))
            dve.wait_ge(gate_ln, 1)
            done(tt(LF, zf, zln, ALU.add))
            done(ts(v8(LF)[:, :, :, 0:4], v8(LF)[:, :, :, 0:4], -1.0, None, ALU.mult))
            dve.wait_ge(alog_exp, 1)
            for s in range(TILES):
                done(stt(v8(LF)[:, :, s, 4:8], v8(LF)[:, :, s, 4:8], -1.0, alog.rearrange("p (d h) -> p d h", d=2),
                         ALU.mult, ALU.mult))
            done(ts(v4(BETA), v4(betaexp), 1.0, None, ALU.add))
            done(dve.reciprocal(BETA, BETA), gate_lf)
            dve.wait_ge(unit_out, unit_no[("rowi", 1, 1)] + 1)
            for d in range(2):
                done(dve.tensor_tensor_scan(MR[:, d, 0:P], ROWF[:, d, 0:P], ROWI[:, d, 0:P], 0.0, ALU.add, ALU.max))
                done(dve.tensor_tensor_scan(MR[:, d, P:T], ROWF[:, d, P:T], ROWI[:, d, P:T], M0[0:4, d:d + 1], ALU.add,
                                            ALU.max), m_scanned)
            mv = MV.rearrange("p (d s) -> p d s", d=2)
            done(dve.memset(mv[0:4, :, 0:1], 0.0))
            done(dve.tensor_copy(mv[0:4, :, 1:2], MR[:, :, P - 1:P]))
            done(dve.tensor_copy(mv[0:4, :, 2:3], M0[0:4, :].unsqueeze(2)))
            done(dve.tensor_copy(mv[0:4, :, 3:7], MR[:, :, 2 * P - 1:T:P]))
            done(tt(MEX[0:4, :].rearrange("p (n h) -> p n h", h=4), MV[0:4, :].unsqueeze(2).to_broadcast([4, 14, 4]),
                    CST[0:4, C_ID, 0:4].unsqueeze(1).to_broadcast([4, 14, 4]), ALU.mult), mex_ready)
            dve.wait_ge(unit_out, unit_no[("mvb",)] + 1)
            cs, ce, m = v8(CS), v8(CE), v4(MC)
            mb = MVB.rearrange("p (d n h) -> p d n h", d=2, n=7)
            B, G, BE, GE = cs[:, :, :, 0:4], cs[:, :, :, 4:8], ce[:, :, :, 0:4], ce[:, :, :, 4:8]
            arg = [v4(ARG[:, n, :]) for n in range(7)]
            done(tt(v4(CB[:, 0, :]), raw4[:, :, :, 0:4], B, ALU.subtract))
            done(ts(v4(CB[:, 1, :]), G, -1.0, None, ALU.mult))
            done(tt(v4(RV[:, 0, :]), B, m, ALU.subtract))
            done(dve.tensor_copy(v4(RV[:, 1, :]), G))
            done(ts(arg[EN], m, -1.0, None, ALU.mult))
            done(tt(arg[WE], BE, v4(CB[:, 0, :]), ALU.add))
            done(dve.tensor_copy(arg[WI], v4(RV[:, 0, :])))
            done(dve.tensor_copy(arg[DC], BE))
            for s in range(TILES):
                before, after = (0, 1) if s == 0 else (s + 1, s + 2)
                done(tt(arg[WI][:, :, s, :], arg[WI][:, :, s, :], mb[:, :, before, :], ALU.add))
                done(tt(arg[DC][:, :, s, :], arg[DC][:, :, s, :], mb[:, :, before, :], ALU.add))
                done(tt(arg[DC][:, :, s, :], arg[DC][:, :, s, :], mb[:, :, after, :], ALU.subtract))
                done(tt(arg[WE][:, :, s, :], arg[WE][:, :, s, :], mb[:, :, after, :], ALU.subtract))
            done(dve.tensor_copy(arg[EG], G))
            done(tt(arg[EE], GE, G, ALU.subtract))
            done(dve.tensor_copy(arg[ED], GE), arg_ready)

            dve.wait_ge(exp_ready, 1)
            dve.wait_ge(state_loaded, 48)
            dve.wait_ge(unit_out, unit_no[("ktok", "a", TILES - 1)] + 1)

            def ex(n, d, s):
                return v4(EX[:, n, :])[:, d, s, :]

            for s in range(TILES):
                q = 1 if s else 0
                for d in range(2):
                    dve.wait_ge(ml_de[d], s + 1)
                    dve.wait_ge(ml_st[d], s + 1)
                    done(tt(mlb(d, 1), mlb(d, 0), PS[:, 4 * d, :], ALU.mult), ml_sw[d])
                for d in range(2):
                    A, Bk, C, E = (PS[:, 4 * d + n, :] for n in range(4))
                    dve.wait_ge(ml_u[d], s + 1)
                    done(tt(t4[:, 0:4], E[:, 4:8], ex(WI, d, s), ALU.mult))
                    done(tt(t4[:, 0:4], t4[:, 0:4], E[:, 0:4], ALU.add))
                    done(stt(t4b[:, 0:4], t4[:, 0:4], -1.0, t4[:, 0:4], ALU.mult, ALU.max))
                    done(tt(t4b[:, 0:4], t4b[:, 0:4], ex(EN, d, s), ALU.max))
                    done(dve.reciprocal(t4[:, 0:4], t4b[:, 0:4]))
                    w = mlb(d, 3)
                    done(tt(heads(w), heads(Bk), col(ex(WI, d, s), P), ALU.mult))
                    done(tt(w, w, A, ALU.add))
                    y = YA[:, tile_at(d, s), :]
                    if s > 2 or (s == 0 and d == 1):
                        done(tt(heads(w), heads(w), col(t4[:, 0:4], P), ALU.mult))
                        done(tt(y, y, w, ALU.add))
                    else:
                        done(tt(heads(y), heads(w), col(t4[:, 0:4], P), ALU.mult))
                    c = SM[:, q, 4 * d:4 * d + 4, :]
                    nn = NS[:, q, 4 * d:4 * d + 4]
                    done(tt(c, c, col(ex(DC, d, s), P), ALU.mult))
                    done(tt(c, c, heads(C), ALU.add))
                    done(tt(nn, nn, ex(DC, d, s), ALU.mult))
                    done(tt(nn, nn, E[:, 8:12], ALU.add), ml_done[d])

            def sums(y, dst, sq=None):
                for t in range(TILES):
                    v = heads(y[:, t, :])
                    if sq is not None:
                        done(tt(sq, y[:, t, :], y[:, t, :], ALU.mult))
                        v = heads(sq)
                    done(dve.tensor_reduce(dst[:, 4 * t:4 * t + 4], v, AX.X, ALU.add))

            sums(YA, st20)
            done(ts(st20, st20, 1.0 / P, None, ALU.mult))
            for t in range(TILES):
                done(tt(heads(YA[:, t, :]), heads(YA[:, t, :]), col(st20[:, 4 * t:4 * t + 4], P), ALU.subtract))
            sums(YA, st20b, mlb(0, 0))
            done(ts(st20, st20b, 1.0 / P, LN_EPS, ALU.mult, ALU.add), var_ready)

            def gated(y, g, first):
                for t in range(TILES):
                    v = y[:, t, :]
                    done(tt(heads(v), heads(v), col(rstd[:, 4 * t:4 * t + 4], P), ALU.mult))
                    done(tt(v, v, GAIN[:, g, :], ALU.mult))
                    dve.wait_ge(unit_out, unit_no[("tm", ("oa", "zb")[g], t)] + 1)
                    done(tt(v, v, SG[t % 2], ALU.mult), gate_used)

            dve.wait_ge(rstd_ready, 1)
            dve.wait_ge(gain_loaded, 32)
            gated(YA, 0, 0)

            def conv(name, dst, g, first):
                for m in range(4):
                    dve.wait_ge(unit_out, unit_no[("fm", name, m, 1)] + 1)
                    c = 4 * g + m
                    o, i = dst[:, m, :], PRE[:, m, :]
                    done(ts(o, i, convw[:, 12 + c:13 + c], None, ALU.mult))
                    for a, e in ((0, P), (P, T)):
                        done(stt(o[:, a + 1:e], i[:, a:e - 1], convw[:, c:c + 1], o[:, a + 1:e], ALU.mult, ALU.add))
                    done(stt(o[:, 0:P - 1], i[:, 1:P], convw[:, 24 + c:25 + c], o[:, 0:P - 1], ALU.mult, ALU.add))
                    done(stt(o[:, P:T - 1], i[:, P + 1:T], convw[:, 24 + c:25 + c], o[:, P:T - 1], ALU.mult, ALU.add),
                         conv_done)

            def unit_norm(name, dst):
                for m in range(4):
                    dve.wait_ge(unit_out, unit_no[("ssq", name, m, 1)] + 1)
                    done(dve.reciprocal(NRM[:, m, :], NRM[:, m, :]))
                    done(tt(dst[:, m, :], dst[:, m, :], NRM[:, m, :], ALU.mult), normed)

            conv("vd", QT, 2, 0)
            conv("kd", KTR, 1, 4)
            unit_norm("kd", KTR)
            dve.wait_ge(unit_out, unit_no[("vtok", TILES - 1)] + 1)
            conv("qd", QT, 0, 8)
            unit_norm("qd", QT)

            dve.wait_ge(unit_out, unit_no[("ktok", "d", TILES - 1)] + 1)
            for s in range(TILES):
                q = 1 if s else 0
                bk = [[PS[:, 4 * d + n, :] for n in range(4)] for d in range(2)]
                for d in range(2):
                    dve.wait_ge(dl_de[d], s + 1)
                    dve.wait_ge(dl_kk[d], s + 1)
                    done(tt(dlb(d, 1), dlb(d, 0), bk[d][2], ALU.mult), dl_qd[d])
                    done(tt(dlb(d, 2), dlb(d, 0), bk[d][0], ALU.mult), dl_at[d])
                for n in range(1, 7):
                    for d in range(2):
                        dve.wait_ge(dl_p2[d], 6 * s + n)
                        if n < 6:
                            done(tt(dlb(d, 3), dlb(d, 3), bk[d][1], ALU.subtract), dl_x[d])
                        done(tt(dlb(d, 4), dlb(d, 4), bk[d][2], ALU.subtract), dl_xt[d])
                for d in range(2):
                    r = dlb(d, 2)
                    dve.wait_ge(dl_ks[d], s + 1)
                    dve.wait_ge(dl_cm[d], 6 * s + 6)
                    done(tt(heads(r), heads(bk[d][3]), col(ex(EG, d, s), P), ALU.mult))
                    done(tt(r, VTOK[:, tile_at(d, s), :], r, ALU.subtract), dl_r[d])
                for d in range(2):
                    dve.wait_ge(dl_tr[d], s + 1)
                    done(tt(heads(dlb(d, 3)), heads(bk[d][0]), col(v4(BETA)[:, d, s, :], P), ALU.mult), dl_vn[d])
                for d in range(2):
                    w = dlb(d, 0)
                    y = YB[:, tile_at(d, s), :]
                    dve.wait_ge(dl_o[d], s + 1)
                    done(tt(heads(w), heads(bk[d][1]), col(ex(EG, d, s), P), ALU.mult))
                    if s > 2 or (s == 0 and d == 1):
                        done(tt(w, w, bk[d][2], ALU.add))
                        done(tt(y, y, w, ALU.add))
                    else:
                        done(tt(y, w, bk[d][2], ALU.add))
                    c = SD[:, q, 4 * d:4 * d + 4, :]
                    done(tt(c, c, col(ex(ED, d, s), P), ALU.mult))
                    dve.wait_ge(dl_su[d], s + 1)
                    done(tt(c, c, heads(bk[d][3]), ALU.add), dl_done[d])

            sums(YB, st20b, dlb(0, 0))
            done(ts(st20, st20b, 1.0 / P, LN_EPS, ALU.mult, ALU.add), var_ready)
            dve.wait_ge(rstd_ready, 2)
            gated(YB, 1, TILES)
            count_y = [0]

            def layer_norm(nth, t):
                for n in range(2):
                    done(dve.bn_stats(bnst[:, t, n, :], X[:, t, 512 * n:512 * n + 512]))
                done(dve.bn_aggr(bnag[:, t, :], bnst[:, t, :, :]))
                done(ts(lnr[:, t:t + 1], bnag[:, t, 1:2], LN_EPS, None, ALU.add), var_ready)
                dve.wait_ge(rstd_ready, 3 + TILES * nth + t)
                done(ts(X[:, t, :], X[:, t, :], bnag[:, t, 0:1], lnr[:, t:t + 1], ALU.subtract, ALU.mult))
                done(tt(X[:, t, :], X[:, t, :], BC[:, 2, :], ALU.mult))
                done(tt(X[:, t, :], X[:, t, :], BC[:, 3, :], ALU.add), ln_done)

            def residual(l):
                dve.wait_ge(bc_loaded, 64 * (2 * l + 1))
                for n in range(2):
                    for t in range(TILES):
                        j = TILES * n + t
                        dve.wait_ge(unit_out, unit_no[("out", l, n, t)] + 1)
                        c = slice(512 * n, 512 * n + 512)
                        done(tt(YO[j % 2], YO[j % 2], BC[:, min(t, 1), c], ALU.mult))
                        done(stt(X[:, t, c], X[:, t, c], ALPHA, YO[j % 2], ALU.mult, ALU.add), out_used)
                        if n:
                            v = min(t, 1)
                            layer_norm(2 * l, t)
                            dve.wait_ge(bc2_loaded, 64 * (l + 1))
                            done(stt(H2[:, t, :], BC2[:, 2 + v, :], 1.0, X[:, t, :], ALU.add, ALU.mult))
                            done(tt(H2[:, t, :], H2[:, t, :], BC2[:, v, :], ALU.add), h2_ready)

            residual(0)

            def first_max(values, vmax_, cand_, hot):
                done(dve.tensor_reduce(vmax_, values, AX.X, ALU.max))
                done(tt(cand_, values, vmax_.unsqueeze(2).to_broadcast([P, TILES, 4]), ALU.is_equal))
                done(stt(cand_, cand_, -100.0, IOTA[:, 0:4].unsqueeze(1).to_broadcast([P, TILES, 4]), ALU.mult, ALU.add))
                done(dve.tensor_reduce(cmin, cand_, AX.X, ALU.min))
                done(tt(hot, cand_, cmin.unsqueeze(2).to_broadcast([P, TILES, 4]), ALU.is_equal))

            def dve_moe(l):
                dve.wait_ge(unit_out, unit_no[("rt", l, TILES - 1)] + 1)
                dve.wait_ge(router_loaded, 16 * 7 * (l + 1))
                done(tt(LG[:, :, :], LG[:, :, :], RB.unsqueeze(1).to_broadcast([P, TILES, 20]), ALU.add))
                lg = LG[:, :, 0:4]
                first_max(lg, gmax, cand, ghot)
                g3 = gx[:, 0:20].rearrange("p (t c) -> p t c", t=TILES)
                done(tt(g3, lg, gmax.unsqueeze(2).to_broadcast([P, TILES, 4]), ALU.subtract))
                r4 = rtmp.rearrange("p (t g e) -> p t g e", t=TILES, g=4)
                done(tt(r4, LG[:, :, 4:20].rearrange("p t (g e) -> p t g e", g=4),
                        ghot.unsqueeze(3).to_broadcast([P, TILES, 4, 4]), ALU.mult))
                done(dve.tensor_reduce(LE, rtmp.rearrange("p (t g e) -> p t e g", t=TILES, g=4), AX.X, ALU.add))
                first_max(LE, vmax, cand, hot1)
                done(stt(LE2, hot1, NEG, LE, ALU.mult, ALU.add))
                first_max(LE2, vsec, cand, hot2)
                done(tt(gx[:, 20:25], vsec, vmax, ALU.subtract), route_arg)
                dve.wait_ge(route_exp, l + 1)
                done(dve.tensor_reduce(gsum, g3, AX.X, ALU.add))
                done(dve.reciprocal(gw, gsum))
                done(ts(gsum, gx[:, 20:25], 1.0, None, ALU.add))
                done(dve.reciprocal(gsum, gsum))
                done(tt(WSEL[:, 0, :], gsum, gw, ALU.mult))
                done(tt(WSEL[:, 1, :], WSEL[:, 0, :], gx[:, 20:25], ALU.mult))
                for c, hot in enumerate((hot1, hot2)):
                    done(tt(HE[:, c].rearrange("p t (g e) -> p t g e", g=4), ghot.unsqueeze(3).to_broadcast([P, TILES, 4, 4]),
                            hot.unsqueeze(2).to_broadcast([P, TILES, 4, 4]), ALU.mult))
                done(tt(HALL.rearrange("p (t e) -> p t e", t=TILES), HE[:, 0], HE[:, 1], ALU.add), hot_ready)
                dve.wait_ge(unit_out, unit_no[("cnt", l)] + 1)
                b4 = big[:, 0:64].rearrange("p (e j) -> p e j", e=16)
                done(tt(b4, CNT.unsqueeze(2).to_broadcast([P, 16, 4]), IOTA[:, 9:13].unsqueeze(1).to_broadcast([P, 16, 4]),
                        ALU.is_gt))
                done(dve.tensor_reduce(OV, b4, AX.X, ALU.add))
                done(dve.tensor_tensor_scan(OVC, OV, zero16, 0.0, ALU.add, ALU.add))
                done(tt(OBASE, OVC, OV, ALU.subtract))
                done(ts(OBASE, OBASE, float(P), float(P * (NEXP - 1) - 1), ALU.mult, ALU.add))
                done(ts(EBASE, IOTA[:, 16:32], float(P), -1.0, ALU.mult, ALU.add))
                done(tt(OBASE, OBASE, EBASE, ALU.subtract))
                done(ts(past, RK, float(P), None, ALU.is_gt))
                rk, ps = (x.rearrange("p (t e) -> p t e", t=TILES) for x in (RK, past))
                done(tt(ps, ps, OBASE.unsqueeze(1).to_broadcast([P, TILES, 16]), ALU.mult))
                done(tt(rk, rk, EBASE.unsqueeze(1).to_broadcast([P, TILES, 16]), ALU.add))
                done(tt(rk, rk, ps, ALU.add))
                for c in range(2):
                    r3 = rtmp.rearrange("p (t e) -> p t e", t=TILES)
                    done(tt(r3, rk, HE[:, c], ALU.mult))
                    done(dve.tensor_reduce(slotf[:, TILES * c:TILES * c + TILES], r3, AX.X, ALU.add))
                nt = 2 * TILES
                tiles_ = IOTA[:, 16:16 + ETILES].unsqueeze(1).to_broadcast([P, nt, ETILES])
                bt = big.rearrange("p (n i) -> p n i", n=nt)
                done(ts(low, slotf, 1.0 / P, None, ALU.mult))
                done(tt(bt, low.unsqueeze(2).to_broadcast([P, nt, ETILES]), tiles_, ALU.is_ge))
                done(dve.tensor_reduce(tile_at_slot, bt, AX.X, ALU.add))
                done(ts(tile_at_slot, tile_at_slot, -1.0, None, ALU.add))
                done(stt(low, tile_at_slot, -float(P), slotf, ALU.mult, ALU.add))
                done(tt(HOTT, tiles_, tile_at_slot.unsqueeze(2).to_broadcast([P, nt, ETILES]), ALU.is_equal))
                for c in range(2):
                    done(tt(HOTT[:, TILES * c:TILES * c + TILES], HOTT[:, TILES * c:TILES * c + TILES],
                            IOTA[:, 48:53].unsqueeze(2).to_broadcast([P, TILES, ETILES]), ALU.mult))
                done(tt(HOTL, iota_row.unsqueeze(1).to_broadcast([P, nt, P]), low.unsqueeze(2).to_broadcast([P, nt, P]),
                        ALU.is_equal), slots_ready)
                bo = big[:, 0:16 * (ETILES - NEXP)].rearrange("p (i e) -> p i e", i=ETILES - NEXP)
                done(tt(bo, OVC.unsqueeze(1).to_broadcast([P, ETILES - NEXP, 16]),
                        IOTA[:, 16:16 + ETILES - NEXP].unsqueeze(2).to_broadcast([P, ETILES - NEXP, 16]), ALU.is_le))
                done(dve.tensor_reduce(eotf[:, NEXP:ETILES], bo, AX.X, ALU.add))
                done(ts(eotf[:, NEXP:ETILES], eotf[:, NEXP:ETILES], float(NEXP - 1), None, ALU.min))
                done(dve.tensor_copy(eotf[:, 0:NEXP], IOTA[:, 16:32]))
                done(ts(ngf, OVC[:, 15:16], float(NEXP), None, ALU.add))
                done(tt(big[:, 0:GROUPS], ngf.to_broadcast([P, GROUPS]), IOTA[:, 53:53 + GROUPS], ALU.is_gt))
                done(dve.tensor_reduce(ngf, big[:, 0:GROUPS], AX.X, ALU.add))
                done(dve.tensor_copy(NG, ngf))
                done(dve.tensor_copy(EOT, eotf), routed)
                dve.wait_ge(unit_done, unit_no[("tok", l)] + 1)
                dve.tensor_copy(TOKI, PS[:, unit_no[("tok", l)] % BANKS, 0:ETILES]).then_inc(unit_out, 1)
                done(dve.tensor_copy(IDX[:, :, :], slotf.rearrange("p (c t) -> p c t", c=2)), slots_cast)

                def gated_values(i, u):
                    dve.wait_ge(silu_out, i + (ETILES * l + 1))
                    dve.tensor_tensor(HIDR[:, u, :], AU[:, u, :], PS[:, 2 + u, 256:512], ALU.mult).then_inc(hid_ready, 1)

                def rows_out(i, j, u, first):
                    if not first:
                        dve.wait_ge(ye_stored[u], 16 * j + 16 * GROUPS * l)
                    dve.wait_ge(down_done, i + (ETILES * l + 1))
                    dve.tensor_copy(YE[:, u, :].rearrange("p (h c) -> p h c", h=2), PS[:, 5:7, :]).then_inc(ye_ready, 1)

                def group(j, first=False):
                    gated_values(3 * j, 0)
                    gated_values(3 * j + 1, 1)
                    rows_out(3 * j, j, 0, first)
                    gated_values(3 * j + 2, 2)
                    rows_out(3 * j + 1, j, 1, first)
                    rows_out(3 * j + 2, j, 2, first)

                group(0, True)
                groups = dve.value_load(NG[0:1, 0:1], min_val=1, max_val=GROUPS)
                with dve.Fori(1, SURE) as j:
                    group(j)
                with dve.Fori(SURE, GROUPS) as j:
                    with dve.If(j < groups):
                        group(j)
                    with dve.Else():
                        for moved in (hid_ready, ye_ready):
                            dve.wait_ge(moved, 3 * j + ETILES * l)
                            dve.sem_inc(moved, 3)
                dve.wait_ge(ye_ready, ETILES * (l + 1))
                count["ye_ready"] = ETILES * (l + 1)
                dve.wait_ge(bc_loaded, 64 * (2 * l + 2))
                for t in range(TILES):
                    g = YG[:, t % 2]
                    dve.wait_ge(yg_gathered[t % 2], 32 * (t // 2 + 1 + l * (3 - t % 2)))
                    done(ts(g[:, 0, :], g[:, 0, :], WSEL[:, 0, t:t + 1], None, ALU.mult))
                    done(stt(g[:, 0, :], g[:, 1, :], WSEL[:, 1, t:t + 1], g[:, 0, :], ALU.mult, ALU.add))
                    done(tt(g[:, 0, :], g[:, 0, :], BC[:, min(t, 1), :], ALU.mult))
                    done(stt(X[:, t, :], X[:, t, :], ALPHA, g[:, 0, :], ALU.mult, ALU.add), yg_used)
                    layer_norm(2 * l + 1, t)

            dve_moe(0)

            def rotate(x, heads_, t):
                w = heads_ * HD
                tmp = RTMP[:, 0:w]
                cos, sin = (ROPE[:, a, t - 1, :] for a in range(2))
                xs = x.rearrange("p h (a f i) -> p h a f i", a=2, f=2)
                ys = tmp.rearrange("p (h a f i) -> p h a f i", h=heads_, a=2, f=2)
                sn = sin.rearrange("p (a f i) -> p a f i", a=2, f=2)
                for f in range(2):
                    done(tt(ys[:, :, :, f, :], xs[:, :, :, 1 - f, :],
                            sn[:, :, f, :].unsqueeze(1).to_broadcast([P, heads_, 2, HD // 4]), ALU.mult))
                done(tt(x, x, cos.unsqueeze(1).to_broadcast([P, heads_, HD]), ALU.mult))
                return tt(x, x, tmp.rearrange("p (h i) -> p h i", h=heads_), ALU.add)

            done(dve.memset(KZERO, 0.0), keys_ready)
            dve.wait_ge(attn_loaded, 64)
            for t in range(1, TILES):
                dve.wait_ge(unit_out, unit_no[("qkv", 2, t)] + 1)
                done(rotate(KD[:, t, :, :], KVH, t), keys_ready)
            for n in range(2):
                for t in range(TILES):
                    dve.wait_ge(unit_out, unit_no[("qkv", n, t)] + 1)
                    x = QR[:, t, 512 * n:512 * n + 512].rearrange("p (h i) -> p h i", h=8)
                    if t:
                        done(rotate(x, 8, t), queries_ready)
                    else:
                        done(dve.tensor_copy(RTMP[:, 0:1], x[:, 0, 0:1]), queries_ready)
            dve.wait_ge(unit_out, unit_no[("qT", TILES - 1, 1)] + 1)
            for n, c in enumerate((C_ID, C_NF, C_NB)):
                done(dve.tensor_copy(MASKS[:, n, :], CST[:, c, :]), masks_ready)

            def normalise(g):
                c = slice(8 * g, 8 * g + 8)
                dve.wait_ge(sink_exp, g + 1)
                dve.wait_ge(pv_done, 8 * g + 8)
                done(tt(ES[:, c], ES[:, c], RS[:, c], ALU.add))
                done(dve.reciprocal(ES[:, c], ES[:, c]))
                o = QR[:, g // 2, 512 * (g % 2):512 * (g % 2) + 512].rearrange("p (h i) -> p h i", h=8)
                done(tt(o, PS[:, 6 + g % 2, :].rearrange("p (h i) -> p h i", h=8),
                        ES[:, c].unsqueeze(2).to_broadcast([P, 8, HD]), ALU.mult), o_ready)

            for n in range(STEPS):
                h = n % HC
                w = P * len(key_tiles(n // HC)[1])
                dve.wait_ge(s_done, n + 1)
                done(dve.tensor_reduce(NM[:, n:n + 1], PS[:, n % 3, 0:w], AX.X, ALU.max))
                done(ts(NM[:, n:n + 1], NM[:, n:n + 1], SINK[:, h:h + 1], -1.0, ALU.max, ALU.mult), max_ready)
                if n % 8 == 7:
                    done(tt(ES[:, n - 7:n + 1], SINK[:, h - 7:h + 1], NM[:, n - 7:n + 1], ALU.add), sink_arg)
                if n % 8 == 5 and n > 8:
                    normalise((n - 8) // 8)
            normalise(STEPS // 8 - 1)
            residual(1)
            dve_moe(1)

        @block.tensor
        def _(pe):
            def begin(name):
                n = unit_no[name]
                if n >= BANKS:
                    pe.wait_ge(unit_out, n - BANKS + 1)
                return PS[:, n % BANKS, :]

            def out_of(name):
                pe.wait_ge(unit_out, unit_no[name] + 1)

            def weights(item):
                n = load_no[item]
                pe.wait_ge(slot_arrived[slot_of(n)], arrived_at[n])
                return slot_cols(n, KT, 32 if item == ("in", "gates") else 512), slot_of(n)

            pe.wait_ge(const_loaded, 80)
            b = begin(("cT",))
            pe.transpose(b[:, 0:16], cin, CST[0:16, C_ID, 0:16]).then_inc(unit_done, 1)
            b = begin(("convT",))
            pe.transpose(b[:, 0:36], convrow, CST[0:36, C_ID, 0:36]).then_inc(unit_done, 1)

            def mod_rows(name):
                part = mod_parts[name]

                def partial(l, c):
                    b = begin(("mod", l, c))
                    w, s = weights(("mod", l, c))
                    for k in range(KT):
                        g = k % 4
                        pe.matmul(b[32 * g:32 * g + 32, :], csil[:, 32 * k:32 * k + 32], w[:, k, :],
                                  start=(k < 4), stop=False)
                    for g in range(4):
                        i = pe.matmul(b[32 * g:32 * g + 32, g * P:(g + 1) * P], CST[0:1, C_ONES, 0:32],
                                      SLOTS[0:1, s, 4096 + g * P:4096 + (g + 1) * P], start=False, stop=True)
                    i.then_inc(unit_done, 1)

                for j, (l, c) in enumerate(part):
                    for lc in part[0:2] if j == 0 else part[j + 1:j + 2]:
                        partial(*lc)
                    b = begin(("modS", l, c))
                    out_of(("mod", l, c))
                    pe.matmul(b[0:2, :], IOTA[:, 64:66], MSUM[:, c % 2, :], start=True, stop=True).then_inc(unit_done, 1)
                    if c < 4:
                        b = begin(("modT", l, c))
                        out_of(("modS", l, c))
                        for q in range(4):
                            i = pe.transpose(b[:, 2 * q:2 * q + 2], MROW[:, c % 2, q * P:(q + 1) * P], CST[0:2, C_ID, 0:2])
                        i.then_inc(unit_done, 1)

            def transposes_of_x(l):
                for k in range(KT):
                    b = begin(("hTlat", l, k))
                    for t in range(1, TILES):
                        i = pe.transpose(b[:, (t - 1) * P:t * P], X[:, t, k * P:(k + 1) * P], ident)
                    i.then_inc(unit_done, 1)
                for g in range(2):
                    b = begin(("hTctx", l, g))
                    for q in range(4):
                        i = pe.transpose(b[:, q * P:(q + 1) * P], X[:, 0, (4 * g + q) * P:(4 * g + q + 1) * P], ident)
                    i.then_inc(unit_done, 1)

            def feature_major(name):
                w, s = weights(("in", name))
                for m in range(4):
                    for h in range(2):
                        b = begin(("fm", name, m, h))
                        for k in range(KT):
                            i = pe.matmul(b[:, 0:320], w[:, k, m * P:(m + 1) * P], HT[:, k, 320 * h:320 * h + 320],
                                          start=(k == 0), stop=(k == KT - 1))
                        i.then_inc(unit_done, 1)

            def token_major(name, width=512):
                w, s = weights(("in", name))
                for t in range(TILES):
                    b = begin(("tm", name, t))
                    for k in range(KT):
                        i = pe.matmul(b[:, 0:width], HT[:, k, t * P:(t + 1) * P], w[:, k, :],
                                      start=(k == 0), stop=(k == KT - 1))
                    i.then_inc(unit_done, 1)

            def head_transposes(name, src):
                for t in range(TILES):
                    b = begin(name + (t,))
                    for h in range(HEADS):
                        i = pe.transpose(b[:, h * P:(h + 1) * P], src[:, h, t * P:(t + 1) * P], ident)
                    i.then_inc(unit_done, 1)

            out_of(("cT",))
            mod_rows("first")
            pe.wait_ge(x_loaded, 32)
            transposes_of_x(0)
            out_of(("hTctx", 0, 1))
            token_major("gates", 32)
            feature_major("qa")
            mod_rows("qa")
            pe.wait_ge(gate_lf, 1)
            for d in range(2):
                b = begin(("cs", d))
                pe.matmul(b[:, 0:40], CST[:, (C_UPI, C_LOI)[d], :], LF[:, 40 * d:40 * d + 40], start=True, stop=True)\
                    .then_inc(unit_done, 1)
            b = begin(("ce",))
            pe.matmul(b[:, 0:80], ones, LF, start=True, stop=True).then_inc(unit_done, 1)
            for name, src, c in (("rowf", v8(LF), 0), ("rowi", raw4, 0)):
                for d in range(2):
                    for part, steps in enumerate((range(4), range(4, 5))):
                        b = begin((name, d, part))
                        for j, s in enumerate(steps):
                            i = pe.matmul(b[0:4, j * P:(j + 1) * P], src[:, d, s, 0:4], (ident, flip)[d], start=True, stop=True)
                        i.then_inc(unit_done, 1)
            feature_major("ka")
            mod_rows("ka")
            for d in range(2):
                b = begin(("mcol", d))
                pe.wait_ge(m_scanned, d + 1)
                for s in range(TILES):
                    i = pe.matmul(b[:, 4 * s:4 * s + 4], MR[:, d, s * P:(s + 1) * P], CST[0:4, C_ID, 0:4], start=True, stop=True)
                i.then_inc(unit_done, 1)
            b = begin(("mflip",))
            out_of(("mcol", 1))
            pe.matmul(b[:, 0:20], flip, rev, start=True, stop=True).then_inc(unit_done, 1)
            b = begin(("mvb",))
            pe.wait_ge(mex_ready, 1)
            pe.matmul(b[:, 0:56], CST[0:4, C_ONES, :], MEX[0:4, :], start=True, stop=True).then_inc(unit_done, 1)
            token_major("va")
            mod_rows("va")
            out_of(("fm", "ka", 3, 1))
            head_transposes(("ktok", "a"), KTR)

            out_of(("ktok", "a", TILES - 1))
            pe.wait_ge(state_loaded, 48)
            pe.wait_ge(pool_const, 9)
            pe.wait_ge(exp_ready, 1)

            def decay(d, s, which, bank_):
                for h in range(HEADS):
                    o = bank_[:, h * P:(h + 1) * P]
                    v = v4(RV[:, which, :])[:, d, s, h:h + 1]
                    pe.matmul(o, v.to_broadcast([P, P]), ident, start=True, stop=False)
                    i = pe.matmul(o, ident, CST[:, (C_NF, C_NB)[d], :], start=False, stop=True)
                return i

            for s in range(TILES):
                q = 1 if s else 0
                for d in range(2):
                    A, Bk, C, E = (PS[:, 4 * d + n, :] for n in range(4))
                    tk = slice(tile_at(d, s) * P, tile_at(d, s) * P + P)
                    if s:
                        pe.wait_ge(ml_done[d], s)
                    for h in range(HEADS):
                        i = pe.matmul(A[:, h * P:(h + 1) * P], KTR[:, h, tk], QT[:, h, tk], start=True, stop=True)
                    i.then_inc(ml_st[d], 1)
                    decay(d, s, 0, Bk).then_inc(ml_db[d], 1)
                for d in range(2):
                    A, Bk, C, E = (PS[:, 4 * d + n, :] for n in range(4))
                    t = tile_at(d, s)
                    tk = slice(t * P, t * P + P)
                    pe.wait_ge(ml_sw[d], s + 1)
                    for h in range(HEADS):
                        sw = mlb(d, 1)[:, h * P:(h + 1) * P]
                        pe.matmul(A[:, h * P:(h + 1) * P], sw, VTOK[:, t, h * P:(h + 1) * P], start=True, stop=True)
                        pe.matmul(E[:, h:h + 1], sw, CST[:, C_ONES, 0:1], start=True, stop=True)
                        pe.matmul(Bk[:, h * P:(h + 1) * P], QT[:, h, tk], SM[:, q, 4 * d + h, :], start=True, stop=True)
                        pe.matmul(E[:, 4 + h:5 + h], QT[:, h, tk], NS[:, q, 4 * d + h:4 * d + h + 1], start=True, stop=True)
                    pe.wait_ge(ml_vw[d], s + 1)
                    for h in range(HEADS):
                        kk = KTOK[:, t, h * P:(h + 1) * P]
                        pe.matmul(C[:, h * P:(h + 1) * P], kk, mlb(d, 2)[:, h * P:(h + 1) * P], start=True, stop=True)
                        i = pe.matmul(E[:, 8 + h:9 + h], kk, v4(EX[:, WE, :])[:, d, s, h:h + 1], start=True, stop=True)
                    i.then_inc(ml_u[d], 1)
            for d in range(2):
                pe.wait_ge(ml_done[d], TILES)
            token_major("oa")
            feature_major("vd")
            mod_rows("vd")
            pe.wait_ge(silu_done, 4)
            head_transposes(("vtok",), QT)
            feature_major("kd")
            mod_rows("kd")

            def square_sums(name, first):
                for m in range(4):
                    for h in range(2):
                        b = begin(("ssq", name, m, h))
                        pe.wait_ge(sq_ready, first + m + 1)
                        pe.matmul(b[:, 0:320], ones, SQ[:, m, 320 * h:320 * h + 320], start=True, stop=True)\
                            .then_inc(unit_done, 1)

            square_sums("kd", 0)
            mod_rows("kd2")
            pe.wait_ge(normed, 4)
            head_transposes(("ktok", "d"), KTR)
            feature_major("qd")
            mod_rows("qd")
            square_sums("qd", 4)
            mod_rows("qd2")
            pe.wait_ge(normed, 8)

            out_of(("modS",) + mod_parts["qd2"][-1])
            for s in range(TILES):
                q = 1 if s else 0
                bk = [[PS[:, 4 * d + n, :] for n in range(4)] for d in range(2)]

                def mm4(o, lhsT, rhs):
                    for h in range(HEADS):
                        c = slice(h * P, (h + 1) * P)
                        i = pe.matmul(o[:, c], lhsT[:, c], rhs[:, c], start=True, stop=True)
                    return i

                for d in range(2):
                    A, Bk, C, E = bk[d]
                    tk = slice(tile_at(d, s) * P, tile_at(d, s) * P + P)
                    if s:
                        pe.wait_ge(dl_done[d], s)
                    for h in range(HEADS):
                        c = slice(h * P, (h + 1) * P)
                        pe.matmul(A[:, c], KTR[:, h, tk], KTR[:, h, tk], start=True, stop=True)
                        i = pe.matmul(C[:, c], KTR[:, h, tk], QT[:, h, tk], start=True, stop=True)
                    i.then_inc(dl_kk[d], 1)
                    decay(d, s, 1, Bk).then_inc(dl_db[d], 1)
                    for h in range(HEADS):
                        c = slice(h * P, (h + 1) * P)
                        i = pe.matmul(E[:, c], KTR[:, h, tk], SD[:, q, 4 * d + h, :], start=True, stop=True)
                    i.then_inc(dl_ks[d], 1)
                for d in range(2):
                    pe.wait_ge(dl_xt1[d], s + 1)
                    for h in range(HEADS):
                        c = slice(h * P, (h + 1) * P)
                        i = pe.transpose(bk[d][0][:, c], dlb(d, 4)[:, c], ident)
                    i.then_inc(dl_x1t[d], 1)
                for n in range(1, 7):
                    for d in range(2):
                        if n == 1:
                            pe.wait_ge(dl_x1[d], s + 1)
                        else:
                            pe.wait_ge(dl_x[d], 5 * s + n - 1)
                        pe.wait_ge(dl_cm[d], 6 * s + n)
                        mm4(bk[d][0], dlb(d, 5 + n % 2), dlb(d, 3)).then_inc(dl_p1[d], 1)
                    for d in range(2):
                        pe.wait_ge(dl_p1s[d], 6 * s + n)
                        pe.wait_ge(dl_xt[d], 6 * s + n - 1) if n > 1 else pe.wait_ge(dl_qd[d], s + 1)
                        if n < 6:
                            mm4(bk[d][1], dlb(d, 4), dlb(d, 0))
                        mm4(bk[d][2], dlb(d, 0), dlb(d, 4)).then_inc(dl_p2[d], 1)
                for d in range(2):
                    A, Bk, C, E = bk[d]
                    tk = slice(tile_at(d, s) * P, tile_at(d, s) * P + P)
                    for h in range(HEADS):
                        c = slice(h * P, (h + 1) * P)
                        pe.matmul(Bk[:, c], QT[:, h, tk], SD[:, q, 4 * d + h, :], start=True, stop=True)
                    pe.wait_ge(dl_xt[d], 6 * s + 6)
                    pe.wait_ge(dl_r[d], s + 1)
                    mm4(A, dlb(d, 4), dlb(d, 2)).then_inc(dl_tr[d], 1)
                for d in range(2):
                    A, Bk, C, E = bk[d]
                    pe.wait_ge(dl_vn[d], s + 1)
                    mm4(C, dlb(d, 1), dlb(d, 3)).then_inc(dl_o[d], 1)
                    pe.wait_ge(dl_vw[d], s + 1)
                    mm4(E, KTOK[:, tile_at(d, s), :], dlb(d, 2)).then_inc(dl_su[d], 1)
            for d in range(2):
                pe.wait_ge(dl_done[d], TILES)
            token_major("zb")
            pe.wait_ge(gate_used, 2 * TILES)
            out_of(("tm", "zb", TILES - 1))

            def y_transposes(l, head):
                for k in range(KT):
                    for part, tiles in enumerate((range(4), range(4, 5))):
                        b = begin(("yT", l, k, part))
                        for j, t in enumerate(tiles):
                            i = pe.transpose(b[:, j * P:(j + 1) * P], head(k, t), ident)
                        i.then_inc(unit_done, 1)
                out_of(("yT", l, KT - 1, 1))

            def out_proj(l):
                for n in range(2):
                    w, s = weights(("wout", l, n))
                    for t in range(TILES):
                        b = begin(("out", l, n, t))
                        for k in range(KT):
                            i = pe.matmul(b, HT[:, k, t * P:(t + 1) * P], w[:, k, :], start=(k == 0), stop=(k == KT - 1))
                        i.then_inc(unit_done, 1)
    
            y_transposes(0, lambda k, t: (YA, YB)[k // 4][:, t, (k % 4) * P:(k % 4 + 1) * P])
            out_proj(0)

            def pe_moe(l):
                if l == 0:
                    mod_rows("norm")
                for t in range(TILES + 1):
                    if t < TILES:
                        pe.wait_ge(h2_ready, TILES * l + t + 1)
                        for g in range(2):
                            b = begin(("h2T", l, t, g))
                            for q in range(4):
                                i = pe.transpose(b[:, q * P:(q + 1) * P], H2[:, t, (4 * g + q) * P:(4 * g + q + 1) * P], ident)
                            i.then_inc(unit_done, 1)
                    if t:
                        pe.wait_ge(router_loaded, 16 * 7 * (l + 1))
                        b = begin(("rt", l, t - 1))
                        out_of(("h2T", l, t - 1, 1))
                        for k in range(KT):
                            i = pe.matmul(b[:, 0:20], H2T[:, k, (t - 1) * P:t * P], RW[:, k, :], start=(k == 0), stop=(k == KT - 1))
                        i.then_inc(unit_done, 1)
                b = begin(("iota", l))
                pe.matmul(b[:, 0:P], IOTA[:, 48:49].to_broadcast([P, P]), ident, start=True, stop=True).then_inc(unit_done, 1)
                pe.wait_ge(hot_ready, l + 1)
                b = begin(("rank", l))
                for t in range(TILES):
                    for s in range(t + 1):
                        i = pe.matmul(b[:, 16 * t:16 * t + 16], ones if s < t else CST[:, C_UPI, :], HALL[:, 16 * s:16 * s + 16],
                                      start=(s == 0), stop=(s == t))
                i.then_inc(unit_done, 1)
                b = begin(("cnt", l))
                for t in range(TILES):
                    i = pe.matmul(b[:, 0:16], ones, HALL[:, 16 * t:16 * t + 16], start=(t == 0), stop=(t == TILES - 1))
                i.then_inc(unit_done, 1)
                b = begin(("tok", l))
                pe.wait_ge(slots_ready, l + 1)
                for n in range(2 * TILES):
                    i = pe.matmul(b[:, 0:ETILES], HOTL[:, n, :], HOTT[:, n, :], start=(n == 0), stop=(n == 2 * TILES - 1))
                i.then_inc(unit_done, 1)
                out_of(("tok", l))
                n0 = load_no[("moe", l)]

                def transposes(i, u, j, first=False):
                    pe.wait_ge(rows_gathered[l][u], 16 * j + 16)
                    if not first:
                        pe.wait_ge(xt_out, i + ETILES * l)
                    for k in range(KT):
                        m = pe.transpose(PS[:, k // 4, (k % 4) * P:(k % 4 + 1) * P], XG[:, u, k * P:(k + 1) * P], ident)
                    m.then_inc(xt_done, 1)

                def gate_up(i, j, u, first):
                    w = SLOTS[:, u, 0:4096].rearrange("p (m k c) -> p m k c", m=2, k=KT)
                    pe.wait_ge(slot_arrived[u], 48 * j + arrived_at[n0 + u])
                    pe.wait_ge(xt_out, i + (ETILES * l + 1))
                    if not first:
                        pe.wait_ge(hid_ready, i + (ETILES * l - 2))
                    for k in range(KT):
                        x = pe.matmul(PS[:, 2 + u, :].rearrange("p (m c) -> p m c", m=2), XGT[:, u, k, :], w[:, :, k, :],
                                      start=(k == 0), stop=(k == KT - 1))
                    x.then_inc(gu_done, 1)

                def down(i, u, first=False):
                    pe.wait_ge(hid_ready, i + (ETILES * l + 1))
                    for m in range(2):
                        x = pe.transpose(PS[:, 7, m * P:(m + 1) * P], HIDR[:, u, m * P:(m + 1) * P], ident)
                    x.then_inc(ht_done, 1)
                    pe.wait_ge(ht_out, i + (ETILES * l + 1))
                    if not first:
                        pe.wait_ge(ye_ready, i + ETILES * l)
                    w = SLOTS[:, u, 4096:6144].rearrange("p (k c) -> p k c", k=2)
                    for h in range(2):
                        for m in range(2):
                            x = pe.matmul(PS[:, 5 + h, :], HID[:, u, m, :], w[:, m, 512 * h:512 * h + 512],
                                          start=(m == 0), stop=(m == 1))
                    x.then_inc(down_done, 1)

                def group(j, first=False):
                    i = 3 * j
                    transposes(i, 0, j, first)
                    gate_up(i, j, 0, first)
                    transposes(i + 1, 1, j)
                    gate_up(i + 1, j, 1, first)
                    down(i, 0, first and not l)
                    transposes(i + 2, 2, j)
                    gate_up(i + 2, j, 2, first)
                    down(i + 1, 1)
                    down(i + 2, 2)

                group(0, True)
                pe.wait_ge(routed, l + 1)
                groups = pe.value_load(NG[0:1, 0:1], min_val=1, max_val=GROUPS)
                with pe.Fori(1, SURE) as j:
                    group(j)
                with pe.Fori(SURE, GROUPS) as j:
                    with pe.If(j < groups):
                        group(j)
                    with pe.Else():
                        for moved in (xt_done, gu_done, ht_done, down_done):
                            pe.wait_ge(moved, 3 * j + ETILES * l)
                            pe.sem_inc(moved, 3)

            pe_moe(0)

            pe.wait_ge(ye_ready, ETILES)
            mod_rows("moe")
            pe.wait_ge(ln_done, 2 * TILES)
            transposes_of_x(1)
            out_of(("hTctx", 1, 1))
            for n in (2, 0, 1):
                w, _ = weights(("qkv", n))
                for t in range(TILES):
                    b = begin(("qkv", n, t))
                    for k in range(KT):
                        i = pe.matmul(b, HT[:, k, t * P:(t + 1) * P], w[:, k, :], start=(k == 0), stop=(k == KT - 1))
                    i.then_inc(unit_done, 1)
            out_of(("qkv", 2, 0))
            for t in range(TILES + 1):
                if t < TILES:
                    pe.wait_ge(keys_ready, t + 1)
                else:
                    pe.wait_ge(attn_loaded, 64)
                for r in range(2):
                    b = begin(("kT", t, r))
                    for g in range(KVH):
                        a = 2 * HD * (KVH * t + g) + HD * (1 - r)
                        i = pe.transpose(b[:, g * P:(g + 1) * P], BCF[:, a:a + 2 * HD], ident)
                    i.then_inc(unit_done, 1)
            for t in range(TILES):
                for g in range(2):
                    b = begin(("qT", t, g))
                    pe.wait_ge(queries_ready, TILES * g + t + 1)
                    for q in range(4):
                        i = pe.transpose(b[:, q * P:(q + 1) * P], QR[:, t, 512 * g + q * P:512 * g + (q + 1) * P], ident)
                    i.then_inc(unit_done, 1)
            out_of(("qT", TILES - 1, 1))
            pe.wait_ge(masks_ready, 3)

            def scores(n):
                t, h = n // HC, n % HC
                local, cols = key_tiles(t)
                b = PS[:, n % 3, :]
                q = QTT[:, h // 2, t * P:(t + 1) * P]
                kk = KTT[h % 2][:, h // 4, :]
                if n >= 3:
                    pe.wait_ge(p_ready, n - 2)
                for j, kt in enumerate(cols):
                    o = b[:, j * P:(j + 1) * P]
                    m = {t - 1: 1, t + 1: 2}.get(kt) if t and kt < TILES else None
                    i = pe.matmul(o, q, kk[:, kt * P:(kt + 1) * P], start=True, stop=m is None)
                    if m is not None:
                        i = pe.matmul(o, MASKS[:, 0, :], MASKS[:, m, :], start=False, stop=True)
                i.then_inc(s_done, 1)

            def weight_transposes(n):
                pe.wait_ge(p_ready, n + 1)
                if n >= 3:
                    pe.wait_ge(pt_out, n - 2)
                for j in range(len(key_tiles(n // HC)[1])):
                    i = pe.transpose(PS[:, 3 + n % 3, j * P:(j + 1) * P], PB[:, n % 3, j * P:(j + 1) * P], ident)
                i.then_inc(pt_done, 1)

            def values(n):
                t, h = n // HC, n % HC
                cols = key_tiles(t)[1]
                pe.wait_ge(pt_out, n + 1)
                if h % 8 == 0 and n >= HC:
                    pe.wait_ge(o_ready, n // 8 - 1)
                for j, kt in enumerate(cols):
                    i = pe.matmul(PS[:, 6 + h // 8, HD * (h % 8):HD * (h % 8) + HD], PTB[:, n % 3, j * P:(j + 1) * P],
                                  V[:, kt, HD * (h // 4):HD * (h // 4) + HD], start=(j == 0), stop=(j == len(cols) - 1))
                i.then_inc(pv_done, 1)

            for n in range(STEPS + 3):
                if n < STEPS:
                    scores(n)
                if 2 <= n < STEPS + 2:
                    weight_transposes(n - 2)
                if n >= 3:
                    values(n - 3)
            pe.wait_ge(o_ready, STEPS // 8)
            y_transposes(1, lambda k, t: QR[:, t, k * P:(k + 1) * P])
            out_proj(1)
            pe_moe(1)


_OUTS = [((1, P, D), "float32"), ((1, LAT, D), "float32"), ((1, 1, 2, HEADS, P, P), "float32"),
         ((1, 1, 2, HEADS, P), "float32"), ((1, 1, 2, HEADS), "float32"), ((1, 1, 2, HEADS, P, P), "float32"),
         ((1, 1, KVH, P, HD), "float32"), ((1, 1, KVH, P, HD), "float32")]


def kernel(**inputs):
    import numpy as _np
    import concourse.bacc as _bacc
    from concourse import mybir as _mybir
    from concourse.bass_utils import run_bass_kernel_spmd as _run

    nc = _bacc.Bacc("TRN2", target_bir_lowering=False, num_devices=1)
    data = dict(inputs)
    data["consts"] = constants()
    data["ropes"] = rope_tables()
    data["iotas"] = iotas()
    arrays, ins = {}, {}
    for name, a in data.items():
        a = _np.ascontiguousarray(a)
        arrays[f"in_{name}"] = a
        ins[name] = nc.dram_tensor(f"in_{name}", a.shape, _mybir.dt.from_np(a.dtype), kind="ExternalInput").ap()
    outs = [nc.dram_tensor(f"out_{i}", s, _mybir.dt.from_np(_np.dtype(t)), kind="ExternalOutput").ap()
            for i, (s, t) in enumerate(_OUTS)]
    build(nc, ins, outs)
    r = _run(nc, [arrays], core_ids=[0])
    return tuple(r.results[0][f"out_{i}"] for i in range(len(_OUTS)))
```

```python
import concourse.bass as bass
from concourse import mybir
from contextlib import ExitStack
import numpy as np

D = 1024
P = 128
KT = D // P
TILES = 5
T = TILES * P
LAT = T - P
HEADS = 4
HW = HEADS * P
DEPTH = 2
EVEN_IN = 4128
NEXP, GRP, EPG, FF = 16, 4, 4, 256
HC, KVH, HD = 16, 4, 64
ALPHA = float((2 * DEPTH) ** 0.25)
LN_EPS = 1e-5
NEG = -1e30
SLOT = 6144
NSLOT = 3
ETILES = 27
GROUPS = ETILES // 3
SURE = -(-NEXP // 3)
SLOTS_E = ETILES * P
KSLOT = 0
BANKS = 8
SMALLS = 2440

C_ID, C_FLIP, C_UPI, C_LOI, C_ONES = range(5)
C_LEV = (5, 12)
N_CONST = 19


def constants():
    p, f = np.meshgrid(np.arange(P), np.arange(P), indexing="ij")
    m = np.zeros((N_CONST, P, P), np.float32)
    m[C_ID] = p == f
    m[C_FLIP] = p + f == P - 1
    m[C_UPI] = p <= f
    m[C_LOI] = p >= f
    m[C_ONES] = 1.0
    for n in range(7):
        b = 1 << n
        u = (p // (2 * b) == f // (2 * b)) & (p % (2 * b) < b) & (f % (2 * b) >= b)
        m[C_LEV[0] + n] = u
        m[C_LEV[1] + n] = u.T
    return np.ascontiguousarray(m.transpose(1, 0, 2))


def masks():
    p, f = np.meshgrid(np.arange(P), np.arange(P), indexing="ij")
    m = np.stack([p == f, np.where(p <= f, 0.0, NEG), np.where(p >= f, 0.0, NEG)], axis=1)
    return np.ascontiguousarray(m.astype(np.float32))


def iotas():
    m = np.zeros((P, 66), np.float32)
    m[0::32, 64] = 1.0
    m[16::32, 65] = 1.0
    m[:, 0:4] = np.arange(4)
    m[:, 8:13] = P * np.arange(TILES)
    m[:, 16:16 + ETILES] = np.arange(ETILES)
    m[:, 53:53 + GROUPS] = 3 * np.arange(GROUPS)
    m[:, 48:53] = np.arange(P)[:, None] + P * np.arange(TILES)
    return m


def rope_tables():
    half = HD // 4
    inv = 10000.0 ** (-np.arange(half, dtype=np.float32) / half)
    t = np.arange(LAT)
    out = np.zeros((2, LAT, 2, 2, half), np.float32)
    for a, pos in enumerate((t // 64, t % 64)):
        ang = pos.astype(np.float32)[:, None] * inv[None, :].astype(np.float32)
        out[0, :, a, :, :] = np.cos(ang)[:, None, :]
        out[1, :, a, 0, :] = -np.sin(ang)
        out[1, :, a, 1, :] = np.sin(ang)
    return np.ascontiguousarray(out.reshape(2, TILES - 1, P, HD).transpose(2, 0, 1, 3))


def tile_at(d, s):
    return s if d == 0 or s == 0 else TILES - s


def modulation_parts():
    order = [(l, c) for l in range(DEPTH) for c in range(12)]
    sizes = {"first": 4, "qa": 1, "ka": 1, "va": 1, "oa": 1, "vd": 1, "kd": 1, "qd": 1, "zb": 1, "out00": 3, "out01": 3,
             "moe": 0, "qkv2": 2, "qkv0": 2, "qkv1": 2}
    assert sum(sizes.values()) == len(order)
    out, a = {}, 0
    for name, n in sizes.items():
        out[name] = order[a:a + n]
        a += n
    return out


def fills(stage, step):
    part = modulation_parts().get(stage, [])
    if len(part) == 1:
        return {2: [("mod",) + part[0]], 3: [("modS",) + part[0]]}.get(step, [])
    if len(part) == 2:
        return [(("mod", "modS")[step % 2],) + part[step // 2]] if step < 4 else []
    if len(part) == 3:
        return ([("modS",) + part[step - 1]] if 1 <= step <= 3 else []) + ([("mod",) + part[step]] if step < 3 else [])
    return []


def with_transposes(items):
    return [x for item in items for x in [item] + ([("modT",) + item[1:]] if item[0] == "modS" and item[2] < 4 else [])]


def weight_loads():
    parts = modulation_parts()

    def mod(name, slots):
        return [(("mod",) + lc, slots[n % len(slots)]) for n, lc in enumerate(parts[name])]

    out = mod("first", (0, 1)) + [(("in", "gates"), 0)]
    for n, name in enumerate(("qa", "ka", "va", "oa", "vd", "kd", "qd", "zb")):
        out += [(("in", name), (n + 1) % 2)] + mod(name, (n % 2,))
    for n in range(2):
        out += [(("wout", 0, n), (n + 1) % 2)] + mod(f"out0{n}", (n % 2,))
    out += [(("moe", 0), 0)]
    out += mod("moe", (0, 1, 2))
    out += [(("qkv", 2), 1), (("qkv", 0), 2)] + mod("qkv2", (0,)) + [(("qkv", 1), 0)] + mod("qkv0", (1,))
    out += [(("wout", 1, 0), 1)] + mod("qkv1", (2,)) + [(("wout", 1, 1), 2)]
    out += [(("moe", 1), 0)]
    return out


def unit_order():
    u = [("cT",)]
    u += [("convT",)]

    def mod(name):
        out, part = [], modulation_parts()[name]
        for j, (l, c) in enumerate(part):
            out += [("mod",) + lc for lc in (part[0:2] if j == 0 else part[j + 1:j + 2])]
            out.append(("modS", l, c))
            if c < 4:
                out.append(("modT", l, c))
        return out

    def hT(l, tiles):
        return [("hT", l, t, g) for t in tiles for g in range(2)]

    def fm(name):
        out = []
        for m in range(4):
            out += [("fm", name, m, half) for half in range(2)] + with_transposes(fills(name, m))
        return out

    def tm(name, tiles=range(TILES)):
        return [x for t in tiles for x in [("tm", name, t)] + with_transposes(fills(name, t))]

    def out_rows(l):
        return [x for n in range(2) for t in range(TILES) 
                for x in [("out", l, n, t)] + with_transposes(fills(f"out{l}{n}", t))]

    u += mod("first") + hT(0, [0]) + [("hTlat", k) for k in range(KT)] + [("gatesT", 0), ("gatesT", 1), ("gates",)]
    u += fm("qa")
    u += [("cs", 0), ("cs", 1), ("ce",)]
    u += [(n, d, part) for n in ("rowf", "rowi") for d in range(2) for part in range(2)]
    u += fm("ka")
    u += [("mcol", 0), ("mcol", 1), ("mflip",), ("mvb",)]
    u += tm("va") + [("ktok", "a", t) for t in range(TILES)]
    u += tm("oa")
    u += fm("vd") + fm("kd") + [("vtok", t) for t in range(TILES)]
    u += [("ssq", "kd", m, half) for m in range(4) for half in range(2)]
    u += fm("qd") + [("ktok", "d", t) for t in range(TILES)]
    u += [("ssq", "qd", m, half) for m in range(4) for half in range(2)]
    u += tm("zb", range(0, 2)) + tm("zb", range(2, TILES))
    u += [("yT", 0, k, part) for k in range(KT) for part in range(2)]
    u += out_rows(0)

    def router(l):
        out = []
        for t in range(TILES + 1):
            if t < TILES:
                out += [("h2T", l, t, g) for g in range(2)]
            if t:
                out.append(("rt", l, t - 1))
        return out + [("iota", l), ("rank", l), ("tok", l)]

    u += router(0)
    u += mod("moe") + hT(1, range(TILES - 1)) + [("qkv", 2, 0)] + hT(1, [TILES - 1])
    u += [x for n in (2, 0, 1) for t in range(TILES)
          for x in ([("qkv", n, t)] if (n, t) != (2, 0) else []) + with_transposes(fills(f"qkv{n}", t))]
    u += [("kT", t, r) for t in range(TILES + 1) for r in range(2)]
    u += [("qT", t, g) for t in range(TILES) for g in range(2)]
    u += [("yT", 1, k, part) for k in range(KT) for part in range(2)]
    u += out_rows(1)
    u += router(1)
    return u


def build(nc, ins, outs):
    f32 = mybir.dt.float32
    ALU = mybir.AluOpType
    ACT = mybir.ActivationFunctionType
    AX = mybir.AxisListType

    ctx = ExitStack()
    with ctx:
        def sb(name, shape, dt=f32):
            return ctx.enter_context(nc.sbuf_tensor(name, shape, dt))

        def sem(name):
            return ctx.enter_context(nc.semaphore(name))

        X = sb("X", [P, TILES, D])
        HT = sb("HT", [P, KT, T])
        SLOTS = sb("SLOTS", [P, NSLOT, SLOT])
        CST = sb("CST", [P, N_CONST, P])
        MB = sb("MB", [P, 3, P], mybir.dt.bfloat16)
        Z = sb("Z", [P, 6 * 2560])
        QT, KTR = (Z[:, n * 2560:(n + 1) * 2560].rearrange("p (h t) -> p h t", h=HEADS) for n in range(2))
        KTOK, VTOK, YA, YB = (Z[:, n * 2560:(n + 1) * 2560].rearrange("p (t c) -> p t c", t=TILES) for n in range(2, 6))
        H2T = Z[:, 0:5120].rearrange("p (k t) -> p k t", k=KT)
        H2 = Z[:, 10240:15360].rearrange("p (t c) -> p t c", t=TILES)
        XG = Z[:, 0:3072].rearrange("p (b c) -> p b c", b=3)
        XGT = Z[:, 3072:6144].rearrange("p (b k c) -> p b k c", b=3, k=KT)
        YE = Z[:, 6144:9216].rearrange("p (b c) -> p b c", b=3)
        AU = Z[:, 9216:9984].rearrange("p (b c) -> p b c", b=3)
        HID = Z[:, 9984:10752].rearrange("p (b m c) -> p b m c", b=3, m=2)
        HIDR = Z[:, 10752:11520].rearrange("p (b c) -> p b c", b=3)
        YG = Z[:, 0:5120].rearrange("p (t c) -> p t c", t=TILES)
        BC = sb("BC", [P, 4, D])
        SMALL = sb("SMALL", [P, SMALLS])
        PS = ctx.enter_context(nc.psum_tensor("PS", [P, BANKS, 512], f32))

        at = [0]

        def small(n):
            a = at[0]
            at[0] += n
            assert at[0] <= SMALLS, at[0]
            return SMALL[:, a:a + n]

        ident, flip, ones = CST[:, C_ID, :], CST[:, C_FLIP, :], CST[:, C_ONES, :]
        SCR = SLOTS[:, 2, :]
        PRE = Z[:, 12800:15360].rearrange("p (m t) -> p m t", m=4)
        BCF = BC[:, :, :].rearrange("p a b -> p (a b)")
        SM = BCF[:, 0:2048].rearrange("p (s u v) -> p s u v", s=2, u=2 * HEADS)
        SD = BCF[:, 2048:4096].rearrange("p (s u v) -> p s u v", s=2, u=2 * HEADS)

        csil = small(KT * 32)
        MODT = [small(KT * 4).rearrange("p (k j) -> p k j", k=KT) for _ in range(DEPTH)]
        convw = small(36)
        MSUM = SLOTS[:, 0, 5120:6144].rearrange("p (b c) -> p b c", b=2)
        MROW = MSUM[0:2]
        CMB = SLOTS[:, 0, 5120:6144].rearrange("p (d c) -> p d c", d=2)
        GAIN = SLOTS[:, 1, 4608:5632].rearrange("p (g c) -> p g c", g=2)
        GATEST = Z[0:32, 7680:7680 + T]
        SG = [SLOTS[:, 0, 4608:5120], SLOTS[:, 1, 5632:6144]]
        SQ = SCR[:, 0:2560].rearrange("p (m t) -> p m t", m=4)
        NRM = SCR[:, 2560:5120].rearrange("p (m t) -> p m t", m=4)
        graw = small(TILES * 32).rearrange("p (t c) -> p t c", t=TILES)
        raw = small(2 * TILES * 16)
        raw4 = raw.rearrange("p (d s c) -> p d s c", d=2, s=TILES)
        gbias = small(32).rearrange("p (d c) -> p d c", d=2)
        alog = small(8)
        lcoef = small(16).rearrange("p (d c) -> p d c", d=2)
        zf = small(2 * TILES * 8)
        zabs = small(2 * TILES * 8)
        zexp = zln = zabs
        LF = small(2 * TILES * 8)
        CS = small(2 * TILES * 8)
        CE = small(2 * TILES * 8)
        MC = small(2 * TILES * 4)
        rev = small(TILES * 4)
        MVB = small(56)
        MV = small(14)
        MEX = small(56)
        M0 = small(2)
        BETA = small(2 * TILES * 4)
        ARG = small(7 * 40).rearrange("p (n c) -> p n c", n=7)
        EX = small(7 * 40).rearrange("p (n c) -> p n c", n=7)
        WI, EN, WE, DC, EG, EE, ED = range(7)
        RV = small(2 * 40).rearrange("p (n c) -> p n c", n=2)
        CB = small(2 * 40).rearrange("p (n c) -> p n c", n=2)
        NS = small(16).rearrange("p (s u) -> p s u", s=2)
        t4 = small(8)
        t4b = small(8)
        st20 = small(20)
        st20b = small(20)
        half = small(20)
        rstd = small(20)
        bnst = ARG[:, 0:2, :].rearrange("p n c -> p (n c)")[:, 0:TILES * 12].rearrange("p (t s c) -> p t s c", t=TILES, s=2)
        bnag = ARG[:, 2, 0:TILES * 2].rearrange("p (t c) -> p t c", t=TILES)
        lnr = small(TILES)
        lnb = small(TILES)
        eps = small(2)

        def v4(x):
            return x.rearrange("p (d s h) -> p d s h", d=2, s=TILES)

        def v8(x):
            return x.rearrange("p (d s h) -> p d s h", d=2, s=TILES)

        def heads(x):
            return x.rearrange("p (h v) -> p h v", h=HEADS)

        def col(x, n):
            return x.unsqueeze(2).to_broadcast([P, HEADS, n])

        ROWF = SCR[0:4, 0:2 * T].rearrange("p (d t) -> p d t", d=2)
        ROWI = SCR[0:4, 2 * T:4 * T].rearrange("p (d t) -> p d t", d=2)
        MR = SCR[0:4, 4 * T:6 * T].rearrange("p (d t) -> p d t", d=2)
        cin = SCR[0:16, 0:P]
        convrow = SCR[0:36, P:2 * P]
        mask_in = SCR[:, 4 * P:7 * P].rearrange("p (n c) -> p n c", n=3)

        def mlb(d, n):
            return SCR[:, (4 * d + n) * 512:(4 * d + n + 1) * 512]

        def dlb(d, n):
            if n == 6:
                return CMB[:, d, :]
            return SCR[:, (6 * d + n) * 512:(6 * d + n + 1) * 512]

        def mask(c):
            return CST[:, c, :].unsqueeze(1).to_broadcast([P, HEADS, P])

        YO = [Z[:, 9216:9728], Z[:, 9728:10240]]
        BC2 = Z[:, 5120:9216].rearrange("p (r c) -> p r c", r=4)
        betaexp = small(40)
        mod_dram = nc.dram_tensor("mod_rows", [DEPTH, 2, 6 * D], f32).ap()
        ht = [0]
        HTF = HT[:, :, :].rearrange("p k t -> p (k t)")

        def routing(n):
            a = ht[0]
            ht[0] += n
            return HTF[:, a:a + n]

        LG = routing(TILES * 20).rearrange("p (t c) -> p t c", t=TILES)
        gmax, cmin, gsum, gw, vmax, vsec = (routing(TILES) for _ in range(6))
        cand, ghot, LE, hot1, hot2, LE2 = (routing(TILES * 4).rearrange("p (t c) -> p t c", t=TILES) for _ in range(6))
        gx = routing(TILES * 5)
        WSEL = routing(2 * TILES).rearrange("p (c t) -> p c t", c=2)
        HE = routing(2 * TILES * 16).rearrange("p (c t e) -> p c t e", c=2, t=TILES)
        HALL = routing(TILES * 16)
        RK = routing(2 * TILES * 16)
        rtmp = routing(TILES * 16)
        CNT = routing(16)
        OV, OVC, EBASE, OBASE = (routing(16) for _ in range(4))
        past = routing(TILES * 16)
        iota_row = routing(P)
        tile_at_slot = routing(2 * TILES)
        low = routing(2 * TILES)
        HOTT = routing(4 * TILES * ETILES).rearrange("p (n i) -> p n i", n=2 * TILES)
        WSLOT = routing(ETILES)
        HOTL = routing(2 * TILES * P).rearrange("p (n i) -> p n i", n=2 * TILES)
        zero16 = small(16)
        big = routing(2 * TILES * ETILES)
        slotf = routing(2 * TILES)
        eotf = routing(ETILES)
        i32 = mybir.dt.int32
        IDX = routing(2 * TILES).bitcast(i32).rearrange("p (c t) -> p c t", c=2)
        EOT = routing(ETILES).bitcast(i32)
        TOKI = routing(ETILES).bitcast(i32)
        ngf = routing(1)
        NG = routing(1).bitcast(i32)
        TOKSEL = routing(3).bitcast(i32)
        assert ht[0] <= 5120
        IOTA = small(66)
        tokgate = small(2)
        RW = raw.rearrange("p (k c) -> p k c", k=KT)
        RB = small(20)
        h2_dram = nc.dram_tensor("h2_rows", [T, D], f32).ap()
        yg_dram = nc.dram_tensor("expert_rows", [SLOTS_E, D], f32).ap()
        SINK = small(HC)

        QR = Z[:, 10240:15360].rearrange("p (t c) -> p t c", t=TILES)
        QTT = Z[:, 0:5120].rearrange("p (g t) -> p g t", g=HC // 2)
        V = Z[:, 5120:6656].rearrange("p (t c) -> p t c", t=TILES + 1)
        KTT = [Z[:, 6656:9728].rearrange("p (g t) -> p g t", g=KVH), SLOTS[:, KSLOT, 0:3072].rearrange("p (g t) -> p g t", g=KVH)]
        ROPE = Z[:, 9728:10240].rearrange("p (a t i) -> p a t i", a=2, t=TILES - 1)
        KEYS = 64 + 2 * HD * KVH * (TILES + 1)
        KD = BCF[:, HD:KEYS].rearrange("p (t g r i) -> p t g r i", t=TILES + 1, g=KVH, r=2)[:, :, :, 0, :]
        KZERO = BCF[:, 0:KEYS + HD].rearrange("p (n r i) -> p n r i", r=2, i=HD)[:, :, 0, :]
        RTMP = BC[:, 3, 512:1024]
        PB = HTF[:, 0:1536].rearrange("p (b c) -> p b c", b=3)
        PTB = HTF[:, 1536:3072].rearrange("p (b c) -> p b c", b=3)
        STEPS = TILES * HC
        NM = HTF[:, 3072:3072 + STEPS]
        RS = HTF[:, 3200:3200 + STEPS]
        ES = HTF[:, 3328:3328 + STEPS]

        MASKS = HTF[:, 3456:3456 + 8 * P // 2].bitcast(mybir.dt.bfloat16)
        BEFORE, AFTER, LAST = P, 3 * P, 5 * P

        def key_tiles(t):
            if t == 0:
                return [0], [0]
            local = list(range(max(1, t - 1), min(TILES - 1, t + 1) + 1))
            return local, local + [TILES]

        const_loaded = sem("const_loaded")
        x_loaded = sem("x_loaded")
        small_loaded = sem("small_loaded")
        state_loaded = sem("state_loaded")
        slot_arrived = [sem(f"slot{n}_arrived") for n in range(NSLOT)]
        unit_done = sem("unit_done")
        unit_out = sem("unit_out")
        mod_stored = [sem(f"mod_stored{n}") for n in range(2)]
        dve_order = sem("dve_order")
        pool_order = sem("pool_order")
        act_order = sem("act_order")
        gate_abs = sem("gate_abs")
        gate_ln = sem("gate_ln")
        gate_lf = sem("gate_lf")
        m_scanned = sem("m_scanned")
        mex_ready = sem("mex_ready")
        arg_ready = sem("arg_ready")
        exp_ready = sem("exp_ready")
        pool_const = sem("pool_const")

        def pair(name):
            return [sem(f"{name}{d}") for d in range(2)]

        ml_st, ml_db, ml_de, ml_sw, ml_vw, ml_u, ml_done = (
            pair("ml_" + n) for n in ("scores", "decay", "exp", "weights", "vw", "update", "done"))
        dl_kk, dl_db, dl_de, dl_at, dl_cm, dl_xt1, dl_x1t, dl_x1, dl_p1, dl_p1s, dl_p2, dl_x, dl_ks, dl_r, dl_tr, \
            dl_vn, dl_o, dl_vw, dl_su, dl_done = (
                pair("dl_" + n) for n in ("kk", "decay", "exp", "at", "cm", "xt1", "x1t", "x1", "p1", "p1s", "p2",
                                          "x", "ks", "r", "tr", "vn", "o", "vw", "su", "done"))
        ml_num, dl_num = pair("ml_num"), pair("dl_num")
        conv_done = sem("conv_done")
        sq_ready = sem("sq_ready")
        silu_done = sem("silu_done")
        normed = sem("normed")
        gate_used = sem("gate_used")
        var_ready = sem("var_ready")
        rstd_ready = sem("rstd_ready")
        gain_loaded = sem("gain_loaded")
        alog_exp = sem("alog_exp")
        dl_qd, dl_xt, dl_y = pair("dl_qd"), pair("dl_xt"), pair("dl_y")
        bc_loaded = sem("bc_loaded")
        bc2_loaded = sem("bc2_loaded")
        out_used = sem("out_used")
        ln_done = sem("ln_done")
        h2_scaled = sem("h2_scaled")
        h2_ready = sem("h2_ready")
        h2_stored = sem("h2_stored")
        router_loaded = sem("router_loaded")
        rows_cleared = sem("rows_cleared")
        route_arg = sem("route_arg")
        route_exp = sem("route_exp")
        hot_ready = sem("hot_ready")
        routed = sem("routed")
        tok_picked = sem("tok_picked")
        slots_ready = sem("slots_ready")
        slots_cast = sem("slots_cast")
        ht_done = sem("ht_done")
        ht_out = sem("ht_out")
        rows_gathered = [[sem(f"rows_gathered{l}_{n}") for n in range(3)] for l in range(DEPTH)]
        xt_done = sem("xt_done")
        xt_out = sem("xt_out")
        gu_done = sem("gu_done")
        silu_out = sem("silu_out")
        hid_ready = sem("hid_ready")
        down_done = sem("down_done")
        ye_ready = sem("ye_ready")
        ye2_ready = sem("ye2_ready")
        ln_shift = sem("ln_shift")
        ln_scaled = sem("ln_scaled")
        ln_gained = sem("ln_gained")
        ye_stored = [sem(f"ye_stored{n}") for n in range(3)]
        yg_gathered = [sem(f"yg_gathered{n}") for n in range(TILES)]
        states_stored = sem("states_stored")
        attn_loaded = sem("attn_loaded")
        caches_stored = sem("caches_stored")
        keys_ready = sem("keys_ready")
        queries_ready = sem("queries_ready")
        masks_ready = sem("masks_ready")
        s_done = sem("s_done")
        max_ready = sem("max_ready")
        p_ready = sem("p_ready")
        pt_done = sem("pt_done")
        pt_out = sem("pt_out")
        pv_done = sem("pv_done")
        sink_arg = sem("sink_arg")
        sink_exp = sem("sink_exp")
        o_ready = sem("o_ready")
        x_stored = sem("x_stored")

        loads = [item for item, _ in weight_loads()]
        load_no, slots = {}, []
        for item, slot in weight_loads():
            load_no[item] = len(slots)
            slots += [n % NSLOT for n in range(ETILES)] if item[0] == "moe" else [slot]
        item_of = {load_no[item]: item for item in loads}
        first_moe = load_no[("moe", 0)]

        def slot_of(n):
            return slots[n]

        def last_in_slot(n):
            return max(m for m in range(n) if slot_of(m) == slot_of(n))

        def dmas_of(item):
            return {"mod": 2, "moe": 3}.get(item[0], 1) if item != ("in", "gates") else 2

        arrived_at, count = {}, [0] * NSLOT
        for item in loads:
            for j in range(ETILES if item[0] == "moe" else 1):
                s = slot_of(load_no[item] + j)
                count[s] += 16 * dmas_of(item)
                arrived_at[load_no[item] + j] = count[s]

        units = unit_order()
        unit_no = {name: n for n, name in enumerate(units)}
        assert len(unit_no) == len(units)

        def last_unit(item):
            if item[0] == "mod":
                return item
            if item[0] == "wout":
                return ("out", item[1], item[2], TILES - 1)
            if item[0] == "qkv":
                return item + (TILES - 1,)
            if item[1] == "gates":
                return ("gatesT", 1)
            if item[1] in ("qa", "ka", "vd", "kd", "qd"):
                return ("fm", item[1], 3, 1)
            return ("tm", item[1], TILES - 1)

        assert slot_of(load_no["qkv", 1]) == KSLOT
        mod_parts = modulation_parts()
        rows_stored, stored = {}, [0, 0]
        for name, part in mod_parts.items():
            for _, c in part:
                stored[c % 2] += c >= 4
            for n in range(2):
                rows_stored[n, name] = stored[n]

        def slot_cols(n, k, cols):
            return SLOTS[:, slot_of(n), 0:k * cols].rearrange("p (k c) -> p k c", k=k)

        w_in = ins["w_in_even"][0].rearrange("(k p) n -> p k n", p=P)
        in_at = {"qa": 0, "ka": 512, "va": 1024, "oa": 1536, "qd": 2064, "kd": 2576, "vd": 3088, "zb": 3600}

        block = ctx.enter_context(nc.Block())

        @block.sync
        def _(sp):
            def load(item):
                n = load_no[item]
                if n >= 2:
                    m = last_in_slot(n)
                    if first_moe <= m < first_moe + ETILES:
                        sp.wait_ge(down_done, m - first_moe + 1)
                    else:
                        sp.wait_ge(unit_done, unit_no[last_unit(item_of[m])] + 1)
                s = slot_of(n)
                a = slot_arrived[s]
                kind = item[0]
                if kind == "mod":
                    _, l, c = item
                    w = ins["w_mod"][l].rearrange("(k p) n -> p k n", p=P)
                    sp.dma_start(slot_cols(n, KT, 512), w[:, :, c * 512:(c + 1) * 512]).then_inc(a, 16)
                    sp.dma_start(SLOTS[0:1, s, 4096:4608], ins["b_mod"][l:l + 1, c * 512:(c + 1) * 512]).then_inc(a, 16)
                elif item == ("in", "gates"):
                    dst = slot_cols(n, KT, 32)
                    sp.dma_start(dst[:, :, 0:16], w_in[:, :, 2048:2064]).then_inc(a, 16)
                    sp.dma_start(dst[:, :, 16:32], w_in[:, :, 4112:4128]).then_inc(a, 16)
                elif kind == "in":
                    c = in_at[item[1]]
                    sp.dma_start(slot_cols(n, KT, 512), w_in[:, :, c:c + 512]).then_inc(a, 16)
                elif kind == "qkv":
                    w = ins["w_qkv_odd"][0].rearrange("(k p) n -> p k n", p=P)
                    sp.dma_start(slot_cols(n, KT, 512), w[:, :, item[1] * 512:(item[1] + 1) * 512]).then_inc(a, 16)
                elif kind == "wout":
                    _, l, c = item
                    w = (ins["w_out_even"], ins["w_out_odd"])[l][0].rearrange("(k p) n -> p k n", p=P)
                    sp.dma_start(slot_cols(n, KT, 512), w[:, :, c * 512:(c + 1) * 512]).then_inc(a, 16)

            def load_router(l):
                sp.dma_start(RW[:, :, 0:4], ins["w_grp"][l].rearrange("(k p) c -> p k c", p=P)).then_inc(router_loaded, 16)
                for g in range(GRP):
                    sp.dma_start(RW[:, :, 4 + 4 * g:8 + 4 * g], ins["w_erouter"][l, g].rearrange("(k p) c -> p k c", p=P))\
                        .then_inc(router_loaded, 16)
                sp.dma_start(RB[:, 0:4], ins["b_grp"][l].partition_broadcast(P)).then_inc(router_loaded, 16)
                sp.dma_start(RB[:, 4:20], ins["b_erouter"][l].rearrange("g e -> (g e)").partition_broadcast(P))\
                    .then_inc(router_loaded, 16)

            for item in loads[:first_moe]:
                if item == ("in", "qd"):
                    sp.wait_ge(arg_ready, 1)
                    load_router(0)
                load(item)

            def sync_moe(l):
                n0 = load_no[("moe", l)]
                if l == 0:
                    sp.wait_ge(gate_used, 2 * TILES)
                for n in range(2):
                    sp.wait_ge(mod_stored[n], 16 * rows_stored[n, ("out01", "qkv1")[l]])
                weights = [ins[n][l] for n in ("w_gate", "w_up", "w_down")]

                def load_expert(u, e):
                    for m, w in enumerate(weights):
                        k = KT if m < 2 else 2
                        dst = SLOTS[:, u, 2048 * m:2048 * m + 2048].rearrange("p (k c) -> p k c", k=k)
                        sp.dma_start(dst, w[e].rearrange("o (k p) c -> p (o k) c", p=P))\
                            .then_inc(slot_arrived[u], 16)

                def store_rows(j, u):
                    i = 3 * j + u
                    sp.wait_ge(ye_ready, i + (ETILES * l + 1))
                    sp.wait_ge(ye2_ready, i + (ETILES * l + 1))
                    sp.dma_start(yg_dram[bass.ds(P * i, P), :], YE[:, u, :]).then_inc(ye_stored[u], 16)

                for u in range(3):
                    if l or u < 2:
                        sp.wait_ge(unit_done, unit_no[last_unit(item_of[last_in_slot(n0 + u)])] + 1)
                    if l and u == KSLOT:
                        sp.wait_ge(s_done, STEPS)
                    load_expert(u, slice(u, u + 1))
                sp.wait_ge(routed, l + 1)
                groups = sp.value_load(NG[0:1, 0:1], min_val=1, max_val=GROUPS)

                def load_next(j):
                    for u in range(3):
                        sp.wait_ge(down_done, 3 * j + (ETILES * l + u + 1))
                        e = sp.value_load(EOT[0:1, bass.ds(3 * j + (3 + u), 1)], min_val=0, max_val=NEXP - 1)
                        load_expert(u, bass.ds(e, 1))

                def store_group(j):
                    for u in range(3):
                        store_rows(j, u)

                def pass_over_stores(j):
                    for u in range(3):
                        sp.wait_ge(ye_stored[u], 16 * j + 16 * GROUPS * l)
                        sp.sem_inc(ye_stored[u], 16)

                with sp.Fori(0, SURE - 1) as j:
                    load_next(j)
                    store_group(j)
                with sp.Fori(SURE - 1, GROUPS - 1) as j:
                    with sp.If(j + 1 < groups):
                        load_next(j)
                    with sp.Else():
                        for u in range(3):
                            sp.wait_ge(slot_arrived[u], 48 * j + arrived_at[n0 + u])
                            sp.sem_inc(slot_arrived[u], 48)
                    with sp.If(j < groups):
                        store_group(j)
                    with sp.Else():
                        pass_over_stores(j)
                with sp.If(groups > GROUPS - 1):
                    store_group(GROUPS - 1)
                with sp.Else():
                    pass_over_stores(GROUPS - 1)

            sync_moe(0)
            for t in range(TILES):
                sp.wait_ge(yg_gathered[t], 32)
            load_router(1)
            for item in loads[loads.index(("moe", 0)) + 1:-1]:
                load(item)
            sync_moe(1)
            for t in range(TILES):
                sp.wait_ge(ln_done, 3 * TILES + t + 1)
                dst = outs[0][0] if t == 0 else outs[1][0, (t - 1) * P:t * P, :]
                sp.dma_start(dst, X[:, t, :]).then_inc(x_stored, 16)
            sp.wait_ge(x_stored, 16 * TILES)

        @block.gpsimd
        def _(pool):
            order = [0]

            def done(ins_, s=None):
                if s is None:
                    order[0] += 1
                    ins_.then_inc(pool_order, 1)
                    pool.wait_ge(pool_order, order[0])

            sl = small_loaded
            pool.dma_start(gbias[:, :, 0:8], ins["mlstm_gate_b"][0].rearrange("d t h -> (d t h)").partition_broadcast(P)
                           .rearrange("p (d c) -> p d c", d=2)).then_inc(sl, 16)
            pool.dma_start(gbias[:, :, 12:16], ins["delta_dt_bias"][0].rearrange("d h -> (d h)").partition_broadcast(P)
                           .rearrange("p (d c) -> p d c", d=2)).then_inc(sl, 16)
            pool.dma_start(alog, ins["delta_a_log"][0].rearrange("d h -> (d h)").partition_broadcast(P)).then_inc(sl, 16)
            pool.dma_start(M0[0:4, :], ins["state_mlstm_m"][0, 0].rearrange("d h -> h d"),
                           allow_slow_non_contiguous=True).then_inc(sl, 16)
            pool.memset(gbias[:, :, 8:12], 0.0).then_inc(pool_const, 1)
            pool.memset(half, -0.5).then_inc(pool_const, 1)
            pool.memset(eps[:, 0:1], P * 1e-6).then_inc(pool_const, 1)
            pool.memset(eps[:, 1:2], 1e-6).then_inc(pool_const, 1)
            pool.memset(lcoef, -1.0).then_inc(pool_const, 1)
            pool.memset(SM[:, 0], 0.0).then_inc(pool_const, 1)
            pool.memset(SD[:, 0], 0.0).then_inc(pool_const, 1)
            pool.memset(NS[:, 0], 0.0).then_inc(pool_const, 1)
            pool.memset(zero16, 0.0).then_inc(pool_const, 1)
            pool.dma_start(SM[:, 1], ins["state_mlstm_c"][0, 0].rearrange("d h k v -> k (d h) v")).then_inc(state_loaded, 16)
            pool.dma_start(SD[:, 1], ins["state_delta"][0, 0].rearrange("d h k v -> k (d h) v")).then_inc(state_loaded, 16)
            pool.dma_start(NS[:, 1], ins["state_mlstm_n"][0, 0].rearrange("d h k -> k (d h)"),
                           allow_slow_non_contiguous=True).then_inc(state_loaded, 16)

            pool.dma_start(GAIN[:, 0, :], ins["mlstm_norm_g"][0].partition_broadcast(P)).then_inc(gain_loaded, 16)
            pool.dma_start(GAIN[:, 1, :], ins["delta_norm_g"][0].partition_broadcast(P)).then_inc(gain_loaded, 16)
            for s in range(TILES):
                for d in range(2):
                    if s == 0 and d == 0:
                        pool.wait_ge(exp_ready, 1)
                        pool.wait_ge(unit_out, unit_no[("tm", "va", TILES - 1)] + 1)
                        pool.wait_ge(pool_const, 9)
                        spare = ETILES - 3 * SURE
                        pool.dma_start(yg_dram[3 * SURE * P:SLOTS_E, :].rearrange("(i p) c -> p i c", p=P),
                                       SD[:, 0].rearrange("p u v -> p (u v)").unsqueeze(1).to_broadcast([P, spare, D]))\
                            .then_inc(rows_cleared, 16)
                    if s:
                        pool.wait_ge(ml_u[d], s)
                    w = v4(EX[:, WE, :])[:, d, s, :]
                    pool.tensor_tensor(heads(mlb(d, 2)), heads(VTOK[:, tile_at(d, s), :]), col(w, P), ALU.mult)\
                        .then_inc(ml_vw[d], 1)
            pool.wait_ge(var_ready, 1)
            pool.tensor_tensor(rstd, st20, half, ALU.pow).then_inc(rstd_ready, 1)
            pool.wait_ge(rows_cleared, 16)
            for n in range(2):
                pool.wait_ge(mod_stored[n], 16 * rows_stored[n, "qd"])
            for s in range(TILES):
                for d in range(2):
                    at_ = dlb(d, 2)
                    pool.wait_ge(dl_at[d], s + 1)
                    lev = C_LEV[d]
                    pool.tensor_tensor(heads(dlb(d, 6)), heads(at_), mask(lev + 1), ALU.mult).then_inc(dl_cm[d], 1)
                for n in range(2, 7):
                    for d in range(2):
                        if n >= 3:
                            pool.wait_ge(dl_p1[d], 6 * s + n - 2)
                        else:
                            pool.wait_ge(dl_xt1[d], s + 1)
                        pool.tensor_tensor(heads(dlb(d, 5 + n % 2)), heads(dlb(d, 2)), mask(C_LEV[d] + n), ALU.mult)\
                            .then_inc(dl_cm[d], 1)
                for d in range(2):
                    pool.wait_ge(dl_vn[d], s + 1)
                    pool.tensor_tensor(heads(dlb(d, 2)), heads(dlb(d, 3)), col(v4(EX[:, EE, :])[:, d, s, :], P), ALU.mult)\
                        .then_inc(dl_vw[d], 1)
            pool.wait_ge(var_ready, 2)
            pool.tensor_tensor(rstd, st20, half, ALU.pow).then_inc(rstd_ready, 1)

            bc = [0]

            def load_bc(rows, dst=BC, loaded=bc_loaded):
                for j, r in enumerate(rows):
                    pool.dma_start(dst[:, j, :], r.partition_broadcast(P)).then_inc(loaded, 16)

            def roots(nth, tiles=range(TILES)):
                for t in tiles:
                    pool.wait_ge(var_ready, 3 + TILES * nth + t)
                    pool.tensor_tensor(lnr[:, t:t + 1], lnr[:, t:t + 1], half[:, 0:1], ALU.pow).then_inc(rstd_ready, 1)

            def residual_tiles(l):
                for it in range(TILES + 1):
                    if it < TILES:
                        roots(2 * l, [it])
                    if it:
                        t = it - 1
                        if t == 0:
                            pool.wait_ge(bc2_loaded, 64 * (l + 1))
                        pool.wait_ge(h2_scaled, TILES * l + t + 1)
                        pool.tensor_tensor(H2[:, t, :], H2[:, t, :], BC2[:, min(t, 1), :], ALU.add).then_inc(h2_ready, 1)

            def mod_row(l, v, m):
                return mod_dram[l, v, m * D:(m + 1) * D]

            for d in range(2):
                pool.wait_ge(dl_done[d], TILES)
            pool.dma_start(outs[2][0, 0].rearrange("d h k v -> k (d h) v"), SM[:, 0]).then_inc(states_stored, 16)
            pool.dma_start(outs[5][0, 0].rearrange("d h k v -> k (d h) v"), SD[:, 0]).then_inc(states_stored, 16)
            pool.dma_start(outs[3][0, 0].rearrange("d h k -> k (d h)"), NS[:, 0],
                           allow_slow_non_contiguous=True).then_inc(states_stored, 16)
            pool.dma_start(outs[4][0, 0].rearrange("d h -> h d"), MV[0:4, 1:14:7],
                           allow_slow_non_contiguous=True).then_inc(states_stored, 16)
            pool.wait_ge(states_stored, 64)
            for n in range(2):
                pool.wait_ge(mod_stored[n], 16 * rows_stored[n, "zb"])
            load_bc([mod_row(0, 0, 2), mod_row(0, 1, 2), ins["ln_g"][0, 0], ins["ln_b"][0, 0]])
            load_bc([mod_row(0, 0, 3), mod_row(0, 1, 3), mod_row(0, 0, 4), mod_row(0, 1, 4)], BC2, bc2_loaded)
            residual_tiles(0)

            def pool_moe(l):
                for t in range(TILES):
                    pool.wait_ge(h2_ready, TILES * l + t + 1)
                    pool.dma_start(h2_dram[t * P:(t + 1) * P, :], H2[:, t, :]).then_inc(h2_stored, 16)
                pool.wait_ge(ln_done, TILES * (2 * l + 1))
                load_bc([mod_row(l, 0, 5), mod_row(l, 1, 5), ins["ln_g"][l, 1], ins["ln_b"][l, 1]])
                pool.wait_ge(unit_out, unit_no[("tok", l)] + 1)
                pool.wait_ge(h2_stored, 16 * TILES * (l + 1))

                def gate(n):
                    pool.tensor_tensor(tokgate[:, n:n + 1], half[:, 0:1], half[:, 0:1], ALU.mult)

                def gather(j, u, first):
                    i = 3 * j + u
                    if not first:
                        pool.wait_ge(xt_done, i + (ETILES * l - 2))
                        gate(0)
                    pool.tensor_copy(TOKSEL[:, u:u + 1], TOKI[:, bass.ds(i, 1)]).then_inc(tok_picked, 1)
                    pool.wait_ge(tok_picked, i + (ETILES * l + 1))
                    gate(1)
                    pool.indirect_dma_start(XG[:, u, :], None, h2_dram,
                                            bass.IndirectOffsetOnAxis(ap=TOKSEL[:, u:u + 1], axis=0))\
                        .then_inc(rows_gathered[l][u], 16)

                for u in range(3):
                    gather(0, u, True)
                pool.wait_ge(routed, l + 1)
                groups = pool.value_load(NG[0:1, 0:1], min_val=1, max_val=GROUPS)
                with pool.Fori(1, SURE) as j:
                    for u in range(3):
                        gather(j, u, False)
                with pool.Fori(SURE, GROUPS) as j:
                    with pool.If(j < groups):
                        for u in range(3):
                            gather(j, u, False)
                    with pool.Else():
                        pool.wait_ge(tok_picked, 3 * j + ETILES * l)
                        pool.sem_inc(tok_picked, 3)
                pool.wait_ge(slots_cast, l + 1)
                for u in range(3):
                    pool.wait_ge(ye_stored[u], 16 * GROUPS * (l + 1))
                for c in range(2):
                    for t in range(TILES):
                        if c:
                            pool.wait_ge(yg_gathered[t], 32 * l + 16)
                        pool.indirect_dma_start(YG[:, t, :], None, yg_dram,
                                                bass.IndirectOffsetOnAxis(ap=IDX[:, c, t:t + 1], axis=0),
                                                compute_op=(ALU.bypass, ALU.add)[c]).then_inc(yg_gathered[t], 16)
                for it in range(TILES + 2):
                    if it < TILES:
                        roots(2 * l + 1, [it])
                    if it >= 2:
                        pool.wait_ge(ln_gained, TILES * l + it - 1)
                        pool.tensor_tensor(X[:, it - 2, :], X[:, it - 2, :], BC[:, 3, :], ALU.add).then_inc(ln_done, 1)

            pool_moe(0)

            pool.dma_start(ROPE, ins["ropes"]).then_inc(attn_loaded, 16)
            pool.dma_start(V[:, TILES, :].rearrange("p (g i) -> p g i", g=KVH), ins["cache_v"][0, 0].rearrange("g s i -> s g i"))\
                .then_inc(attn_loaded, 16)
            pool.dma_start(SINK, ins["attn_sink"][0].partition_broadcast(P)).then_inc(attn_loaded, 16)
            pool.wait_ge(ln_done, 2 * TILES)
            pool.dma_start(KD[:, TILES, :, :], ins["cache_k"][0, 0].rearrange("g s i -> s g i")).then_inc(attn_loaded, 16)
            pool.wait_ge(unit_out, unit_no[("qkv", 2, 0)] + 1)
            pool.dma_start(outs[6][0, 0].rearrange("g s i -> s g i"), KD[:, 0, :, :]).then_inc(caches_stored, 16)
            pool.dma_start(outs[7][0, 0].rearrange("g s i -> s g i"), V[:, 0, :].rearrange("p (g i) -> p g i", g=KVH))\
                .then_inc(caches_stored, 16)
            pool.wait_ge(caches_stored, 32)
            pool.wait_ge(unit_out, unit_no[("kT", TILES, 1)] + 1)
            pool.wait_ge(queries_ready, 2 * TILES)
            for n in range(2):
                pool.wait_ge(mod_stored[n], 16 * rows_stored[n, "qkv1"])
            load_bc([mod_row(1, 0, 2), mod_row(1, 1, 2), ins["ln_g"][1, 0], ins["ln_b"][1, 0]])
            pool.wait_ge(pv_done, STEPS)
            load_bc([mod_row(1, 0, 3), mod_row(1, 1, 3), mod_row(1, 0, 4), mod_row(1, 1, 4)], BC2, bc2_loaded)
            residual_tiles(1)
            pool_moe(1)

        @block.scalar
        def _(act):
            act.dma_start(CST[:, :, :], ins["consts"]).then_inc(const_loaded, 16)
            act.dma_start(cin[0:8, :], ins["c_ctx"].rearrange("(k p) -> k p", p=P)).then_inc(const_loaded, 16)
            act.dma_start(cin[8:16, :], ins["c"][0].rearrange("(k p) -> k p", p=P)).then_inc(const_loaded, 16)
            act.dma_start(convrow, ins["delta_conv_w"][0].rearrange("j (m p) -> (j m) p", p=P)).then_inc(const_loaded, 16)
            act.dma_start(IOTA, ins["iotas"]).then_inc(const_loaded, 16)
            act.dma_start(mask_in, ins["masks"]).then_inc(const_loaded, 16)
            act.dma_start(X[:, 0, :], ins["x_prompt"][0]).then_inc(x_loaded, 16)
            act.dma_start(X[:, 1:TILES, :], ins["x_sample"][0].rearrange("(t p) n -> p t n", p=P)).then_inc(x_loaded, 16)

            def take(name):
                n = unit_no[name]
                act.wait_ge(unit_done, n + 1)
                return PS[:, n % BANKS, :]

            b = take(("cT",))
            act.activation(csil.rearrange("p (k v r) -> p k v r", k=KT, v=2),
                           b[:, 0:16].rearrange("p (v k) -> p k v", v=2).unsqueeze(3).to_broadcast([P, KT, 2, 16]),
                           ACT.Silu).then_inc(unit_out, 1)
            b = take(("convT",))
            act.activation(convw, b[:, 0:36], ACT.Copy).then_inc(unit_out, 1)

            def mod_partial(l, c):
                b = take(("mod", l, c))
                if l or c >= 6:
                    act.wait_ge(mod_stored[c % 2], 16 * (4 * l + max(0, (c - 4) // 2)))
                act.activation(MSUM[:, c % 2, :], b, ACT.Copy).then_inc(unit_out, 1)

            def mod_sum(l, c):
                b = take(("modS", l, c))
                act.activation(MROW[:, c % 2, :], b[0:2, :], ACT.Copy).then_inc(unit_out, 1)
                if c < 4:
                    b = take(("modT", l, c))
                    dst = MODT[l][:, 4 * (c % 2):4 * (c % 2) + 4, 2 * (c // 2):2 * (c // 2) + 2]
                    act.activation(dst, b[:, 0:8].rearrange("p (q v) -> p q v", q=4), ACT.Copy,
                                   bias=float(c // 2)).then_inc(unit_out, 1)
                else:
                    act.wait_ge(unit_out, unit_no[("modS", l, c)] + 1)
                    act.dma_start(mod_dram[l, :, c * 512:(c + 1) * 512], MROW[:, c % 2, :]).then_inc(mod_stored[c % 2], 16)

            def fill(stage, step):
                for kind, l, c in fills(stage, step):
                    if kind == "mod":
                        mod_partial(l, c)
                    elif kind == "modS":
                        mod_sum(l, c)

            def mod_rows(name):
                part = mod_parts[name]
                for j, lc in enumerate(part):
                    for ahead in part[0:2] if j == 0 else part[j + 1:j + 2]:
                        mod_partial(*ahead)
                    mod_sum(*lc)

            def modulate(l, t):
                v = min(t, 1)
                for g in range(2):
                    b = take(("hT", l, t, g))
                    for q in range(4):
                        k = 4 * g + q
                        i = act.activation(HT[:, k, t * P:(t + 1) * P], b[:, q * P:(q + 1) * P], ACT.Identity,
                                           bias=MODT[l][:, k, v:v + 1], scale=MODT[l][:, k, 2 + v:3 + v])
                    i.then_inc(unit_out, 1)

            def feature_major(name, dst, scale=1.0, before=None):
                for m in range(4):
                    if before is not None:
                        before(m)
                    for h in range(2):
                        b = take(("fm", name, m, h))
                        act.activation(dst[:, m, 320 * h:320 * h + 320], b[:, 0:320], ACT.Copy, scale=scale)\
                            .then_inc(unit_out, 1)
                    fill(name, m)

            mod_rows("first")
            act.wait_ge(unit_out, unit_no[("modT", 0, 3)] + 1)
            modulate(0, 0)
            for k in range(KT):
                b = take(("hTlat", k))
                act.activation(HT[:, k, P:T], b, ACT.Identity, bias=MODT[0][:, k, 1:2], scale=MODT[0][:, k, 3:4])\
                    .then_inc(unit_out, 1)
            for h in range(2):
                b = take(("gatesT", h))
                act.activation(GATEST[:, 320 * h:320 * h + 320], b[0:32, 0:320], ACT.Copy).then_inc(unit_out, 1)
            b = take(("gates",))
            act.activation(graw, b[:, 0:32 * TILES].rearrange("p (t c) -> p t c", t=TILES), ACT.Copy).then_inc(unit_out, 1)
            act.wait_ge(gate_abs, 1)
            act.activation(zexp, zabs, ACT.Exp, scale=-1.0).then_inc(act_order, 1)
            act.wait_ge(act_order, 1)
            act.activation(zln, zexp, ACT.Ln, bias=1.0).then_inc(gate_ln, 1)
            act.activation(v4(betaexp), raw4[:, :, :, 8:12], ACT.Exp, scale=-1.0)
            act.activation(alog, alog, ACT.Exp).then_inc(alog_exp, 1)
            feature_major("qa", QT)
            for d in range(2):
                b = take(("cs", d))
                act.activation(CS[:, 40 * d:40 * d + 40], b[:, 0:40], ACT.Copy).then_inc(unit_out, 1)
            b = take(("ce",))
            act.activation(CE, b[:, 0:80], ACT.Copy).then_inc(unit_out, 1)
            for name, dst in (("rowf", ROWF), ("rowi", ROWI)):
                for d in range(2):
                    for part, (a, e) in enumerate(((0, 512), (512, T))):
                        b = take((name, d, part))
                        act.activation(dst[:, d, a:e], b[0:4, 0:e - a], ACT.Copy).then_inc(unit_out, 1)
            feature_major("ka", KTR, P ** -0.5)
            b = take(("mcol", 0))
            act.activation(MC[:, 0:20], b[:, 0:20], ACT.Copy).then_inc(unit_out, 1)
            b = take(("mcol", 1))
            act.activation(rev, b[:, 0:20], ACT.Copy).then_inc(unit_out, 1)
            b = take(("mflip",))
            act.activation(MC[:, 20:40], b[:, 0:20], ACT.Copy).then_inc(unit_out, 1)
            b = take(("mvb",))
            act.activation(MVB, b[:, 0:56], ACT.Copy).then_inc(unit_out, 1)
            act.wait_ge(arg_ready, 1)
            act.activation(EX[:, :, :], ARG[:, :, :], ACT.Exp).then_inc(exp_ready, 1)
            for t in range(TILES):
                b = take(("tm", "va", t))
                act.activation(VTOK[:, t, :], b, ACT.Copy).then_inc(unit_out, 1)
                fill("va", t)
            for t in range(TILES):
                b = take(("ktok", "a", t))
                act.activation(KTOK[:, t, :], b, ACT.Copy).then_inc(unit_out, 1)

            for s in range(TILES):
                for d in range(2):
                    act.wait_ge(ml_db[d], s + 1)
                    if s:
                        act.wait_ge(ml_sw[d], s)
                    for h in range(HEADS):
                        i = act.activation(mlb(d, 0)[:, h * P:(h + 1) * P], PS[:, 4 * d + 1, h * P:(h + 1) * P], ACT.Exp,
                                           bias=v4(CB[:, 0, :])[:, d, s, h:h + 1])
                    i.then_inc(ml_de[d], 1)

            def gate(name, func, used0, tiles=range(TILES)):
                for t in tiles:
                    b = take(("tm", name, t))
                    if t >= 2 or used0:
                        act.wait_ge(gate_used, used0 + t - 1)
                    act.activation(SG[t % 2], b, func).then_inc(unit_out, 1)
                    fill(name, t)

            gate("oa", ACT.Sigmoid, 0)

            def silu_conv(dst, first, m):
                act.wait_ge(conv_done, first + m + 1)
                act.activation(dst[:, m, :], dst[:, m, :], ACT.Silu).then_inc(silu_done, 1)

            def norms(name, dst, first, scale):
                for m in range(4):
                    act.wait_ge(silu_done, first + m + 1)
                    if name == "qd":
                        act.wait_ge(unit_out, unit_no[("ssq", "kd", 3, 1)] + 1)
                        act.wait_ge(normed, 4)
                    act.activation(SQ[:, m, :], dst[:, m, :], ACT.Square).then_inc(sq_ready, 1)
                for m in range(4):
                    for h in range(2):
                        b = take(("ssq", name, m, h))
                        act.activation(NRM[:, m, 320 * h:320 * h + 320], b[:, 0:320], ACT.Sqrt, scale=scale,
                                       bias=eps[:, 0:1] if name == "qd" else eps[:, 1:2]).then_inc(unit_out, 1)

            feature_major("vd", PRE)
            feature_major("kd", PRE, before=lambda m: silu_conv(QT, 0, m))
            for t in range(TILES):
                b = take(("vtok", t))
                act.activation(VTOK[:, t, :], b, ACT.Copy).then_inc(unit_out, 1)
            for m in range(4):
                silu_conv(KTR, 4, m)
            norms("kd", KTR, 4, 1.0)
            feature_major("qd", PRE)
            for t in range(TILES):
                b = take(("ktok", "d", t))
                act.activation(KTOK[:, t, :], b, ACT.Copy).then_inc(unit_out, 1)
            for m in range(4):
                silu_conv(QT, 8, m)
            norms("qd", QT, 8, float(P))
            act.wait_ge(gate_used, TILES)
            gate("zb", ACT.Silu, TILES, range(0, 2))

            for s in range(TILES):
                for d in range(2):
                    act.wait_ge(dl_db[d], s + 1)
                    if s:
                        act.wait_ge(dl_y[d], s)
                    for h in range(HEADS):
                        i = act.activation(dlb(d, 0)[:, h * P:(h + 1) * P], PS[:, 4 * d + 1, h * P:(h + 1) * P], ACT.Exp,
                                           bias=v4(CB[:, 1, :])[:, d, s, h:h + 1])
                    i.then_inc(dl_de[d], 1)
                for d in range(2):
                    act.wait_ge(dl_x1t[d], s + 1)
                    act.activation(dlb(d, 3), PS[:, 4 * d, :], ACT.Copy).then_inc(dl_x1[d], 1)
                for n in range(1, 7):
                    for d in range(2):
                        act.wait_ge(dl_p1[d], 6 * s + n)
                        act.activation(dlb(d, 0), PS[:, 4 * d, :], ACT.Copy).then_inc(dl_p1s[d], 1)
            gate("zb", ACT.Silu, TILES, range(2, TILES))
            for k in range(KT):
                for part, (a, e) in enumerate(((0, 512), (512, T))):
                    b = take(("yT", 0, k, part))
                    act.activation(HT[:, k, a:e], b[:, 0:e - a], ACT.Copy).then_inc(unit_out, 1)

            def out_rows(l):
                for n in range(2):
                    for t in range(TILES):
                        b = take(("out", l, n, t))
                        j = TILES * n + t
                        if j >= 2 or l:
                            act.wait_ge(out_used, 2 * TILES * l + j - 1)
                        act.activation(YO[j % 2], b, ACT.Copy).then_inc(unit_out, 1)
                        fill(f"out{l}{n}", t)

            out_rows(0)

            def act_moe(l):
                for t in range(TILES + 1):
                    if t < TILES:
                        for g in range(2):
                            b = take(("h2T", l, t, g))
                            act.activation(H2T[:, 4 * g:4 * g + 4, t * P:(t + 1) * P], b.rearrange("p (k c) -> p k c", k=4), ACT.Copy)\
                                .then_inc(unit_out, 1)
                    if t:
                        b = take(("rt", l, t - 1))
                        act.activation(LG[:, t - 1, :], b[:, 0:20], ACT.Copy).then_inc(unit_out, 1)
                b = take(("iota", l))
                act.activation(iota_row, b[:, 0:P], ACT.Copy).then_inc(unit_out, 1)
                act.wait_ge(route_arg, l + 1)
                act.activation(gx, gx, ACT.Exp).then_inc(route_exp, 1)
                b = take(("rank", l))
                act.activation(RK, b[:, 0:160], ACT.Copy).then_inc(unit_out, 1)

                def rows_and_silu(i, u):
                    act.wait_ge(xt_done, i + (ETILES * l + 1))
                    for h in range(2):
                        a = act.activation(XGT[:, u, 4 * h:4 * h + 4, :], PS[:, h, :].rearrange("p (k c) -> p k c", k=4), ACT.Copy)
                    a.then_inc(xt_out, 1)
                    act.wait_ge(gu_done, i + (ETILES * l + 1))
                    act.activation(AU[:, u, :], PS[:, 2 + u, 0:256], ACT.Silu).then_inc(silu_out, 1)

                def hidden(i, u):
                    act.wait_ge(ht_done, i + (ETILES * l + 1))
                    act.activation(HID[:, u], PS[:, 7, 0:256].rearrange("p (m c) -> p m c", m=2), ACT.Copy).then_inc(ht_out, 1)

                def rows_out(i, j, u, first):
                    if not first:
                        act.wait_ge(ye_stored[u], 16 * j + 16 * GROUPS * l)
                    act.wait_ge(down_done, i + (ETILES * l + 1))
                    act.activation(YE[:, u, 512:1024], PS[:, 6, :], ACT.Copy, scale=WSLOT[:, bass.ds(i, 1)]).then_inc(ye2_ready, 1)

                def group(j, first=False):
                    rows_and_silu(3 * j, 0)
                    rows_and_silu(3 * j + 1, 1)
                    hidden(3 * j, 0)
                    rows_out(3 * j, j, 0, first)
                    rows_and_silu(3 * j + 2, 2)
                    hidden(3 * j + 1, 1)
                    rows_out(3 * j + 1, j, 1, first)
                    hidden(3 * j + 2, 2)
                    rows_out(3 * j + 2, j, 2, first)

                act.wait_ge(unit_out, unit_no[("tok", l)] + 1)
                act.wait_ge(routed, l + 1)
                groups = act.value_load(NG[0:1, 0:1], min_val=1, max_val=GROUPS)
                group(0, True)
                with act.Fori(1, SURE) as j:
                    group(j)
                with act.Fori(SURE, GROUPS) as j:
                    with act.If(j < groups):
                        group(j)
                    with act.Else():
                        for moved in (xt_out, silu_out, ht_out, ye2_ready):
                            act.wait_ge(moved, 3 * j + ETILES * l)
                            act.sem_inc(moved, 3)

            def scale_rows(l, t):
                act.wait_ge(ln_shift, TILES * l + t + 1)
                act.activation(X[:, t, :], X[:, t, :], ACT.Identity, scale=lnr[:, t:t + 1], bias=lnb[:, t:t + 1])\
                    .then_inc(ln_scaled, 1)

            act_moe(0)

            mod_rows("moe")
            act.wait_ge(unit_out, unit_no[("modT", 1, 3)] + 1)
            for it in range(TILES + 1):
                if it < TILES:
                    scale_rows(0, it)
                if it == 2:
                    for t in range(TILES):
                        act.wait_ge(yg_gathered[t], 32)
                if it >= 2:
                    modulate(1, it - 2)

            def take_qkv(n, t):
                b = take(("qkv", n, t))
                if n < 2:
                    act.activation(QR[:, t, 512 * n:512 * n + 512], b, ACT.Copy, scale=HD ** -0.5).then_inc(unit_out, 1)
                else:
                    act.activation(KD[:, t, :, :], b[:, 0:256].rearrange("p (g i) -> p g i", g=KVH), ACT.Copy)
                    act.activation(V[:, t, :], b[:, 256:512], ACT.Copy).then_inc(unit_out, 1)

            act.wait_ge(ln_done, 2 * TILES)
            take_qkv(2, 0)
            modulate(1, TILES - 1)
            for n in (2, 0, 1):
                for t in range(TILES):
                    if (n, t) != (2, 0):
                        take_qkv(n, t)
                    fill(f"qkv{n}", t)
            for t in range(TILES + 1):
                for r in range(2):
                    b = take(("kT", t, r))
                    act.activation(KTT[r][:, :, t * P:(t + 1) * P], b.rearrange("p (g c) -> p g c", g=KVH), ACT.Copy)\
                        .then_inc(unit_out, 1)
            for t in range(TILES):
                for g in range(2):
                    b = take(("qT", t, g))
                    act.activation(QTT[:, 4 * g:4 * g + 4, t * P:(t + 1) * P], b.rearrange("p (g c) -> p g c", g=4), ACT.Copy)\
                        .then_inc(unit_out, 1)

            def exponentials(n):
                w = P * len(key_tiles(n // HC)[1])
                act.wait_ge(max_ready, n + 1)
                if n >= 3:
                    act.wait_ge(pt_done, n - 2)
                act.activation(PB[:, n % 3, 0:w], PS[:, n % 3, 0:w], ACT.Exp, bias=NM[:, n:n + 1],
                               accum_out=RS[:, n:n + 1]).then_inc(p_ready, 1)

            def take_transposed(n):
                w = P * len(key_tiles(n // HC)[1])
                act.wait_ge(pt_done, n + 1)
                if n >= 3:
                    act.wait_ge(pv_done, n - 2)
                act.activation(PTB[:, n % 3, 0:w], PS[:, 3 + n % 3, 0:w], ACT.Copy).then_inc(pt_out, 1)

            for n in range(STEPS + 2):
                if n < STEPS:
                    exponentials(n)
                if n >= 2:
                    take_transposed(n - 2)
                if n % 8 == 1 and n > 8:
                    g = (n - 8) // 8
                    act.wait_ge(sink_arg, g + 1)
                    act.activation(ES[:, 8 * g:8 * g + 8], ES[:, 8 * g:8 * g + 8], ACT.Exp).then_inc(sink_exp, 1)
            for k in range(KT):
                for part, (a, e) in enumerate(((0, 512), (512, T))):
                    b = take(("yT", 1, k, part))
                    act.activation(HT[:, k, a:e], b[:, 0:e - a], ACT.Copy).then_inc(unit_out, 1)
            out_rows(1)
            act_moe(1)
            for t in range(TILES):
                scale_rows(1, t)

        @block.vector
        def _(dve):
            count = {}

            def done(i, s=dve_order):
                count[s.name] = count.get(s.name, 0) + 1
                i.then_inc(s, 1)
                dve.wait_ge(s, count[s.name])

            tt, ts, stt = dve.tensor_tensor, dve.tensor_scalar, dve.scalar_tensor_tensor

            dve.wait_ge(const_loaded, 96)
            done(dve.tensor_copy(MB[:, :, :], mask_in), masks_ready)
            dve.wait_ge(unit_out, unit_no[("gates",)] + 1)
            dve.wait_ge(small_loaded, 64)
            dve.wait_ge(pool_const, 9)
            for d in range(2):
                for s in range(TILES):
                    t = tile_at(d, s)
                    dve.tensor_copy(raw4[:, d, s, 0:8], graw[:, t, 8 * d:8 * d + 8])
                    done(dve.tensor_copy(raw4[:, d, s, 8:16].rearrange("p (g c) -> p g c", g=2),
                                         graw[:, t, 16:32].rearrange("p (g e c) -> p g e c", g=2, e=2)[:, :, d, :]))
            for s in range(TILES):
                done(tt(raw4[:, :, s, :], raw4[:, :, s, :], gbias[:, :, :], ALU.add))
            z = v8(zf)
            done(ts(z[:, :, :, 0:4], raw4[:, :, :, 4:8], -1.0, None, ALU.mult))
            done(dve.tensor_copy(z[:, :, :, 4:8], raw4[:, :, :, 12:16]))
            done(stt(zabs, zf, -1.0, zf, ALU.mult, ALU.max), gate_abs)
            done(ts(zf, zf, 0.0, None, ALU.max))
            dve.wait_ge(gate_ln, 1)
            done(tt(LF, zf, zln, ALU.add))
            done(ts(v8(LF)[:, :, :, 0:4], v8(LF)[:, :, :, 0:4], -1.0, None, ALU.mult))
            dve.wait_ge(alog_exp, 1)
            for s in range(TILES):
                done(stt(v8(LF)[:, :, s, 4:8], v8(LF)[:, :, s, 4:8], -1.0, alog.rearrange("p (d h) -> p d h", d=2),
                         ALU.mult, ALU.mult))
            done(ts(v4(BETA), v4(betaexp), 1.0, None, ALU.add))
            done(dve.reciprocal(BETA, BETA), gate_lf)
            dve.wait_ge(unit_out, unit_no[("rowi", 1, 1)] + 1)
            for d in range(2):
                done(dve.tensor_tensor_scan(MR[:, d, 0:P], ROWF[:, d, 0:P], ROWI[:, d, 0:P], 0.0, ALU.add, ALU.max))
                done(dve.tensor_tensor_scan(MR[:, d, P:T], ROWF[:, d, P:T], ROWI[:, d, P:T], M0[0:4, d:d + 1], ALU.add,
                                            ALU.max), m_scanned)
            mv = MV.rearrange("p (d s) -> p d s", d=2)
            done(dve.memset(mv[0:4, :, 0:1], 0.0))
            done(dve.tensor_copy(mv[0:4, :, 1:2], MR[:, :, P - 1:P]))
            done(dve.tensor_copy(mv[0:4, :, 2:3], M0[0:4, :].unsqueeze(2)))
            done(dve.tensor_copy(mv[0:4, :, 3:7], MR[:, :, 2 * P - 1:T:P]))
            done(tt(MEX[0:4, :].rearrange("p (n h) -> p n h", h=4), MV[0:4, :].unsqueeze(2).to_broadcast([4, 14, 4]),
                    CST[0:4, C_ID, 0:4].unsqueeze(1).to_broadcast([4, 14, 4]), ALU.mult), mex_ready)
            dve.wait_ge(unit_out, unit_no[("mvb",)] + 1)
            cs, ce, m = v8(CS), v8(CE), v4(MC)
            mb = MVB.rearrange("p (d n h) -> p d n h", d=2, n=7)
            B, G, BE, GE = cs[:, :, :, 0:4], cs[:, :, :, 4:8], ce[:, :, :, 0:4], ce[:, :, :, 4:8]
            arg = [v4(ARG[:, n, :]) for n in range(7)]
            done(tt(v4(CB[:, 0, :]), raw4[:, :, :, 0:4], B, ALU.subtract))
            done(ts(v4(CB[:, 1, :]), G, -1.0, None, ALU.mult))
            done(tt(v4(RV[:, 0, :]), B, m, ALU.subtract))
            done(dve.tensor_copy(v4(RV[:, 1, :]), G))
            done(ts(arg[EN], m, -1.0, None, ALU.mult))
            done(tt(arg[WE], BE, v4(CB[:, 0, :]), ALU.add))
            done(dve.tensor_copy(arg[WI], v4(RV[:, 0, :])))
            done(dve.tensor_copy(arg[DC], BE))
            for s in range(TILES):
                before, after = (0, 1) if s == 0 else (s + 1, s + 2)
                done(tt(arg[WI][:, :, s, :], arg[WI][:, :, s, :], mb[:, :, before, :], ALU.add))
                done(tt(arg[DC][:, :, s, :], arg[DC][:, :, s, :], mb[:, :, before, :], ALU.add))
                done(tt(arg[DC][:, :, s, :], arg[DC][:, :, s, :], mb[:, :, after, :], ALU.subtract))
                done(tt(arg[WE][:, :, s, :], arg[WE][:, :, s, :], mb[:, :, after, :], ALU.subtract))
            done(dve.tensor_copy(arg[EG], G))
            done(tt(arg[EE], GE, G, ALU.subtract))
            done(dve.tensor_copy(arg[ED], GE), arg_ready)

            dve.wait_ge(exp_ready, 1)
            dve.wait_ge(state_loaded, 48)
            dve.wait_ge(unit_out, unit_no[("ktok", "a", TILES - 1)] + 1)

            def ex(n, d, s):
                return v4(EX[:, n, :])[:, d, s, :]

            for s in range(TILES):
                q = 1 if s else 0
                for d in range(2):
                    dve.wait_ge(ml_de[d], s + 1)
                    dve.wait_ge(ml_st[d], s + 1)
                    done(tt(mlb(d, 1), mlb(d, 0), PS[:, 4 * d, :], ALU.mult), ml_sw[d])
                for d in range(2):
                    A, Bk, C, E = (PS[:, 4 * d + n, :] for n in range(4))
                    dve.wait_ge(ml_u[d], s + 1)
                    w = mlb(d, 3)
                    done(tt(heads(w), heads(Bk), col(ex(WI, d, s), P), ALU.mult))
                    done(tt(w, w, A, ALU.add), ml_num[d])
                    c = SM[:, q, 4 * d:4 * d + 4, :]
                    nn = NS[:, q, 4 * d:4 * d + 4]
                    done(tt(c, c, col(ex(DC, d, s), P), ALU.mult))
                    done(tt(c, c, heads(C), ALU.add))
                    done(tt(nn, nn, ex(DC, d, s), ALU.mult))
                    done(tt(nn, nn, E[:, 8:12], ALU.add))
                    done(tt(t4[:, 0:4], E[:, 4:8], ex(WI, d, s), ALU.mult))
                    done(tt(t4[:, 0:4], t4[:, 0:4], E[:, 0:4], ALU.add), ml_done[d])
                    done(stt(t4b[:, 0:4], t4[:, 0:4], -1.0, t4[:, 0:4], ALU.mult, ALU.max))
                    done(tt(t4b[:, 0:4], t4b[:, 0:4], ex(EN, d, s), ALU.max))
                    done(dve.reciprocal(t4[:, 0:4], t4b[:, 0:4]))
                    y = YA[:, tile_at(d, s), :]
                    if s > 2 or (s == 0 and d == 1):
                        done(tt(heads(w), heads(w), col(t4[:, 0:4], P), ALU.mult))
                        done(tt(y, y, w, ALU.add))
                    else:
                        done(tt(heads(y), heads(w), col(t4[:, 0:4], P), ALU.mult))

            def sums(y, dst, sq=None):
                for t in range(TILES):
                    v = heads(y[:, t, :])
                    if sq is not None:
                        done(tt(sq, y[:, t, :], y[:, t, :], ALU.mult))
                        v = heads(sq)
                    done(dve.tensor_reduce(dst[:, 4 * t:4 * t + 4], v, AX.X, ALU.add))

            sums(YA, st20)
            done(ts(st20, st20, 1.0 / P, None, ALU.mult))
            for t in range(TILES):
                done(tt(heads(YA[:, t, :]), heads(YA[:, t, :]), col(st20[:, 4 * t:4 * t + 4], P), ALU.subtract))
            sums(YA, st20b, mlb(0, 0))
            done(ts(st20, st20b, 1.0 / P, LN_EPS, ALU.mult, ALU.add), var_ready)

            def gated(y, g, first):
                for t in range(TILES):
                    v = y[:, t, :]
                    done(tt(heads(v), heads(v), col(rstd[:, 4 * t:4 * t + 4], P), ALU.mult))
                    done(tt(v, v, GAIN[:, g, :], ALU.mult))
                    dve.wait_ge(unit_out, unit_no[("tm", ("oa", "zb")[g], t)] + 1)
                    done(tt(v, v, SG[t % 2], ALU.mult), gate_used)

            dve.wait_ge(rstd_ready, 1)
            dve.wait_ge(gain_loaded, 32)
            gated(YA, 0, 0)

            def conv(name, dst, g, first):
                for m in range(4):
                    dve.wait_ge(unit_out, unit_no[("fm", name, m, 1)] + 1)
                    c = 4 * g + m
                    o, i = dst[:, m, :], PRE[:, m, :]
                    done(ts(o, i, convw[:, 12 + c:13 + c], None, ALU.mult))
                    for a, e in ((0, P), (P, T)):
                        done(stt(o[:, a + 1:e], i[:, a:e - 1], convw[:, c:c + 1], o[:, a + 1:e], ALU.mult, ALU.add))
                    done(stt(o[:, 0:P - 1], i[:, 1:P], convw[:, 24 + c:25 + c], o[:, 0:P - 1], ALU.mult, ALU.add))
                    done(stt(o[:, P:T - 1], i[:, P + 1:T], convw[:, 24 + c:25 + c], o[:, P:T - 1], ALU.mult, ALU.add),
                         conv_done)

            def unit_norm(name, dst):
                for m in range(4):
                    dve.wait_ge(unit_out, unit_no[("ssq", name, m, 1)] + 1)
                    done(dve.reciprocal(NRM[:, m, :], NRM[:, m, :]))
                    done(tt(dst[:, m, :], dst[:, m, :], NRM[:, m, :], ALU.mult), normed)

            conv("vd", QT, 2, 0)
            conv("kd", KTR, 1, 4)
            unit_norm("kd", KTR)
            dve.wait_ge(unit_out, unit_no[("vtok", TILES - 1)] + 1)
            conv("qd", QT, 0, 8)
            unit_norm("qd", QT)

            dve.wait_ge(unit_out, unit_no[("ktok", "d", TILES - 1)] + 1)
            for s in range(TILES):
                q = 1 if s else 0
                bk = [[PS[:, 4 * d + n, :] for n in range(4)] for d in range(2)]
                for d in range(2):
                    dve.wait_ge(dl_de[d], s + 1)
                    dve.wait_ge(dl_kk[d], s + 1)
                    done(tt(dlb(d, 1), dlb(d, 0), bk[d][2], ALU.mult), dl_qd[d])
                    done(tt(dlb(d, 2), dlb(d, 0), bk[d][0], ALU.mult))
                    done(tt(heads(dlb(d, 2)), heads(dlb(d, 2)), col(v4(BETA)[:, d, s, :], P), ALU.mult), dl_at[d])
                    done(tt(heads(dlb(d, 5)), heads(dlb(d, 2)), mask(C_LEV[d]), ALU.mult))
                    done(tt(heads(dlb(d, 4)), mask(C_ID), heads(dlb(d, 5)), ALU.subtract), dl_xt1[d])
                for n in range(1, 7):
                    for d in range(2):
                        dve.wait_ge(dl_p2[d], 6 * s + n)
                        if n < 6:
                            done(tt(dlb(d, 3), dlb(d, 3), bk[d][1], ALU.subtract), dl_x[d])
                        done(tt(dlb(d, 4), dlb(d, 4), bk[d][2], ALU.subtract), dl_xt[d])
                for d in range(2):
                    r = dlb(d, 2)
                    dve.wait_ge(dl_ks[d], s + 1)
                    dve.wait_ge(dl_cm[d], 6 * s + 6)
                    done(tt(heads(r), heads(bk[d][3]), col(ex(EG, d, s), P), ALU.mult))
                    done(tt(r, VTOK[:, tile_at(d, s), :], r, ALU.subtract), dl_r[d])
                for d in range(2):
                    dve.wait_ge(dl_tr[d], s + 1)
                    done(tt(heads(dlb(d, 3)), heads(bk[d][0]), col(v4(BETA)[:, d, s, :], P), ALU.mult), dl_vn[d])
                for d in range(2):
                    c = SD[:, q, 4 * d:4 * d + 4, :]
                    done(tt(heads(dlb(d, 0)), heads(bk[d][1]), col(ex(EG, d, s), P), ALU.mult))
                    done(tt(c, c, col(ex(ED, d, s), P), ALU.mult))
                for d in range(2):
                    w = dlb(d, 0)
                    y = YB[:, tile_at(d, s), :]
                    dve.wait_ge(dl_o[d], s + 1)
                    done(tt(w, w, bk[d][2], ALU.add), dl_num[d])
                    c = SD[:, q, 4 * d:4 * d + 4, :]
                    dve.wait_ge(dl_su[d], s + 1)
                    done(tt(c, c, heads(bk[d][3]), ALU.add), dl_done[d])
                    if s > 2 or (s == 0 and d == 1):
                        done(tt(y, y, w, ALU.add), dl_y[d])
                    else:
                        done(dve.tensor_copy(y, w), dl_y[d])

            sums(YB, st20b, dlb(0, 0))
            done(ts(st20, st20b, 1.0 / P, LN_EPS, ALU.mult, ALU.add), var_ready)
            dve.wait_ge(rstd_ready, 2)
            gated(YB, 1, TILES)
            count_y = [0]

            def statistics(t):
                for n in range(2):
                    done(dve.bn_stats(bnst[:, t, n, :], X[:, t, 512 * n:512 * n + 512]))
                done(dve.bn_aggr(bnag[:, t, :], bnst[:, t, :, :]))
                done(ts(lnr[:, t:t + 1], bnag[:, t, 1:2], LN_EPS, None, ALU.add), var_ready)

            def layer_norm(nth, t):
                statistics(t)
                dve.wait_ge(rstd_ready, 3 + TILES * nth + t)
                done(ts(X[:, t, :], X[:, t, :], bnag[:, t, 0:1], lnr[:, t:t + 1], ALU.subtract, ALU.mult))
                done(tt(X[:, t, :], X[:, t, :], BC[:, 2, :], ALU.mult))
                done(tt(X[:, t, :], X[:, t, :], BC[:, 3, :], ALU.add), ln_done)

            def residual(l):
                dve.wait_ge(bc_loaded, 64 * (2 * l + 1))
                for n in range(2):
                    for t in range(TILES):
                        j = TILES * n + t
                        dve.wait_ge(unit_out, unit_no[("out", l, n, t)] + 1)
                        c = slice(512 * n, 512 * n + 512)
                        done(tt(YO[j % 2], YO[j % 2], BC[:, min(t, 1), c], ALU.mult))
                        done(stt(X[:, t, c], X[:, t, c], ALPHA, YO[j % 2], ALU.mult, ALU.add), out_used)
                        if n:
                            v = min(t, 1)
                            layer_norm(2 * l, t)
                            dve.wait_ge(bc2_loaded, 64 * (l + 1))
                            done(stt(H2[:, t, :], BC2[:, 2 + v, :], 1.0, X[:, t, :], ALU.add, ALU.mult), h2_scaled)

            residual(0)

            def first_max(values, vmax_, cand_, hot):
                done(dve.tensor_reduce(vmax_, values, AX.X, ALU.max))
                done(tt(cand_, values, vmax_.unsqueeze(2).to_broadcast([P, TILES, 4]), ALU.is_equal))
                done(stt(cand_, cand_, -100.0, IOTA[:, 0:4].unsqueeze(1).to_broadcast([P, TILES, 4]), ALU.mult, ALU.add))
                done(dve.tensor_reduce(cmin, cand_, AX.X, ALU.min))
                done(tt(hot, cand_, cmin.unsqueeze(2).to_broadcast([P, TILES, 4]), ALU.is_equal))

            def dve_moe(l):
                dve.wait_ge(unit_out, unit_no[("rt", l, TILES - 1)] + 1)
                dve.wait_ge(router_loaded, 16 * 7 * (l + 1))
                done(tt(LG[:, :, :], LG[:, :, :], RB.unsqueeze(1).to_broadcast([P, TILES, 20]), ALU.add))
                lg = LG[:, :, 0:4]
                first_max(lg, gmax, cand, ghot)
                g3 = gx[:, 0:20].rearrange("p (t c) -> p t c", t=TILES)
                done(tt(g3, lg, gmax.unsqueeze(2).to_broadcast([P, TILES, 4]), ALU.subtract))
                r4 = rtmp.rearrange("p (t g e) -> p t g e", t=TILES, g=4)
                done(tt(r4, LG[:, :, 4:20].rearrange("p t (g e) -> p t g e", g=4),
                        ghot.unsqueeze(3).to_broadcast([P, TILES, 4, 4]), ALU.mult))
                done(dve.tensor_reduce(LE, rtmp.rearrange("p (t g e) -> p t e g", t=TILES, g=4), AX.X, ALU.add))
                first_max(LE, vmax, cand, hot1)
                done(stt(LE2, hot1, NEG, LE, ALU.mult, ALU.add))
                first_max(LE2, vsec, cand, hot2)
                done(tt(gx[:, 20:25], vsec, vmax, ALU.subtract), route_arg)
                for c, hot in enumerate((hot1, hot2)):
                    done(tt(HE[:, c].rearrange("p t (g e) -> p t g e", g=4), ghot.unsqueeze(3).to_broadcast([P, TILES, 4, 4]),
                            hot.unsqueeze(2).to_broadcast([P, TILES, 4, 4]), ALU.mult))
                done(tt(HALL.rearrange("p (t e) -> p t e", t=TILES), HE[:, 0], HE[:, 1], ALU.add), hot_ready)
                dve.wait_ge(route_exp, l + 1)
                done(dve.tensor_reduce(gsum, g3, AX.X, ALU.add))
                done(dve.reciprocal(gw, gsum))
                done(ts(gsum, gx[:, 20:25], 1.0, None, ALU.add))
                done(dve.reciprocal(gsum, gsum))
                done(tt(WSEL[:, 0, :], gsum, gw, ALU.mult))
                done(tt(WSEL[:, 1, :], WSEL[:, 0, :], gx[:, 20:25], ALU.mult))
                dve.wait_ge(unit_out, unit_no[("rank", l)] + 1)
                done(dve.tensor_reduce(CNT, RK[:, 80:160].rearrange("p (t e) -> p e t", t=TILES), AX.X, ALU.add))
                b4 = big[:, 0:64].rearrange("p (e j) -> p e j", e=16)
                done(tt(b4, CNT.unsqueeze(2).to_broadcast([P, 16, 4]), IOTA[:, 9:13].unsqueeze(1).to_broadcast([P, 16, 4]),
                        ALU.is_gt))
                done(dve.tensor_reduce(OV, b4, AX.X, ALU.add))
                done(dve.tensor_tensor_scan(OVC, OV, zero16, 0.0, ALU.add, ALU.add))
                done(tt(OBASE, OVC, OV, ALU.subtract))
                done(ts(OBASE, OBASE, float(P), float(P * (NEXP - 1) - 1), ALU.mult, ALU.add))
                done(ts(EBASE, IOTA[:, 16:32], float(P), -1.0, ALU.mult, ALU.add))
                done(tt(OBASE, OBASE, EBASE, ALU.subtract))
                done(ts(past, RK[:, 0:80], float(P), None, ALU.is_gt))
                rk, ps = (x.rearrange("p (t e) -> p t e", t=TILES) for x in (RK[:, 0:80], past))
                done(tt(ps, ps, OBASE.unsqueeze(1).to_broadcast([P, TILES, 16]), ALU.mult))
                done(tt(rk, rk, EBASE.unsqueeze(1).to_broadcast([P, TILES, 16]), ALU.add))
                done(tt(rk, rk, ps, ALU.add))
                for c in range(2):
                    r3 = rtmp.rearrange("p (t e) -> p t e", t=TILES)
                    done(tt(r3, rk, HE[:, c], ALU.mult))
                    done(dve.tensor_reduce(slotf[:, TILES * c:TILES * c + TILES], r3, AX.X, ALU.add))
                nt = 2 * TILES
                tiles_ = IOTA[:, 16:16 + ETILES].unsqueeze(1).to_broadcast([P, nt, ETILES])
                bt = big.rearrange("p (n i) -> p n i", n=nt)
                done(ts(low, slotf, 1.0 / P, None, ALU.mult))
                done(tt(bt, low.unsqueeze(2).to_broadcast([P, nt, ETILES]), tiles_, ALU.is_ge))
                done(dve.tensor_reduce(tile_at_slot, bt, AX.X, ALU.add))
                done(ts(tile_at_slot, tile_at_slot, -1.0, None, ALU.add))
                done(stt(low, tile_at_slot, -float(P), slotf, ALU.mult, ALU.add))
                hot, weighted = HOTT[:, :, 0:ETILES], HOTT[:, :, ETILES:2 * ETILES]
                done(tt(hot, tiles_, tile_at_slot.unsqueeze(2).to_broadcast([P, nt, ETILES]), ALU.is_equal))
                done(tt(weighted, hot, WSEL[:, :, :].rearrange("p c t -> p (c t)").unsqueeze(2).to_broadcast([P, nt, ETILES]),
                        ALU.mult))
                for c in range(2):
                    half_ = hot[:, TILES * c:TILES * c + TILES]
                    done(tt(half_, half_, IOTA[:, 48:53].unsqueeze(2).to_broadcast([P, TILES, ETILES]), ALU.mult))
                done(tt(HOTL, iota_row.unsqueeze(1).to_broadcast([P, nt, P]), low.unsqueeze(2).to_broadcast([P, nt, P]),
                        ALU.is_equal), slots_ready)
                bo = big[:, 0:16 * (ETILES - NEXP)].rearrange("p (i e) -> p i e", i=ETILES - NEXP)
                done(tt(bo, OVC.unsqueeze(1).to_broadcast([P, ETILES - NEXP, 16]),
                        IOTA[:, 16:16 + ETILES - NEXP].unsqueeze(2).to_broadcast([P, ETILES - NEXP, 16]), ALU.is_le))
                done(dve.tensor_reduce(eotf[:, NEXP:ETILES], bo, AX.X, ALU.add))
                done(ts(eotf[:, NEXP:ETILES], eotf[:, NEXP:ETILES], float(NEXP - 1), None, ALU.min))
                done(dve.tensor_copy(eotf[:, 0:NEXP], IOTA[:, 16:32]))
                done(ts(ngf, OVC[:, 15:16], float(NEXP), None, ALU.add))
                done(tt(big[:, 0:GROUPS], ngf.to_broadcast([P, GROUPS]), IOTA[:, 53:53 + GROUPS], ALU.is_gt))
                done(dve.tensor_reduce(ngf, big[:, 0:GROUPS], AX.X, ALU.add))
                done(dve.tensor_copy(NG, ngf))
                done(dve.tensor_copy(EOT, eotf), routed)
                dve.wait_ge(unit_done, unit_no[("tok", l)] + 1)
                b = PS[:, unit_no[("tok", l)] % BANKS, :]
                dve.tensor_copy(TOKI, b[:, 0:ETILES])
                dve.tensor_copy(WSLOT, b[:, ETILES:2 * ETILES]).then_inc(unit_out, 1)
                dve.wait_ge(unit_out, unit_no[("tok", l)] + 1)
                done(dve.tensor_copy(IDX[:, :, :], slotf.rearrange("p (c t) -> p c t", c=2)), slots_cast)

                def gated_values(i, u):
                    dve.wait_ge(silu_out, i + (ETILES * l + 1))
                    dve.tensor_tensor(HIDR[:, u, :], AU[:, u, :], PS[:, 2 + u, 256:512], ALU.mult).then_inc(hid_ready, 1)

                def rows_out(i, j, u, first):
                    if not first:
                        dve.wait_ge(ye_stored[u], 16 * j + 16 * GROUPS * l)
                    dve.wait_ge(down_done, i + (ETILES * l + 1))
                    dve.tensor_scalar(YE[:, u, 0:512], PS[:, 5, :], WSLOT[:, bass.ds(i, 1)], None, ALU.mult).then_inc(ye_ready, 1)

                def group(j, first=False):
                    gated_values(3 * j, 0)
                    gated_values(3 * j + 1, 1)
                    rows_out(3 * j, j, 0, first)
                    gated_values(3 * j + 2, 2)
                    rows_out(3 * j + 1, j, 1, first)
                    rows_out(3 * j + 2, j, 2, first)

                group(0, True)
                groups = dve.value_load(NG[0:1, 0:1], min_val=1, max_val=GROUPS)
                with dve.Fori(1, SURE) as j:
                    group(j)
                with dve.Fori(SURE, GROUPS) as j:
                    with dve.If(j < groups):
                        group(j)
                    with dve.Else():
                        for moved in (hid_ready, ye_ready):
                            dve.wait_ge(moved, 3 * j + ETILES * l)
                            dve.sem_inc(moved, 3)
                dve.wait_ge(ye_ready, ETILES * (l + 1))
                count["ye_ready"] = ETILES * (l + 1)
                dve.wait_ge(bc_loaded, 64 * (2 * l + 2))
                for it in range(TILES + 2):
                    if it < TILES:
                        g = YG[:, it, :]
                        dve.wait_ge(yg_gathered[it], 32 * (l + 1))
                        done(tt(g, g, BC[:, min(it, 1), :], ALU.mult))
                        done(stt(X[:, it, :], X[:, it, :], ALPHA, g, ALU.mult, ALU.add))
                        statistics(it)
                    if 1 <= it <= TILES:
                        t = it - 1
                        dve.wait_ge(rstd_ready, 3 + TILES * (2 * l + 1) + t)
                        done(stt(lnb[:, t:t + 1], bnag[:, t, 0:1], -1.0, lnr[:, t:t + 1], ALU.mult, ALU.mult), ln_shift)
                    if it >= 2:
                        t = it - 2
                        dve.wait_ge(ln_scaled, TILES * l + t + 1)
                        done(tt(X[:, t, :], X[:, t, :], BC[:, 2, :], ALU.mult), ln_gained)
                count["ln_done"] += TILES

            dve_moe(0)

            def rotate(x, heads_, t):
                w = heads_ * HD
                tmp = RTMP[:, 0:w]
                cos, sin = (ROPE[:, a, t - 1, :] for a in range(2))
                xs = x.rearrange("p h (a f i) -> p h a f i", a=2, f=2)
                ys = tmp.rearrange("p (h a f i) -> p h a f i", h=heads_, a=2, f=2)
                sn = sin.rearrange("p (a f i) -> p a f i", a=2, f=2)
                for f in range(2):
                    done(tt(ys[:, :, :, f, :], xs[:, :, :, 1 - f, :],
                            sn[:, :, f, :].unsqueeze(1).to_broadcast([P, heads_, 2, HD // 4]), ALU.mult))
                done(tt(x, x, cos.unsqueeze(1).to_broadcast([P, heads_, HD]), ALU.mult))
                return tt(x, x, tmp.rearrange("p (h i) -> p h i", h=heads_), ALU.add)

            dve.wait_ge(ln_done, 2 * TILES)
            done(dve.memset(KZERO, 0.0), keys_ready)
            dve.wait_ge(attn_loaded, 64)
            for t in range(1, TILES):
                dve.wait_ge(unit_out, unit_no[("qkv", 2, t)] + 1)
                done(rotate(KD[:, t, :, :], KVH, t), keys_ready)
            for n in range(2):
                for t in range(TILES):
                    dve.wait_ge(unit_out, unit_no[("qkv", n, t)] + 1)
                    x = QR[:, t, 512 * n:512 * n + 512].rearrange("p (h i) -> p h i", h=8)
                    if t:
                        done(rotate(x, 8, t), queries_ready)
                    else:
                        done(dve.tensor_copy(RTMP[:, 0:1], x[:, 0, 0:1]), queries_ready)
            dve.wait_ge(unit_out, unit_no[("qT", TILES - 1, 1)] + 1)
            done(dve.memset(MASKS, 0.0))
            for a, n in ((0, 0), (BEFORE, 1), (AFTER, 2), (LAST, 1)):
                done(dve.tensor_copy(MASKS[:, a:a + P], MB[:, n, :]), masks_ready)

            def normalise(g):
                c = slice(8 * g, 8 * g + 8)
                dve.wait_ge(sink_exp, g + 1)
                dve.wait_ge(pv_done, 8 * g + 8)
                done(tt(ES[:, c], ES[:, c], RS[:, c], ALU.add))
                done(dve.reciprocal(ES[:, c], ES[:, c]))
                o = QR[:, g // 2, 512 * (g % 2):512 * (g % 2) + 512].rearrange("p (h i) -> p h i", h=8)
                done(tt(o, PS[:, 6 + g % 2, :].rearrange("p (h i) -> p h i", h=8),
                        ES[:, c].unsqueeze(2).to_broadcast([P, 8, HD]), ALU.mult), o_ready)

            for n in range(STEPS):
                h = n % HC
                w = P * len(key_tiles(n // HC)[1])
                dve.wait_ge(s_done, n + 1)
                done(dve.tensor_reduce(NM[:, n:n + 1], PS[:, n % 3, 0:w], AX.X, ALU.max))
                done(ts(NM[:, n:n + 1], NM[:, n:n + 1], SINK[:, h:h + 1], -1.0, ALU.max, ALU.mult), max_ready)
                if n % 8 == 7:
                    done(tt(ES[:, n - 7:n + 1], SINK[:, h - 7:h + 1], NM[:, n - 7:n + 1], ALU.add), sink_arg)
                if n % 8 == 5 and n > 8:
                    normalise((n - 8) // 8)
            normalise(STEPS // 8 - 1)
            residual(1)
            dve_moe(1)

        @block.tensor
        def _(pe):
            def begin(name):
                n = unit_no[name]
                if n >= BANKS:
                    pe.wait_ge(unit_out, n - BANKS + 1)
                return PS[:, n % BANKS, :]

            def out_of(name):
                pe.wait_ge(unit_out, unit_no[name] + 1)

            def weights(item):
                n = load_no[item]
                pe.wait_ge(slot_arrived[slot_of(n)], arrived_at[n])
                return slot_cols(n, KT, 32 if item == ("in", "gates") else 512), slot_of(n)

            pe.wait_ge(const_loaded, 96)
            b = begin(("cT",))
            pe.transpose(b[:, 0:16], cin, CST[0:16, C_ID, 0:16]).then_inc(unit_done, 1)
            b = begin(("convT",))
            pe.transpose(b[:, 0:36], convrow, CST[0:36, C_ID, 0:36]).then_inc(unit_done, 1)

            def mod_partial(l, c):
                b = begin(("mod", l, c))
                w, s = weights(("mod", l, c))
                for k in range(KT):
                    g = k % 4
                    pe.matmul(b[32 * g:32 * g + 32, :], csil[:, 32 * k:32 * k + 32], w[:, k, :], start=(k < 4), stop=False)
                for g in range(4):
                    i = pe.matmul(b[32 * g:32 * g + 32, g * P:(g + 1) * P], CST[0:1, C_ONES, 0:32],
                                  SLOTS[0:1, s, 4096 + g * P:4096 + (g + 1) * P], start=False, stop=True)
                i.then_inc(unit_done, 1)

            def mod_sum(l, c):
                b = begin(("modS", l, c))
                out_of(("mod", l, c))
                pe.matmul(b[0:2, :], IOTA[:, 64:66], MSUM[:, c % 2, :], start=True, stop=True).then_inc(unit_done, 1)
                if c < 4:
                    b = begin(("modT", l, c))
                    out_of(("modS", l, c))
                    for q in range(4):
                        i = pe.transpose(b[:, 2 * q:2 * q + 2], MROW[:, c % 2, q * P:(q + 1) * P], CST[0:2, C_ID, 0:2])
                    i.then_inc(unit_done, 1)

            def fill(stage, step):
                for kind, l, c in fills(stage, step):
                    if kind == "mod":
                        mod_partial(l, c)
                    elif kind == "modS":
                        mod_sum(l, c)

            def mod_rows(name):
                part = mod_parts[name]
                for j, lc in enumerate(part):
                    for ahead in part[0:2] if j == 0 else part[j + 1:j + 2]:
                        mod_partial(*ahead)
                    mod_sum(*lc)

            def transposes_of_x(l, t):
                for g in range(2):
                    b = begin(("hT", l, t, g))
                    for q in range(4):
                        i = pe.transpose(b[:, q * P:(q + 1) * P], X[:, t, (4 * g + q) * P:(4 * g + q + 1) * P], ident)
                    i.then_inc(unit_done, 1)

            def feature_major(name):
                w, s = weights(("in", name))
                for m in range(4):
                    for h in range(2):
                        b = begin(("fm", name, m, h))
                        for k in range(KT):
                            i = pe.matmul(b[:, 0:320], w[:, k, m * P:(m + 1) * P], HT[:, k, 320 * h:320 * h + 320],
                                          start=(k == 0), stop=(k == KT - 1))
                        i.then_inc(unit_done, 1)
                    fill(name, m)

            def token_major(name, tiles=range(TILES)):
                w, s = weights(("in", name))
                for t in tiles:
                    b = begin(("tm", name, t))
                    for k in range(KT):
                        i = pe.matmul(b, HT[:, k, t * P:(t + 1) * P], w[:, k, :],
                                      start=(k == 0), stop=(k == KT - 1))
                    i.then_inc(unit_done, 1)
                    fill(name, t)

            def head_transposes(name, src):
                for t in range(TILES):
                    b = begin(name + (t,))
                    for h in range(HEADS):
                        i = pe.transpose(b[:, h * P:(h + 1) * P], src[:, h, t * P:(t + 1) * P], ident)
                    i.then_inc(unit_done, 1)

            out_of(("cT",))
            mod_rows("first")
            pe.wait_ge(x_loaded, 32)
            transposes_of_x(0, 0)
            for k in range(KT):
                b = begin(("hTlat", k))
                for t in range(1, TILES):
                    i = pe.transpose(b[:, (t - 1) * P:t * P], X[:, t, k * P:(k + 1) * P], ident)
                i.then_inc(unit_done, 1)
            out_of(("hTlat", KT - 1))
            w, s = weights(("in", "gates"))
            for h in range(2):
                b = begin(("gatesT", h))
                for k in range(KT):
                    i = pe.matmul(b[0:32, 0:320], w[:, k, :], HT[:, k, 320 * h:320 * h + 320],
                                  start=(k == 0), stop=(k == KT - 1))
                i.then_inc(unit_done, 1)
            b = begin(("gates",))
            out_of(("gatesT", 1))
            for t in range(TILES):
                i = pe.transpose(b[:, 32 * t:32 * t + 32], GATEST[:, t * P:(t + 1) * P], CST[0:32, C_ID, 0:32])
            i.then_inc(unit_done, 1)
            feature_major("qa")
            pe.wait_ge(gate_lf, 1)
            for d in range(2):
                b = begin(("cs", d))
                pe.matmul(b[:, 0:40], CST[:, (C_UPI, C_LOI)[d], :], LF[:, 40 * d:40 * d + 40], start=True, stop=True)\
                    .then_inc(unit_done, 1)
            b = begin(("ce",))
            pe.matmul(b[:, 0:80], ones, LF, start=True, stop=True).then_inc(unit_done, 1)
            for name, src, c in (("rowf", v8(LF), 0), ("rowi", raw4, 0)):
                for d in range(2):
                    for part, steps in enumerate((range(4), range(4, 5))):
                        b = begin((name, d, part))
                        for j, s in enumerate(steps):
                            i = pe.matmul(b[0:4, j * P:(j + 1) * P], src[:, d, s, 0:4], (ident, flip)[d], start=True, stop=True)
                        i.then_inc(unit_done, 1)
            feature_major("ka")
            for d in range(2):
                b = begin(("mcol", d))
                pe.wait_ge(m_scanned, d + 1)
                for s in range(TILES):
                    i = pe.matmul(b[:, 4 * s:4 * s + 4], MR[:, d, s * P:(s + 1) * P], CST[0:4, C_ID, 0:4], start=True, stop=True)
                i.then_inc(unit_done, 1)
            b = begin(("mflip",))
            out_of(("mcol", 1))
            pe.matmul(b[:, 0:20], flip, rev, start=True, stop=True).then_inc(unit_done, 1)
            b = begin(("mvb",))
            pe.wait_ge(mex_ready, 1)
            pe.matmul(b[:, 0:56], CST[0:4, C_ONES, :], MEX[0:4, :], start=True, stop=True).then_inc(unit_done, 1)
            token_major("va")
            out_of(("fm", "ka", 3, 1))
            head_transposes(("ktok", "a"), KTR)

            out_of(("ktok", "a", TILES - 1))
            pe.wait_ge(state_loaded, 48)
            pe.wait_ge(pool_const, 9)
            pe.wait_ge(exp_ready, 1)
            pe.wait_ge(masks_ready, 1)

            def decay(d, s, which, bank_):
                pe.matmul(bank_.rearrange("p (h c) -> p h c", h=HEADS), MB[:, 0, :],
                          MB[:, 1 + d, :].unsqueeze(1).to_broadcast([P, HEADS, P]), start=True, stop=False)
                for h in range(HEADS):
                    v = v4(RV[:, which, :])[:, d, s, h:h + 1]
                    i = pe.matmul(bank_[:, h * P:(h + 1) * P], v.to_broadcast([P, P]), ident, start=False, stop=(h == HEADS - 1))
                return i

            for s in range(TILES):
                q = 1 if s else 0
                for d in range(2):
                    A, Bk, C, E = (PS[:, 4 * d + n, :] for n in range(4))
                    tk = slice(tile_at(d, s) * P, tile_at(d, s) * P + P)
                    if s:
                        pe.wait_ge(ml_num[d], s)
                    for h in range(HEADS):
                        i = pe.matmul(A[:, h * P:(h + 1) * P], KTR[:, h, tk], QT[:, h, tk], start=True, stop=True)
                    i.then_inc(ml_st[d], 1)
                    decay(d, s, 0, Bk).then_inc(ml_db[d], 1)
                for d in range(2):
                    A, Bk, C, E = (PS[:, 4 * d + n, :] for n in range(4))
                    t = tile_at(d, s)
                    tk = slice(t * P, t * P + P)
                    if s:
                        pe.wait_ge(ml_done[d], s)
                    pe.wait_ge(ml_sw[d], s + 1)
                    for h in range(HEADS):
                        sw = mlb(d, 1)[:, h * P:(h + 1) * P]
                        pe.matmul(A[:, h * P:(h + 1) * P], sw, VTOK[:, t, h * P:(h + 1) * P], start=True, stop=True)
                        pe.matmul(E[:, h:h + 1], sw, CST[:, C_ONES, 0:1], start=True, stop=True)
                        pe.matmul(Bk[:, h * P:(h + 1) * P], QT[:, h, tk], SM[:, q, 4 * d + h, :], start=True, stop=True)
                        pe.matmul(E[:, 4 + h:5 + h], QT[:, h, tk], NS[:, q, 4 * d + h:4 * d + h + 1], start=True, stop=True)
                    pe.wait_ge(ml_vw[d], s + 1)
                    for h in range(HEADS):
                        kk = KTOK[:, t, h * P:(h + 1) * P]
                        pe.matmul(C[:, h * P:(h + 1) * P], kk, mlb(d, 2)[:, h * P:(h + 1) * P], start=True, stop=True)
                        i = pe.matmul(E[:, 8 + h:9 + h], kk, v4(EX[:, WE, :])[:, d, s, h:h + 1], start=True, stop=True)
                    i.then_inc(ml_u[d], 1)
            for d in range(2):
                pe.wait_ge(ml_done[d], TILES)
            token_major("oa")
            feature_major("vd")
            feature_major("kd")
            pe.wait_ge(silu_done, 4)
            head_transposes(("vtok",), QT)

            def square_sums(name, first):
                for m in range(4):
                    for h in range(2):
                        b = begin(("ssq", name, m, h))
                        pe.wait_ge(sq_ready, first + m + 1)
                        pe.matmul(b[:, 0:320], ones, SQ[:, m, 320 * h:320 * h + 320], start=True, stop=True)\
                            .then_inc(unit_done, 1)

            square_sums("kd", 0)
            feature_major("qd")
            pe.wait_ge(normed, 4)
            head_transposes(("ktok", "d"), KTR)
            square_sums("qd", 4)
            token_major("zb", range(0, 2))
            pe.wait_ge(normed, 8)

            out_of(("tm", "zb", 1))
            for s in range(TILES):
                q = 1 if s else 0
                bk = [[PS[:, 4 * d + n, :] for n in range(4)] for d in range(2)]

                def mm4(o, lhsT, rhs):
                    for h in range(HEADS):
                        c = slice(h * P, (h + 1) * P)
                        i = pe.matmul(o[:, c], lhsT[:, c], rhs[:, c], start=True, stop=True)
                    return i

                for d in range(2):
                    A, Bk, C, E = bk[d]
                    tk = slice(tile_at(d, s) * P, tile_at(d, s) * P + P)
                    if s:
                        pe.wait_ge(dl_num[d], s)
                    for h in range(HEADS):
                        c = slice(h * P, (h + 1) * P)
                        pe.matmul(A[:, c], KTR[:, h, tk], KTR[:, h, tk], start=True, stop=True)
                        i = pe.matmul(C[:, c], KTR[:, h, tk], QT[:, h, tk], start=True, stop=True)
                    i.then_inc(dl_kk[d], 1)
                    decay(d, s, 1, Bk).then_inc(dl_db[d], 1)
                    if s:
                        pe.wait_ge(dl_done[d], s)
                    for h in range(HEADS):
                        c = slice(h * P, (h + 1) * P)
                        i = pe.matmul(E[:, c], KTR[:, h, tk], SD[:, q, 4 * d + h, :], start=True, stop=True)
                    i.then_inc(dl_ks[d], 1)
                for d in range(2):
                    pe.wait_ge(dl_xt1[d], s + 1)
                    for h in range(HEADS):
                        c = slice(h * P, (h + 1) * P)
                        i = pe.transpose(bk[d][0][:, c], dlb(d, 4)[:, c], ident)
                    i.then_inc(dl_x1t[d], 1)
                for n in range(1, 7):
                    for d in range(2):
                        if n == 1:
                            pe.wait_ge(dl_x1[d], s + 1)
                        else:
                            pe.wait_ge(dl_x[d], 5 * s + n - 1)
                        pe.wait_ge(dl_cm[d], 6 * s + n)
                        mm4(bk[d][0], dlb(d, 5 + n % 2), dlb(d, 3)).then_inc(dl_p1[d], 1)
                    for d in range(2):
                        pe.wait_ge(dl_p1s[d], 6 * s + n)
                        pe.wait_ge(dl_xt[d], 6 * s + n - 1) if n > 1 else pe.wait_ge(dl_qd[d], s + 1)
                        if n < 6:
                            mm4(bk[d][1], dlb(d, 4), dlb(d, 0))
                        mm4(bk[d][2], dlb(d, 0), dlb(d, 4)).then_inc(dl_p2[d], 1)
                for d in range(2):
                    A, Bk, C, E = bk[d]
                    tk = slice(tile_at(d, s) * P, tile_at(d, s) * P + P)
                    for h in range(HEADS):
                        c = slice(h * P, (h + 1) * P)
                        pe.matmul(Bk[:, c], QT[:, h, tk], SD[:, q, 4 * d + h, :], start=True, stop=True)
                    pe.wait_ge(dl_xt[d], 6 * s + 6)
                    pe.wait_ge(dl_r[d], s + 1)
                    mm4(A, dlb(d, 4), dlb(d, 2)).then_inc(dl_tr[d], 1)
                for d in range(2):
                    A, Bk, C, E = bk[d]
                    pe.wait_ge(dl_vn[d], s + 1)
                    mm4(C, dlb(d, 1), dlb(d, 3)).then_inc(dl_o[d], 1)
                    pe.wait_ge(dl_vw[d], s + 1)
                    mm4(E, KTOK[:, tile_at(d, s), :], dlb(d, 2)).then_inc(dl_su[d], 1)
            for d in range(2):
                pe.wait_ge(dl_done[d], TILES)
            token_major("zb", range(2, TILES))
            pe.wait_ge(gate_used, 2 * TILES)
            out_of(("tm", "zb", TILES - 1))

            def y_transposes(l, head):
                for k in range(KT):
                    for part, tiles in enumerate((range(4), range(4, 5))):
                        b = begin(("yT", l, k, part))
                        for j, t in enumerate(tiles):
                            i = pe.transpose(b[:, j * P:(j + 1) * P], head(k, t), ident)
                        i.then_inc(unit_done, 1)
                out_of(("yT", l, KT - 1, 1))

            def out_proj(l):
                for n in range(2):
                    w, s = weights(("wout", l, n))
                    for t in range(TILES):
                        b = begin(("out", l, n, t))
                        for k in range(KT):
                            i = pe.matmul(b, HT[:, k, t * P:(t + 1) * P], w[:, k, :], start=(k == 0), stop=(k == KT - 1))
                        i.then_inc(unit_done, 1)
                        fill(f"out{l}{n}", t)
    
            y_transposes(0, lambda k, t: (YA, YB)[k // 4][:, t, (k % 4) * P:(k % 4 + 1) * P])
            out_proj(0)

            def pe_moe(l):
                for t in range(TILES + 1):
                    if t < TILES:
                        pe.wait_ge(h2_ready, TILES * l + t + 1)
                        for g in range(2):
                            b = begin(("h2T", l, t, g))
                            for q in range(4):
                                i = pe.transpose(b[:, q * P:(q + 1) * P], H2[:, t, (4 * g + q) * P:(4 * g + q + 1) * P], ident)
                            i.then_inc(unit_done, 1)
                    if t:
                        pe.wait_ge(router_loaded, 16 * 7 * (l + 1))
                        b = begin(("rt", l, t - 1))
                        out_of(("h2T", l, t - 1, 1))
                        for k in range(KT):
                            i = pe.matmul(b[:, 0:20], H2T[:, k, (t - 1) * P:t * P], RW[:, k, :], start=(k == 0), stop=(k == KT - 1))
                        i.then_inc(unit_done, 1)
                b = begin(("iota", l))
                pe.matmul(b[:, 0:P], IOTA[:, 48:49].to_broadcast([P, P]), ident, start=True, stop=True).then_inc(unit_done, 1)
                pe.wait_ge(hot_ready, l + 1)
                b = begin(("rank", l))
                pe.matmul(b[:, 0:80], CST[:, C_UPI, :], HALL, start=True, stop=False)
                for t in range(TILES - 1):
                    later = TILES - 1 - t
                    pe.matmul(b[:, 16 * (t + 1):80].rearrange("p (t e) -> p t e", e=16), ones,
                              HALL[:, 16 * t:16 * t + 16].unsqueeze(1).to_broadcast([P, later, 16]), start=False, stop=False)
                pe.matmul(b[:, 80:160], ones, HALL, start=False, stop=True).then_inc(unit_done, 1)
                b = begin(("tok", l))
                pe.wait_ge(slots_ready, l + 1)
                for n in range(2 * TILES):
                    i = pe.matmul(b[:, 0:2 * ETILES], HOTL[:, n, :], HOTT[:, n, :], start=(n == 0), stop=(n == 2 * TILES - 1))
                i.then_inc(unit_done, 1)
                out_of(("tok", l))
                n0 = load_no[("moe", l)]

                def transposes(i, u, j, first=False):
                    pe.wait_ge(rows_gathered[l][u], 16 * j + 16)
                    if not first:
                        pe.wait_ge(xt_out, i + ETILES * l)
                    for k in range(KT):
                        m = pe.transpose(PS[:, k // 4, (k % 4) * P:(k % 4 + 1) * P], XG[:, u, k * P:(k + 1) * P], ident)
                    m.then_inc(xt_done, 1)

                def gate_up(i, j, u, first):
                    w = SLOTS[:, u, 0:4096].rearrange("p (m k c) -> p m k c", m=2, k=KT)
                    pe.wait_ge(slot_arrived[u], 48 * j + arrived_at[n0 + u])
                    pe.wait_ge(xt_out, i + (ETILES * l + 1))
                    if not first:
                        pe.wait_ge(hid_ready, i + (ETILES * l - 2))
                    for k in range(KT):
                        x = pe.matmul(PS[:, 2 + u, :].rearrange("p (m c) -> p m c", m=2), XGT[:, u, k, :], w[:, :, k, :],
                                      start=(k == 0), stop=(k == KT - 1))
                    x.then_inc(gu_done, 1)

                def down(i, u, first=False):
                    pe.wait_ge(hid_ready, i + (ETILES * l + 1))
                    for m in range(2):
                        x = pe.transpose(PS[:, 7, m * P:(m + 1) * P], HIDR[:, u, m * P:(m + 1) * P], ident)
                    x.then_inc(ht_done, 1)
                    pe.wait_ge(ht_out, i + (ETILES * l + 1))
                    w = SLOTS[:, u, 4096:6144].rearrange("p (k c) -> p k c", k=2)
                    for h in range(2):
                        if not first:
                            pe.wait_ge((ye_ready, ye2_ready)[h], i + ETILES * l)
                        for m in range(2):
                            x = pe.matmul(PS[:, 5 + h, :], HID[:, u, m, :], w[:, m, 512 * h:512 * h + 512],
                                          start=(m == 0), stop=(m == 1))
                    x.then_inc(down_done, 1)

                def group(j, first=False):
                    i = 3 * j
                    transposes(i, 0, j, first)
                    gate_up(i, j, 0, first)
                    transposes(i + 1, 1, j)
                    gate_up(i + 1, j, 1, first)
                    down(i, 0, first and not l)
                    transposes(i + 2, 2, j)
                    gate_up(i + 2, j, 2, first)
                    down(i + 1, 1)
                    down(i + 2, 2)

                group(0, True)
                pe.wait_ge(routed, l + 1)
                groups = pe.value_load(NG[0:1, 0:1], min_val=1, max_val=GROUPS)
                with pe.Fori(1, SURE) as j:
                    group(j)
                with pe.Fori(SURE, GROUPS) as j:
                    with pe.If(j < groups):
                        group(j)
                    with pe.Else():
                        for moved in (xt_done, gu_done, ht_done, down_done):
                            pe.wait_ge(moved, 3 * j + ETILES * l)
                            pe.sem_inc(moved, 3)

            pe_moe(0)

            pe.wait_ge(ye_ready, ETILES)
            pe.wait_ge(ye2_ready, ETILES)
            mod_rows("moe")
            for t in range(TILES - 1):
                pe.wait_ge(ln_done, TILES + t + 1)
                transposes_of_x(1, t)

            def qkv_product(n, t):
                w, _ = weights(("qkv", n))
                b = begin(("qkv", n, t))
                out_of(("hT", 1, t, 1))
                for k in range(KT):
                    i = pe.matmul(b, HT[:, k, t * P:(t + 1) * P], w[:, k, :], start=(k == 0), stop=(k == KT - 1))
                i.then_inc(unit_done, 1)

            qkv_product(2, 0)
            pe.wait_ge(ln_done, 2 * TILES)
            transposes_of_x(1, TILES - 1)
            for n in (2, 0, 1):
                for t in range(TILES):
                    if (n, t) != (2, 0):
                        qkv_product(n, t)
                    fill(f"qkv{n}", t)
            out_of(("qkv", 2, 0))
            for t in range(TILES + 1):
                if t < TILES:
                    pe.wait_ge(keys_ready, t + 1)
                else:
                    pe.wait_ge(attn_loaded, 64)
                for r in range(2):
                    b = begin(("kT", t, r))
                    for g in range(KVH):
                        a = 2 * HD * (KVH * t + g) + HD * (1 - r)
                        i = pe.transpose(b[:, g * P:(g + 1) * P], BCF[:, a:a + 2 * HD], ident)
                    i.then_inc(unit_done, 1)
            for t in range(TILES):
                for g in range(2):
                    b = begin(("qT", t, g))
                    pe.wait_ge(queries_ready, TILES * g + t + 1)
                    for q in range(4):
                        i = pe.transpose(b[:, q * P:(q + 1) * P], QR[:, t, 512 * g + q * P:512 * g + (q + 1) * P], ident)
                    i.then_inc(unit_done, 1)
            out_of(("qT", TILES - 1, 1))
            pe.wait_ge(masks_ready, 5)

            def scores(n):
                t, h = n // HC, n % HC
                local, cols = key_tiles(t)
                b = PS[:, n % 3, :]
                q = QTT[:, h // 2, t * P:(t + 1) * P]
                kk = KTT[h % 2][:, h // 4, :]
                if n >= 3:
                    pe.wait_ge(p_ready, n - 2)
                if t:
                    a = LAST if t == TILES - 1 else BEFORE if t > 1 else BEFORE + P
                    w = P * len(cols)
                    pe.matmul(b[:, 0:w], MASKS[:, 0:P], MASKS[:, a:a + w], start=True, stop=False)
                runs = [cols] if cols[-1] - cols[0] == len(cols) - 1 else [local, [TILES]]
                a = 0
                for r, run in enumerate(runs):
                    i = pe.matmul(b[:, a:a + P * len(run)], q, kk[:, run[0] * P:(run[-1] + 1) * P], start=(t == 0), stop=(r == len(runs) - 1))
                    a += P * len(run)
                i.then_inc(s_done, 1)

            def weight_transposes(n):
                pe.wait_ge(p_ready, n + 1)
                if n >= 3:
                    pe.wait_ge(pt_out, n - 2)
                for j in range(len(key_tiles(n // HC)[1])):
                    i = pe.transpose(PS[:, 3 + n % 3, j * P:(j + 1) * P], PB[:, n % 3, j * P:(j + 1) * P], ident)
                i.then_inc(pt_done, 1)

            def values(n):
                t, h = n // HC, n % HC
                cols = key_tiles(t)[1]
                pe.wait_ge(pt_out, n + 1)
                if h % 8 == 0 and n >= HC:
                    pe.wait_ge(o_ready, n // 8 - 1)
                for j, kt in enumerate(cols):
                    i = pe.matmul(PS[:, 6 + h // 8, HD * (h % 8):HD * (h % 8) + HD], PTB[:, n % 3, j * P:(j + 1) * P],
                                  V[:, kt, HD * (h // 4):HD * (h // 4) + HD], start=(j == 0), stop=(j == len(cols) - 1))
                i.then_inc(pv_done, 1)

            for n in range(STEPS + 3):
                if n < STEPS:
                    scores(n)
                if 2 <= n < STEPS + 2:
                    weight_transposes(n - 2)
                if n >= 3:
                    values(n - 3)
            pe.wait_ge(o_ready, STEPS // 8)
            y_transposes(1, lambda k, t: QR[:, t, k * P:(k + 1) * P])
            out_proj(1)
            pe_moe(1)


_OUTS = [((1, P, D), "float32"), ((1, LAT, D), "float32"), ((1, 1, 2, HEADS, P, P), "float32"),
         ((1, 1, 2, HEADS, P), "float32"), ((1, 1, 2, HEADS), "float32"), ((1, 1, 2, HEADS, P, P), "float32"),
         ((1, 1, KVH, P, HD), "float32"), ((1, 1, KVH, P, HD), "float32")]


def kernel(**inputs):
    import numpy as _np
    import concourse.bacc as _bacc
    from concourse import mybir as _mybir
    from concourse.bass_utils import run_bass_kernel_spmd as _run

    nc = _bacc.Bacc("TRN2", target_bir_lowering=False, num_devices=1)
    data = dict(inputs)
    data["consts"] = constants()
    data["ropes"] = rope_tables()
    data["iotas"] = iotas()
    data["masks"] = masks()
    arrays, ins = {}, {}
    for name, a in data.items():
        a = _np.ascontiguousarray(a)
        arrays[f"in_{name}"] = a
        ins[name] = nc.dram_tensor(f"in_{name}", a.shape, _mybir.dt.from_np(a.dtype), kind="ExternalInput").ap()
    outs = [nc.dram_tensor(f"out_{i}", s, _mybir.dt.from_np(_np.dtype(t)), kind="ExternalOutput").ap()
            for i, (s, t) in enumerate(_OUTS)]
    build(nc, ins, outs)
    r = _run(nc, [arrays], core_ids=[0])
    return tuple(r.results[0][f"out_{i}"] for i in range(len(_OUTS)))
```
